# Optimizing a Trainium2 kernel written in Bass

```python
import jax, jax.numpy as jnp
from jax import lax
import numpy as np

D_MODEL = 2048
BATCH = 1
SEQ = 256
DEPTH = 2

N_A_LAYERS = DEPTH // 2
N_B_LAYERS = DEPTH - N_A_LAYERS
POOL_WINDOWS = (2, 4, 8, 16)
N_POOL_GROUPS = len(POOL_WINDOWS)
POOL_GROUP_DIM = D_MODEL // N_POOL_GROUPS
HEAD_DIM = 128
N_HEADS = D_MODEL // HEAD_DIM
Q_BLOCK = 128
N_GROUPS = 4
EXPERTS_PER_GROUP = 4
N_EXPERTS = N_GROUPS * EXPERTS_PER_GROUP
TOP_K_IN_GROUP = 2
D_FF_EXPERT = D_MODEL // 4
EPS = 1e-6

kernel_name = "hybrid_pool_stickbreak_hmoe"

def rmsnorm(x, g):
    xf = x.astype(jnp.float32)
    y = xf * lax.rsqrt(jnp.mean(xf * xf, axis=-1, keepdims=True) + EPS)
    return (y * g.astype(jnp.float32)).astype(x.dtype)

def pool_mixer(x, pool_w, pool_scale):
    B, S, D = x.shape
    xf = x.reshape(B, S, N_POOL_GROUPS, POOL_GROUP_DIM).astype(jnp.float32)
    csum = jnp.cumsum(xf, axis=1)
    pos = jnp.arange(S)
    outs = []
    for gi, w in enumerate(POOL_WINDOWS):
        c = csum[:, :, gi]
        c_prev = jnp.pad(c, ((0, 0), (w, 0), (0, 0)))[:, :S]
        cnt = jnp.minimum(pos + 1, w).astype(jnp.float32)[None, :, None]
        outs.append((c - c_prev) / cnt - xf[:, :, gi])
    pooled = jnp.stack(outs, axis=2).astype(x.dtype)
    y = jnp.einsum("bsgc,gcd->bsgd", pooled, pool_w).reshape(B, S, D)
    return y * pool_scale

def head_rms(x, g):
    xf = x.astype(jnp.float32)
    y = xf * lax.rsqrt(jnp.mean(xf * xf, axis=-1, keepdims=True) + EPS)
    return (y * g.astype(jnp.float32)).astype(x.dtype)

def shared_kv(h, kv_norm, w_kv, k_norm):
    B, S, D = h.shape
    kv = rmsnorm(h, kv_norm) @ w_kv
    k, v = jnp.split(kv, 2, axis=-1)
    k = head_rms(k.reshape(B, S, N_HEADS, HEAD_DIM), k_norm)
    v = v.reshape(B, S, N_HEADS, HEAD_DIM)
    return k.transpose(0, 2, 1, 3), v.transpose(0, 2, 1, 3)

def stick_breaking(q, k, v):
    S = q.shape[2]
    scale = HEAD_DIM ** -0.5
    outs = []
    for b0 in range(0, S, Q_BLOCK):
        n_k = b0 + Q_BLOCK
        qb = q[:, :, b0:n_k]
        kb = k[:, :, :n_k]
        vb = v[:, :, :n_k]
        z = jnp.einsum("bhqd,bhkd->bhqk", qb, kb).astype(jnp.float32) * scale
        t_pos = b0 + jnp.arange(Q_BLOCK)
        s_pos = jnp.arange(n_k)
        causal = s_pos[None, :] < t_pos[:, None]
        log_keep = jnp.where(causal, jax.nn.log_sigmoid(-z), 0.0)
        after = lax.cumsum(log_keep, axis=3, reverse=True) - log_keep
        a = jnp.where(causal, jnp.exp(jax.nn.log_sigmoid(z) + after), 0.0)
        outs.append(jnp.einsum("bhqk,bhkd->bhqd", a.astype(vb.dtype), vb))
    return jnp.concatenate(outs, axis=2)

def stick_breaking_layer(x, k, v, w_q, q_norm, w_o):
    B, S, D = x.shape
    q = head_rms((x @ w_q).reshape(B, S, N_HEADS, HEAD_DIM), q_norm)
    o = stick_breaking(q.transpose(0, 2, 1, 3), k, v)
    return o.transpose(0, 2, 1, 3).reshape(B, S, D) @ w_o

def hier_moe(x, w_grp, b_grp, w_rt, b_rt, w_gate, w_up, w_down):
    B, S, D = x.shape
    T = B * S
    xt = x.reshape(T, D)
    grp_logits = (xt @ w_grp + b_grp).astype(jnp.float32)
    grp_prob = jax.nn.softmax(grp_logits, axis=-1)
    g_idx = jnp.argmax(grp_logits, axis=-1)
    g_w = jnp.take_along_axis(grp_prob, g_idx[:, None], axis=-1)
    exp_logits = (jnp.einsum("td,gde->tge", xt, w_rt) + b_rt).astype(jnp.float32)
    sel = jnp.take_along_axis(exp_logits, g_idx[:, None, None], axis=1)[:, 0]
    top_v, top_i = lax.top_k(sel, TOP_K_IN_GROUP)
    top_w = jax.nn.softmax(top_v, axis=-1) * g_w
    within = jnp.sum(jax.nn.one_hot(top_i, EXPERTS_PER_GROUP, dtype=jnp.float32)
                     * top_w[..., None], axis=1)
    gate = (jax.nn.one_hot(g_idx, N_GROUPS, dtype=jnp.float32)[:, :, None]
            * within[:, None, :]).reshape(T, N_EXPERTS).astype(x.dtype)
    h = jax.nn.silu(jnp.einsum("td,edf->tef", xt, w_gate)) * jnp.einsum("td,edf->tef", xt, w_up)
    y = jnp.einsum("tef,efd->td", h * gate[:, :, None], w_down)
    return y.reshape(B, S, D)

def setup_inputs(seed: int = 0) -> dict:
    key = jax.random.key(seed)
    ks = jax.random.split(key, 20)
    f32 = jnp.float32
    D, C, HD, F = D_MODEL, POOL_GROUP_DIM, HEAD_DIM, D_FF_EXPERT

    def nrm(k, shape, fan_in):
        return jax.random.normal(k, shape, f32) * fan_in ** -0.5

    def gain(k, shape):
        return 1.0 + 0.05 * jax.random.normal(k, shape, f32)

    return {
        "x": jax.random.normal(ks[0], (BATCH, SEQ, D), f32),
        "norm_mix": gain(ks[1], (DEPTH, D)),
        "norm_ffn": gain(ks[2], (DEPTH, D)),
        "pool_w": nrm(ks[3], (N_A_LAYERS, N_POOL_GROUPS, C, C), C),
        "pool_scale": gain(ks[4], (N_A_LAYERS, D)),
        "kv_norm": gain(ks[5], (D,)),
        "w_kv": nrm(ks[6], (D, 2 * D), D),
        "k_norm": gain(ks[7], (HD,)),
        "w_q": nrm(ks[8], (N_B_LAYERS, D, D), D),
        "q_norm": gain(ks[9], (N_B_LAYERS, HD)),
        "w_o": nrm(ks[10], (N_B_LAYERS, D, D), D),
        "moe_w_grp": nrm(ks[11], (DEPTH, D, N_GROUPS), D),
        "moe_b_grp": 0.01 * jax.random.normal(ks[12], (DEPTH, N_GROUPS), f32),
        "moe_w_rt": nrm(ks[13], (DEPTH, N_GROUPS, D, EXPERTS_PER_GROUP), D),
        "moe_b_rt": 0.01 * jax.random.normal(ks[14], (DEPTH, N_GROUPS, EXPERTS_PER_GROUP), f32),
        "moe_w_gate": nrm(ks[15], (DEPTH, N_EXPERTS, D, F), D),
        "moe_w_up": nrm(ks[16], (DEPTH, N_EXPERTS, D, F), D),
        "moe_w_down": nrm(ks[17], (DEPTH, N_EXPERTS, F, D), F),
    }

def reference(x, norm_mix, norm_ffn, pool_w, pool_scale, kv_norm, w_kv, k_norm,
              w_q, q_norm, w_o, moe_w_grp, moe_b_grp, moe_w_rt, moe_b_rt,
              moe_w_gate, moe_w_up, moe_w_down):
    h = x
    k = v = None
    for i in range(DEPTH):
        if i < N_A_LAYERS:
            h = h + pool_mixer(rmsnorm(h, norm_mix[i]), pool_w[i], pool_scale[i])
        else:
            j = i - N_A_LAYERS
            if j == 0:
                k, v = shared_kv(h, kv_norm, w_kv, k_norm)
            h = h + stick_breaking_layer(rmsnorm(h, norm_mix[i]), k, v,
                                         w_q[j], q_norm[j], w_o[j])
        h = h + hier_moe(rmsnorm(h, norm_ffn[i]), moe_w_grp[i], moe_b_grp[i],
                         moe_w_rt[i], moe_b_rt[i], moe_w_gate[i], moe_w_up[i],
                         moe_w_down[i])
    return h


_drawn_inputs = setup_inputs


def setup_inputs(seed=0):
    import zlib

    import numpy as np

    out = dict(_drawn_inputs(seed))
    spreads = {}
    factors = {'k_norm': 3.891, 'q_norm': 3.918, 'moe_b_grp': 5.177, 'moe_b_rt': 4.401}
    for name, (base, spread) in spreads.items():
        noise = np.random.default_rng([zlib.crc32(name.encode()), seed]).standard_normal(out[name].shape)
        drawn = base * np.exp(spread * noise) if base else spread * noise
        out[name] = __import__('jax').numpy.asarray(drawn.astype(out[name].dtype))
    for name, factor in factors.items():
        out[name] = (out[name] * factor).astype(out[name].dtype)
    return out
```

```python
from contextlib import ExitStack

import numpy as np

import concourse.bass as bass
from concourse import mybir

F32 = mybir.dt.float32
BF16 = mybir.dt.bfloat16
I32 = mybir.dt.int32
ALU = mybir.AluOpType
ACT = mybir.ActivationFunctionType
AX_X = mybir.AxisListType.X

P = 128
SEQ = 256
D = 2048
NT = SEQ // P
KD = D // P
NG = 4
GD = D // NG
WINDOWS = (2, 4, 8, 16)
HD = 128
NH = D // HD
HG = NH // NG
EXP = 16
EPG = EXP // NG
FF = 512
KF = FF // P
CAP = 64
NPAIR = EXP // 2
NBLK = 4
BLK = D // NBLK
SLOTS = 12
PAIR_SLOTS = 2 * SLOTS
UNIT_BUFS = 3
EPS = 1e-6
BIG = 1e30
F32R = mybir.dt.float32r
ZC = SEQ + P

C_ID, C_TRI, C_ONE, C_NSUF, C_NONE, C_ADD = 0, 128, 256, 384, 512, 640
C_IOTA = C_ADD + ZC
C_RANK = C_IOTA + CAP
C_END = C_RANK + 4
BANDS = NG * 3 * P
V_MIX, V_KV, V_Q, V_FFN, V_HEAD, V_END = 0, 16, 32, 48, 80, 82


def constant_table():
    c = np.zeros((P, C_END), np.float32)
    row, col = np.arange(P)[:, None], np.arange(P)[None, :]
    c[:, C_ID:C_ID + P] = row == col
    c[:, C_TRI:C_TRI + P] = row < col
    c[:, C_ONE:C_ONE + P] = 1.0
    c[:, C_NSUF:C_NSUF + P] = -(row >= col).astype(np.float32)
    c[:, C_NONE:C_NONE + P] = -1.0
    seen = (row < col).astype(np.float32)
    c[:, C_ADD:C_ADD + ZC] = (np.concatenate([seen, np.ones((P, P), np.float32), seen], 1) - 1.0) * BIG
    c[:, C_IOTA:C_IOTA + CAP] = np.arange(CAP)
    c[:, C_RANK:C_RANK + 4] = [4, 3, 2, 1]
    return c


def band_table():
    src, dst = np.arange(SEQ)[:, None], np.arange(SEQ)[None, :]
    out = np.zeros((P, NG, 3, P), np.float32)
    for g, w in enumerate(WINDOWS):
        m = ((src <= dst) & (src > dst - w)) / np.minimum(dst + 1, w) - (src == dst)
        out[:, g, 0], out[:, g, 1], out[:, g, 2] = m[:P, :P], m[:P, P:], m[P:, P:]
    return out.reshape(P, BANDS)


def build(nc, x, norm_mix, norm_ffn, pool_w, pool_scale, kv_norm, w_kv, k_norm, w_q, q_norm, w_o,
          w_grp, b_grp, w_rt, b_rt, w_gate, w_up, w_down, table, bands, out):
    with ExitStack() as ctx:
        def sb(name, shape, dt=F32):
            return ctx.enter_context(nc.sbuf_tensor(name, shape, dt))

        def sem(name):
            return ctx.enter_context(nc.semaphore(name))

        ring = sb("ring", [P, SLOTS, 2048])
        resid = sb("resid", [P, NT, D])
        const = sb("const", [P, C_END])
        vecs = sb("vecs", [P, V_END])
        ffn_gain = sb("ffn_gain", [P, 2, KD])
        bias = sb("bias", [P, 2, 20])
        w_route = sb("w_route", [P, 2, KD, 20])
        ssq_part = sb("ssq_part", [P, NT, NBLK])
        ssq = sb("ssq", [P, NT])
        rs = sb("rs", [P, NT])
        rs_rest = sb("rs_rest", [P, NT])
        rs_parts = sb("rs_parts", [P, NT, 3], BF16)
        rs_slot = sb("rs_slot", [CAP, 2])
        half = sb("half", [P, NT * HG])
        head_ssq = sb("head_ssq", [P, NT, HG])
        head_rs = sb("head_rs", [P, NT, HG])
        flags = sb("flags", [1, 2], I32)
        most = sb("most", [P, 1])
        KB = 1024
        ARENA = -(-nc.sbuf_base // 32) * 32
        sb("arena", [P, 102 * KB // 4])

        def at(offset, name, shape, dt=F32):
            return nc.alloc_sbuf_tensor_at(name, shape, dt, offset=ARENA + offset)


        xs = at(0, "xs", [P, 2, KD, SEQ], F32R)
        ws = at(32 * KB, "ws", [P, UNIT_BUFS, 2, 2, BLK], F32R)
        route_rows = at(0, "route_rows", [KD, 2, 5, 4 * P])
        junk_rows = at(20 * KB, "junk_rows", [P, D])
        band = at(72 * KB, "band", [P, NG, 3, P])
        band_s = at(78 * KB, "band_s", [P, NG, 3, P])
        vec_rows = at(64 * KB, "vec_rows", [V_END, P])
        mixed = at(68 * KB, "mixed", [P, NT, BLK])
        scale_bc = ring[:, SLOTS - 1, :]
        xr = at(56 * KB, "xr", [P, KD, SEQ])
        parts = at(72 * KB, "parts", [P, 3, NT, D], BF16)
        rest = at(96 * KB, "rest", [P, NT, BLK])
        junk = at(100 * KB, "junk", [P, BLK])
        oT = at(56 * KB, "oT", [P, NH, SEQ])
        kT = at(72 * KB, "kT", [P, HG, SEQ])
        qT = at(76 * KB, "qT", [P, HG, SEQ])
        vrow = at(80 * KB, "vrow", [P, NT, HG * HD])
        raw = at(84 * KB, "raw", [P, NT, HG, HD])
        lnk = at(88 * KB, "lnk", [P, HG, ZC])
        soft = at(94 * KB, "soft", [P, HG, ZC])
        att = soft
        squares = at(100 * KB, "squares", [P, HG, HD])
        junk_att = at(88 * KB, "junk_att", [P, D])
        xg = at(0, "xg", [P, 2, KD, CAP])
        y_rows = at(8 * KB, "y_rows", [P, D])
        silu_g = at(16 * KB, "silu_g", [CAP, FF])
        hid = at(18 * KB, "hid", [CAP, FF])
        hidT = at(20 * KB, "hidT", [P, 2, KF, CAP])
        pick = at(22 * KB, "pick", [P, NT, 2, CAP], BF16)
        put = at(23 * KB, "put", [P, NT, 2, CAP])
        putT = at(24 * KB, "putT", [P, SEQ])
        logitsT = at(25 * KB, "logitsT", [20, SEQ])
        lg = at(26 * KB, "lg", [P, NT, 20])
        small = at(26 * KB + 256, "small", [P, 24, NT, 4])
        prod = at(27 * KB + 256, "prod", [P, NT, 4, 4])
        member = at(27 * KB + 512, "member", [P, NT, EXP])
        gate = at(27 * KB + 768, "gate", [P, NT, EXP + 2])
        slot_of = at(28 * KB, "slot_of", [P, NT, EXP + 2])
        over_gate = at(28 * KB + 256, "over_gate", [P, NT, EXP])
        o_silu = at(32 * KB, "o_silu", [P, FF])
        o_hid = at(34 * KB, "o_hid", [P, FF])
        o_hidT = at(36 * KB, "o_hidT", [P, KF, P])

        ident = const[:, C_ID:C_ID + P]
        ones = const[:, C_ONE:C_ONE + P]
        tri = const[:, C_TRI:C_TRI + P]
        iota = const[:, C_IOTA:C_IOTA + CAP]
        rank = const[:, C_RANK:C_RANK + 4]

        ps = ctx.enter_context(nc.psum_tensor("ps", [P, 8, 512], F32))

        slot_loaded = [sem(f"slot_loaded{j}") for j in range(SLOTS)]
        slot_read = sem("slot_read")
        x_loaded = [sem(f"x_loaded{t}") for t in range(NT)]
        table_loaded = sem("table_loaded")
        band_loaded = sem("band_loaded")
        route_loaded = sem("route_loaded")
        smalls_loaded = sem("smalls_loaded")
        ssq_done = sem("ssq_done")
        ms_done = sem("ms_done")
        pool_step = sem("pool_step")
        rs_done = sem("rs_done")
        band_done = sem("band_done")
        vec_turned = sem("vec_turned")
        vec_done = sem("vec_done")
        turned = sem("turned")
        turned_out = sem("turned_out")
        xs_hi = sem("xs_hi")
        xs_lo = sem("xs_lo")
        unit_hi = sem("unit_hi")
        unit_lo = sem("unit_lo")
        unit_used = sem("unit_used")
        tile0_done = sem("tile0_done")
        mixed_done = sem("mixed_done")
        mix_done = sem("mix_done")
        resid_added = sem("resid_added")
        dve_step = sem("dve_step")
        hi_done = sem("hi_done")
        rest_done = [sem(f"rest_done{t}") for t in range(NT)]
        mid_done = [sem(f"mid_done{t}") for t in range(NT)]
        lo_done = [sem(f"lo_done{t}") for t in range(NT)]
        route_mm = sem("route_mm")
        route_act = sem("route_act")
        route_dve = sem("route_dve")
        member_done = sem("member_done")
        rs_parts_done = sem("rs_parts_done")
        pick_done = sem("pick_done")
        put_done = sem("put_done")
        rs_gathered = sem("rs_gathered")
        rs_slot_done = sem("rs_slot_done")
        gathered = sem("gathered")
        xg_done = sem("xg_done")
        silu_done = sem("silu_done")
        hid_done = sem("hid_done")
        hid_turned = sem("hid_turned")
        hidT_done = sem("hidT_done")
        y_act = sem("y_act")
        y_dve = sem("y_dve")
        over = [{n: sem(f"over{l}_{n}") for n in
                 ("loaded", "gu", "silu", "hid", "turned", "hidT", "down", "added")}
                for l in range(2)]
        proj_out = sem("proj_out")
        sq_done = sem("sq_done")
        head_sums = sem("head_sums")
        head_rs_done = sem("head_rs_done")
        head_normed = sem("head_normed")
        heads_turned = sem("heads_turned")
        heads_out = sem("heads_out")
        z_done = sem("z_done")
        act_step = sem("act_step")
        ln_done = sem("ln_done")
        soft_done = sem("soft_done")
        cum_done = sem("cum_done")
        shift_done = sem("shift_done")
        att_done = sem("att_done")
        o_done = sem("o_done")
        o_out = sem("o_out")
        final_ready = sem("final_ready")
        stored = sem("stored")

        START_MOE = [NG, NG + NPAIR * PAIR_SLOTS + NG * SLOTS + NBLK * 4]
        START_ATT = START_MOE[0] + NPAIR * PAIR_SLOTS
        START_O = START_ATT + NG * SLOTS
        UNIT_ATT = 2 * NG
        UNIT_O = UNIT_ATT + 2 * NG * SLOTS
        ADD_BASE = [8, 16 + 8 * NPAIR]
        ADD_O = 8 + 8 * NPAIR
        TURN_ROUTE = [8, 24]
        TURN_ATT = 16
        TILE0_ATT = NG
        TILE0_O = NG + 3 * NG
        SSQ = [2, 2 + 8, 2 + 8 + 2, 2 + 8 + 2 + 8]
        TABLES = 16 * 7
        SMALLS = 16 * 7

        def slot(n):
            return ring[:, n % SLOTS, :]

        def four(n):
            return slot(n).rearrange("p (k c) -> p k c", k=4)

        def when_read(n):
            if n < START_MOE[0]:
                return unit_lo, 2 * n + 2
            if n < START_ATT:
                return slot_read, n - START_MOE[0] + 1
            if n < START_O:
                return unit_lo, UNIT_ATT + 2 * (n - START_ATT) + 2
            if n < START_MOE[1]:
                return unit_lo, UNIT_O + 2 * (n - START_O) + 2
            return slot_read, NPAIR * PAIR_SLOTS + n - START_MOE[1] + 1

        def slot_in(eng, n, i=0, per=0):
            eng.wait_ge(slot_loaded[n % SLOTS], 16 * (n // SLOTS + 1) + i * (16 * per // SLOTS))

        w_gate_v = w_gate.rearrange("l e (p k) f -> l e p k f", k=KD)
        w_up_v = w_up.rearrange("l e (p k) f -> l e p k f", k=KD)
        w_down_v = w_down.rearrange("l e (k p) d -> l e p k d", p=P)
        w_gate_k = w_gate.rearrange("l e (k p) f -> l e p k f", p=P)
        w_up_k = w_up.rearrange("l e (k p) f -> l e p k f", p=P)
        w_kv_v = w_kv.rearrange("(k p) (b c) -> b p k c", p=P, c=BLK)
        w_q_v = w_q[0].rearrange("(k p) (b c) -> b p k c", p=P, c=BLK)
        w_o_v = w_o[0].rearrange("(k p) (b c) -> b p k c", p=P, c=BLK)
        pool_w_v = pool_w[0].rearrange("g (k p) c -> g p k c", p=P)

        X_BANKS = (0, 1, 2, 3, 6, 7, 0, 1)

        def in_tiles(s, t, c):
            return parts[:, s, t, :].rearrange("q (k p) -> q p k", k=KD)[:, c * (BLK // KD):(c + 1) * (BLK // KD), :]

        block = ctx.enter_context(nc.Block())

        @block.sync
        def _(sp):
            def load(n, src, dst=None, i=0, per=0):
                if n >= SLOTS:
                    before, value = when_read(n - SLOTS)
                    sp.wait_ge(before, value + i * per * (2 if before is unit_lo else 1))
                if n == SLOTS - 1:
                    sp.wait_ge(mixed_done, 8)
                sp.dma_start(four(n) if dst is None else dst, src).then_inc(slot_loaded[n % SLOTS], 16)

            def expert(l, e, n0, i=0, per=0):
                for q in range(4):
                    for h, w in enumerate((w_gate_v, w_up_v)):
                        load(n0 + 2 * q + h, w[l, e, :, 4 * q:4 * q + 4, :], None, i, per)
                for q in range(KF):
                    load(n0 + 8 + q, w_down_v[l, e, :, q, :], slot(n0 + 8 + q), i, per)

            def moe(l):
                n0 = START_MOE[l]
                expert(l, 0, n0)
                expert(l, 1, n0 + SLOTS)
                with sp.Fori(1, NPAIR) as i:
                    for b in range(2):
                        expert(l, 2 * i + b, n0 + PAIR_SLOTS + SLOTS * b, i - 1, PAIR_SLOTS)
                sp.wait_ge(route_dve, 3 * (l + 1))
                count = sp.value_load(flags[0:1, l:l + 1], min_val=0, max_val=SEQ)
                with sp.If(count > CAP):
                    sp.wait_ge(slot_read, NPAIR * PAIR_SLOTS * (l + 1))

                    def again(e):
                        for q in range(4):
                            for h, w in enumerate((w_gate_k, w_up_k)):
                                sp.dma_start(four(2 * q + h), w[l, e, :, 4 * q:4 * q + 4, :]).then_inc(over[l]["loaded"], 16)
                            sp.dma_start(slot(8 + q), w_down_v[l, e, :, q, :]).then_inc(over[l]["loaded"], 16)

                    again(0)
                    with sp.Fori(1, EXP) as e:
                        sp.wait_ge(over[l]["down"], NT * e)
                        again(e)
                    sp.wait_ge(over[l]["down"], NT * EXP)
                with sp.Else():
                    sp.nop()

            for t in range(NT):
                sp.dma_start(resid[:, t, :], x[0, t * P:(t + 1) * P, :]).then_inc(x_loaded[t], 16)
            for g in range(NG):
                load(g, pool_w_v[g])
            moe(0)

            def group(g, n, i):
                for kind, src in enumerate((w_kv_v[g], w_q_v[g], w_kv_v[g + NG])):
                    for q in range(4):
                        load(n + 4 * kind + q, src[:, 4 * q:4 * q + 4, :], None, i, SLOTS)

            group(0, START_ATT, 0)
            with sp.Fori(1, NG) as g:
                group(g, START_ATT + SLOTS, g - 1)
            for b in range(NBLK):
                for q in range(4):
                    load(START_O + 4 * b + q, w_o_v[b, :, 4 * q:4 * q + 4, :])
            moe(1)
            sp.wait_ge(resid_added, ADD_BASE[1] + 8 * NPAIR)
            sp.wait_ge(final_ready, 1)
            for t in range(NT):
                sp.dma_start(out[0, t * P:(t + 1) * P, :], resid[:, t, :]).then_inc(stored, 16)
            sp.wait_ge(stored, 16 * NT)

        @block.gpsimd
        def _(pool):
            def inverse_rms(n):
                pool.wait_ge(ms_done, n + 1)
                nc.gpsimd.tensor_tensor(rs[:], ssq[:], half[:, 0:NT], ALU.pow).then_inc(rs_done, 1)

            def tile1_parts(l, c):
                blk = slice(c * BLK, (c + 1) * BLK)
                if l + c:
                    pool.wait_ge(lo_done[1], NBLK * l + c)
                pool.wait_ge(hi_done, 8 * l + 2 * c + 2)
                nc.gpsimd.tensor_tensor(rest[:, 1].rearrange("q (p k) -> q p k", k=KD),
                                        resid[:, 1, blk].rearrange("q (p k) -> q p k", k=KD),
                                        in_tiles(0, 1, c), ALU.subtract).then_inc(rest_done[1], 1)
                pool.wait_ge(mid_done[1], NBLK * l + c + 1)
                nc.gpsimd.tensor_tensor(in_tiles(2, 1, c), rest[:, 1].rearrange("q (p k) -> q p k", k=KD),
                                        in_tiles(1, 1, c), ALU.subtract).then_inc(lo_done[1], 1)

            nc.gpsimd.memset(half[:], -0.5).then_inc(pool_step, 1)
            pool.wait_ge(pool_step, 1)
            inverse_rms(0)
            for c in range(NBLK - 1):
                tile1_parts(0, c)
            inverse_rms(1)
            tile1_parts(0, NBLK - 1)
            inverse_rms(2)
            hs = head_ssq[:, :, :].rearrange("p t h -> p (t h)")
            hr = head_rs[:, :, :].rearrange("p t h -> p (t h)")
            with pool.Fori(0, NG) as g:
                for kind in range(2):
                    pool.wait_ge(head_sums, 2 * g + kind + 1)
                    nc.gpsimd.tensor_tensor(hr, hs, half[:, :], ALU.pow).then_inc(head_rs_done, 1)
            for c in range(NBLK - 1):
                tile1_parts(1, c)
            inverse_rms(3)
            tile1_parts(1, NBLK - 1)

        @block.scalar
        def _(act):
            act.dma_start(const[:], table).then_inc(table_loaded, 16)
            for row, v in ((V_MIX, norm_mix[0]), (V_KV, kv_norm), (V_Q, norm_mix[1]), (V_FFN, norm_ffn[0]),
                           (V_FFN + KD, norm_ffn[1])):
                act.dma_start(vec_rows[row:row + KD, :], v.rearrange("(k p) -> k p", p=P)).then_inc(table_loaded, 16)
            act.dma_start(vec_rows[V_HEAD:V_HEAD + 1, :], k_norm.rearrange("(a p) -> a p", a=1)).then_inc(table_loaded, 16)
            act.dma_start(vec_rows[V_HEAD + 1:V_END, :], q_norm).then_inc(band_loaded, 16)
            act.dma_start(band[:, :, :, :], bands.rearrange("p (g b q) -> p g b q", g=NG, b=3)).then_inc(band_loaded, 16)
            for l in range(2):
                act.dma_start(route_rows[:, l, 0], w_grp[l].rearrange("(k p) g -> k (p g)", k=KD)).then_inc(route_loaded, 16)
                act.dma_start(route_rows[:, l, 1:5], w_rt[l].rearrange("g (k p) e -> k g (p e)", k=KD)).then_inc(route_loaded, 16)
            act.dma_start(scale_bc, pool_scale.to_broadcast([P, D])).then_inc(smalls_loaded, 16)
            for l in range(2):
                act.dma_start(ffn_gain[:, l, :], norm_ffn[l].rearrange("(p k) -> p k", k=KD)).then_inc(smalls_loaded, 16)
                act.dma_start(bias[:, l, 0:4], b_grp[l:l + 1, :].to_broadcast([P, 4])).then_inc(smalls_loaded, 16)
                act.dma_start(bias[:, l, 4:20], b_rt[l:l + 1].rearrange("a g e -> a (g e)").to_broadcast([P, EXP])).then_inc(smalls_loaded, 16)

            def unit(u, n, h, gain=None, used=True, i=0, per_u=0, per_n=0):
                if used:
                    act.wait_ge(unit_used, u - UNIT_BUFS + 1 + i * per_u)
                slot_in(act, n, i, per_n)
                dst = ws[:, u % UNIT_BUFS, 0]
                if gain is None:
                    nc.scalar.activation(dst, four(n)[:, 2 * h:2 * h + 2, :], ACT.Copy).then_inc(unit_hi, 1)
                else:
                    for k in range(2):
                        last = nc.scalar.activation(dst[:, k, :], four(n)[:, 2 * h + k, :], ACT.Copy,
                                                    scale=vecs[:, gain + k:gain + k + 1])
                    last.then_inc(unit_hi, 1)

            def squares_and_first(l, c):
                act.wait_ge(resid_added, (0, ADD_O)[l] + 2 * c + 2)
                for t in range(NT):
                    if c + t or l:
                        act.wait_ge(ssq_done, SSQ[2 * l] + 2 * c + t)
                    nc.scalar.activation(junk[:, :], resid[:, t, c * BLK:(c + 1) * BLK], ACT.Square,
                                         accum_out=ssq_part[:, t, c:c + 1]).then_inc(ssq_done, 1)
                for t in range(NT):
                    nc.scalar.activation(in_tiles(0, t, c),
                                         resid[:, t, c * BLK:(c + 1) * BLK].rearrange("q (p k) -> q p k", k=KD),
                                         ACT.Copy).then_inc(hi_done, 1)

            def second(l, c, t):
                act.wait_ge(rest_done[t], NBLK * l + c + 1)
                nc.scalar.activation(in_tiles(1, t, c), rest[:, t].rearrange("q (p k) -> q p k", k=KD),
                                     ACT.Copy).then_inc(mid_done[t], 1)

            def moe(l):
                n0 = NPAIR * PAIR_SLOTS * l
                act.wait_ge(route_mm, 3 * l + 1)
                nc.scalar.activation(logitsT[:, :], ps[0:20, 6, 0:SEQ], ACT.Copy).then_inc(hidT_done, 1)
                second(l, NBLK - 1, 0)
                second(l, NBLK - 1, 1)
                act.wait_ge(route_dve, 3 * l + 1)
                nc.scalar.activation(small[:, 0], small[:, 0], ACT.Exp).then_inc(route_act, 1)
                act.wait_ge(route_dve, 3 * l + 2)
                nc.scalar.activation(small[:, 1, :, 0:1], small[:, 1, :, 0:1], ACT.Exp).then_inc(route_act, 1)
                with act.Fori(0, NPAIR) as i:
                    for b in range(2):
                        act.wait_ge(slot_read, n0 + SLOTS * (2 * i + b) + 8)
                        nc.scalar.activation(silu_g[:, :], ps[0:CAP, b, :], ACT.Silu,
                                             scale=rs_slot[:, b:b + 1]).then_inc(silu_done, 1)
                        act.wait_ge(hid_turned, EXP * l + 2 * i + b + 1)
                        nc.scalar.activation(putT[:, b * P:(b + 1) * P], ps[:, 1 - b, SEQ:SEQ + P], ACT.Copy)
                        nc.scalar.activation(hidT[:, b], ps[:, 1 - b, 0:KF * CAP].rearrange("p (k s) -> p k s", k=KF),
                                             ACT.Copy).then_inc(hidT_done, 1)
                        act.wait_ge(slot_read, n0 + SLOTS * (2 * i + b + 1))
                        for h in range(2):
                            last = nc.scalar.activation(
                                y_rows[CAP * b:CAP * b + CAP, 2 * h * BLK:(2 * h + 1) * BLK],
                                ps[0:CAP, 2 + h, :], ACT.Copy)
                        last.then_inc(y_act, 1)
                act.wait_ge(route_dve, 3 * (l + 1))
                count = act.value_load(flags[0:1, l:l + 1], min_val=0, max_val=SEQ)
                with act.If(count > CAP):
                    with act.Fori(0, EXP) as e:
                        for t in range(NT):
                            act.wait_ge(over[l]["gu"], NT * e + t + 1)
                            nc.scalar.activation(o_silu[:, :], ps[:, 0, :], ACT.Silu,
                                                 scale=rs[:, t:t + 1]).then_inc(over[l]["silu"], 1)
                            act.wait_ge(over[l]["turned"], NT * e + t + 1)
                            nc.scalar.activation(o_hidT[:, :, :], ps[:, 2, :].rearrange("p (k s) -> p k s", k=KF),
                                                 ACT.Copy).then_inc(over[l]["hidT"], 1)
                    act.wait_ge(over[l]["added"], 4 * NT * EXP)
                with act.Else():
                    act.nop()

            for t in range(NT):
                act.wait_ge(x_loaded[t], 16)
                if t:
                    act.wait_ge(ssq_done, t)
                nc.scalar.activation(junk_rows[:, :], resid[:, t, :], ACT.Square,
                                     accum_out=ssq[:, t:t + 1]).then_inc(ssq_done, 1)
            act.wait_ge(vec_done, 2)
            for u in range(UNIT_BUFS):
                unit(u, u // 2, u % 2, used=False)
            for b in range(8):
                act.wait_ge(turned, b + 1)
                for k in range(2):
                    last = nc.scalar.activation(xs[:, 0, 2 * b + k, :], ps[:, b, k * SEQ:(k + 1) * SEQ], ACT.Copy,
                                                scale=vecs[:, V_MIX + 2 * b + k:V_MIX + 2 * b + k + 1])
                last.then_inc(xs_hi, 1)
            for g in range(NG):
                for u in (2 * g + 3, 2 * g + 4):
                    if u < UNIT_ATT:
                        unit(u, u // 2, u % 2)
                if g:
                    squares_and_first(0, g - 1)
                    second(0, g - 1, 0)
                    second(0, g - 1, 1)
            squares_and_first(0, NBLK - 1)
            moe(0)

            def att_unit(g, j, used=True, i=0):
                kind = j // 8
                k = 2 * (j % 8)
                unit(UNIT_ATT + 24 * g + j, START_ATT + SLOTS * g + j // 2, j % 2, (V_KV, V_Q, V_KV)[kind] + k,
                     used, i, 24, SLOTS)

            def projected(g, kind):
                for t in range(NT):
                    if t == 0:
                        act.wait_ge(tile0_done, TILE0_ATT + 3 * g + kind + 1)
                    else:
                        act.wait_ge(unit_used, UNIT_ATT + 24 * g + 8 * kind + 8)
                    dst = vrow[:, t, :] if kind == 2 else raw[:, t].rearrange("p h d -> p (h d)")
                    nc.scalar.activation(dst, ps[:, 4 + t, :], ACT.Copy, scale=rs[:, t:t + 1]).then_inc(proj_out, 1)

            def heads(g, kind):
                for t in range(NT):
                    act.wait_ge(heads_turned, 4 * g + 2 * kind + t + 1)
                    nc.scalar.activation((kT, qT)[kind][:, :, t * P:(t + 1) * P],
                                         ps[:, 6 + t, :].rearrange("p (h q) -> p h q", h=HG),
                                         ACT.Copy, scale=vecs[:, V_HEAD + kind:V_HEAD + kind + 1]).then_inc(heads_out, 1)

            def log_terms(g):
                act.wait_ge(z_done, g + 1)
                nc.scalar.activation(lnk[:, :, :], ps[:, 0:HG, 0:ZC], ACT.Abs).then_inc(act_step, 1)
                act.wait_ge(act_step, 2 * g + 1)
                nc.scalar.activation(lnk[:, :, :], lnk[:, :, :], ACT.Exp, scale=-1.0).then_inc(act_step, 1)
                act.wait_ge(act_step, 2 * g + 2)
                nc.scalar.activation(lnk[:, :, :], lnk[:, :, :], ACT.Ln, bias=1.0).then_inc(ln_done, 1)

            def weights(g):
                act.wait_ge(shift_done, g + 1)
                nc.scalar.activation(att[:, :, :], lnk[:, :, :], ACT.Exp).then_inc(att_done, 1)

            def group(g, i, first):
                G = g + i

                def units(*js):
                    for j in js:
                        att_unit(g, j, True, i)

                if not first:
                    units(0, 1, 2)
                    log_terms(G - 1)
                units(3, 4, 5, 6, 7, 8, 9)
                projected(G, 0)
                units(10, 11)
                if not first:
                    weights(G - 1)
                units(12, 13)
                heads(G, 0)
                units(14, 15, 16, 17)
                projected(G, 1)
                units(18, 19, 20, 21)
                heads(G, 1)
                units(22, 23)
                projected(G, 2)

            act.wait_ge(resid_added, ADD_O)
            att_unit(0, 0)
            for b in range(8):
                act.wait_ge(turned, TURN_ATT + b + 1)
                nc.scalar.activation(xs[:, 0, 2 * b:2 * b + 2, :],
                                     ps[:, X_BANKS[b], :].rearrange("p (k t) -> p k t", k=2),
                                     ACT.Copy).then_inc(xs_hi, 1)
            att_unit(0, 1)
            att_unit(0, 2)
            for t in range(NT):
                act.wait_ge(ssq_done, SSQ[1] + t)
                nc.scalar.activation(junk_att[:, :], resid[:, t, :], ACT.Square,
                                     accum_out=ssq[:, t:t + 1]).then_inc(ssq_done, 1)
            act.wait_ge(rs_done, 3)
            group(0, 0, True)
            with act.Fori(1, NG) as g:
                group(1, g - 1, False)

            def o_unit(j):
                unit(UNIT_O + j, START_O + j // 2, j % 2)

            def o_chunk(c):
                if c == 0:
                    act.wait_ge(unit_used, UNIT_O)
                if c < 3:
                    act.wait_ge(o_out, 2 * c + 2)
                    nc.scalar.activation(xs[:, 0, 4 * c:4 * c + 4, :], oT[:, 4 * c:4 * c + 4, :],
                                         ACT.Copy).then_inc(xs_hi, 1)
                else:
                    act.wait_ge(o_done, 2 * c + 2)
                    nc.scalar.activation(xs[:, 0, 12:16, :].rearrange("p (b h) t -> p b (h t)", b=2), ps[:, 6:8, :],
                                         ACT.Copy).then_inc(xs_hi, 1)

            o_unit(0)
            o_chunk(0)
            o_unit(1)
            o_unit(2)
            o_chunk(1)
            log_terms(NG - 1)
            o_chunk(2)
            o_unit(3)
            o_unit(4)
            weights(NG - 1)
            o_unit(5)
            o_unit(6)
            o_chunk(3)
            o_unit(7)
            for c in range(NBLK):
                if c + 1 < NBLK:
                    o_unit(8 * c + 8)
                    o_unit(8 * c + 9)
                squares_and_first(1, c)
                if c + 1 < NBLK:
                    o_unit(8 * c + 10)
                    o_unit(8 * c + 11)
                    second(1, c, 0)
                    second(1, c, 1)
                    for j in range(8 * c + 12, 8 * c + 16):
                        o_unit(j)
            moe(1)

        @block.vector
        def _(dve):
            steps = [0]

            def step(ins):
                steps[0] += 1
                ins.then_inc(dve_step, 1)
                dve.wait_ge(dve_step, steps[0])

            def per_feature(gain, n, width):
                return gain.unsqueeze(2).to_broadcast([P, n, width])

            def unit(u, n, h, gain=None, i=0, per_u=0):
                dve.wait_ge(unit_hi, u + 1 + i * per_u)
                b = u % UNIT_BUFS
                src = four(n)[:, 2 * h:2 * h + 2, :]
                if gain is None:
                    nc.vector.tensor_tensor(ws[:, b, 1], src, ws[:, b, 0].bitcast(F32), ALU.subtract).then_inc(unit_lo, 1)
                else:
                    for k in range(2):
                        last = nc.vector.scalar_tensor_tensor(
                            out=ws[:, b, 1, k, :], in0=src[:, k, :], scalar=vecs[:, gain + k:gain + k + 1],
                            in1=ws[:, b, 0, k, :].bitcast(F32), op0=ALU.mult, op1=ALU.subtract)
                    last.then_inc(unit_lo, 1)

            def tile0_parts(l, c):
                blk = slice(c * BLK, (c + 1) * BLK)
                if l + c:
                    dve.wait_ge(lo_done[0], NBLK * l + c)
                dve.wait_ge(hi_done, 8 * l + 2 * c + 1)
                nc.vector.tensor_tensor(rest[:, 0].rearrange("q (p k) -> q p k", k=KD),
                                        resid[:, 0, blk].rearrange("q (p k) -> q p k", k=KD),
                                        in_tiles(0, 0, c), ALU.subtract).then_inc(rest_done[0], 1)

            def tile0_last(l, c):
                dve.wait_ge(mid_done[0], NBLK * l + c + 1)
                nc.vector.tensor_tensor(in_tiles(2, 0, c), rest[:, 0].rearrange("q (p k) -> q p k", k=KD),
                                        in_tiles(1, 0, c), ALU.subtract).then_inc(lo_done[0], 1)

            def router_rows(l, c):
                for j in range(2):
                    dve.wait_ge(turned, TURN_ROUTE[l] + 2 * c + j + 1)
                    k = 4 * c + 2 * j
                    nc.vector.tensor_tensor(xr[:, k:k + 2, :],
                                            ps[:, 2 * (c % 2) + j, :].rearrange("p (k t) -> p k t", k=2),
                                            per_feature(vecs[:, V_FFN + KD * l + k:V_FFN + KD * l + k + 2], 2, SEQ),
                                            ALU.mult).then_inc(turned_out, 1)

            def mean_square(n, whole):
                dve.wait_ge(ssq_done, SSQ[n])
                if not whole:
                    step(nc.vector.tensor_reduce(ssq[:, :], ssq_part[:, :, :], AX_X, ALU.add))
                nc.vector.tensor_scalar(ssq[:, :], ssq[:, :], 1.0 / D, EPS, ALU.mult, ALU.add).then_inc(ms_done, 1)

            def moe(l):
                n0 = NPAIR * PAIR_SLOTS * l
                add0 = ADD_BASE[l]
                L4 = lg[:, :, 0:4]
                router_rows(l, NBLK - 1)
                mean_square(2 * l + 1, False)
                tile0_parts(l, NBLK - 1)
                dve.wait_ge(rs_done, 2 * l + 2)
                step(nc.vector.tensor_copy(rs_parts[:, :, 0], rs[:, :]))
                step(nc.vector.tensor_tensor(rs_rest[:, :], rs[:, :], rs_parts[:, :, 0], ALU.subtract))
                step(nc.vector.tensor_copy(rs_parts[:, :, 1], rs_rest[:, :]))
                nc.vector.tensor_tensor(rs_parts[:, :, 2], rs_rest[:, :], rs_parts[:, :, 1],
                                        ALU.subtract).then_inc(rs_parts_done, 1)
                dve.wait_ge(route_mm, 3 * l + 2)
                for t in range(NT):
                    step(nc.vector.scalar_tensor_tensor(out=lg[:, t, :], in0=ps[:, 7, 32 * t:32 * t + 20],
                                                        scalar=rs[:, t:t + 1], in1=bias[:, l, :], op0=ALU.mult,
                                                        op1=ALU.add))

                def one(i):
                    return small[:, i, :, 0:1]

                def wide(i):
                    return one(i).to_broadcast([P, NT, 4])

                def s4(i):
                    return small[:, i]

                def first_best(src, top, hot, tmp):
                    step(nc.vector.tensor_reduce(one(top), src, AX_X, ALU.max))
                    step(nc.vector.tensor_tensor(s4(tmp), src, wide(top), ALU.is_ge))
                    step(nc.vector.tensor_tensor(s4(tmp), s4(tmp), rank.unsqueeze(1).to_broadcast([P, NT, 4]), ALU.mult))
                    step(nc.vector.tensor_reduce(one(tmp + 1), s4(tmp), AX_X, ALU.max))
                    step(nc.vector.tensor_tensor(s4(hot), s4(tmp), wide(tmp + 1), ALU.is_equal))

                GROUP, TOP_G, SEL, TOP1, HOT1, SEL2, TOP2, HOT2, T0, T1, T2, WITHIN, MSK, SUM = range(2, 16)
                first_best(L4, TOP_G, GROUP, T0)
                nc.vector.tensor_tensor(s4(0), L4, wide(TOP_G), ALU.subtract).then_inc(route_dve, 1)
                step(nc.vector.tensor_tensor(prod[:, :, :, :],
                                             lg[:, :, 4:20].rearrange("p t (g e) -> p t e g", g=NG),
                                             s4(GROUP).unsqueeze(2).to_broadcast([P, NT, 4, 4]), ALU.mult))
                step(nc.vector.tensor_reduce(s4(SEL), prod[:, :, :, :], AX_X, ALU.add))
                first_best(s4(SEL), TOP1, HOT1, T0)
                step(nc.vector.scalar_tensor_tensor(out=s4(SEL2), in0=s4(HOT1), scalar=-BIG, in1=s4(SEL),
                                                    op0=ALU.mult, op1=ALU.add))
                first_best(s4(SEL2), TOP2, HOT2, T0)
                step(nc.vector.tensor_tensor(s4(MSK), s4(HOT1), s4(HOT2), ALU.add))
                nc.vector.tensor_tensor(member[:, :, :].rearrange("p t (g e) -> p t g e", g=NG),
                                        s4(GROUP).unsqueeze(3).to_broadcast([P, NT, NG, 4]),
                                        s4(MSK).unsqueeze(2).to_broadcast([P, NT, NG, 4]), ALU.mult).then_inc(member_done, 1)
                nc.vector.tensor_tensor(one(1), one(TOP2), one(TOP1), ALU.subtract).then_inc(route_dve, 1)
                tile0_last(l, NBLK - 1)
                step(nc.vector.memset(slot_of[:, :, EXP:EXP + 2], -1.0))
                dve.wait_ge(route_mm, 3 * l + 3)
                dve.wait_ge(member_done, l + 1)
                count = ps[:, 7, 64:112].rearrange("p (t e) -> p t e", t=3)
                step(nc.vector.scalar_tensor_tensor(out=slot_of[:, :, 0:EXP], in0=count[:, 0:2, :], scalar=1.0,
                                                    in1=member[:, :, :], op0=ALU.add, op1=ALU.mult))
                step(nc.vector.tensor_scalar(slot_of[:, :, 0:EXP], slot_of[:, :, 0:EXP], -1.0, None, ALU.add))

                step(nc.vector.tensor_reduce(most[:], count[:, 2, :], AX_X, ALU.max))

                def make_pick(i):
                    mine = slot_of[:, :, bass.ds(2 * i, 2)].unsqueeze(3).to_broadcast([P, NT, 2, CAP])
                    nc.vector.tensor_tensor(pick[:, :, :, :], iota.unsqueeze(1).unsqueeze(1).to_broadcast([P, NT, 2, CAP]),
                                            mine, ALU.is_equal).then_inc(pick_done, 1)

                def make_put(i):
                    dve.wait_ge(pick_done, (NPAIR + 1) * l + i + 1)
                    nc.vector.tensor_tensor(put[:, :, :, :], pick[:, :, :, :],
                                            gate[:, :, bass.ds(2 * i, 2)].unsqueeze(3).to_broadcast([P, NT, 2, CAP]),
                                            ALU.mult).then_inc(put_done, 1)

                make_pick(0)
                dve.wait_ge(route_act, 2 * l + 1)
                step(nc.vector.tensor_reduce(one(SUM), s4(0), AX_X, ALU.add))
                dve.wait_ge(route_act, 2 * l + 2)
                step(nc.vector.tensor_scalar(one(T1), one(1), 1.0, None, ALU.add))
                step(nc.vector.tensor_tensor(one(T1), one(T1), one(SUM), ALU.mult))
                step(nc.vector.reciprocal(one(T0), one(T1)))
                step(nc.vector.tensor_tensor(one(T2), one(T0), one(1), ALU.mult))
                step(nc.vector.tensor_tensor(s4(WITHIN), s4(HOT1), wide(T0), ALU.mult))
                step(nc.vector.tensor_tensor(s4(SEL2), s4(HOT2), wide(T2), ALU.mult))
                step(nc.vector.tensor_tensor(s4(WITHIN), s4(WITHIN), s4(SEL2), ALU.add))
                step(nc.vector.memset(gate[:, :, EXP:EXP + 2], 0.0))
                step(nc.vector.tensor_tensor(gate[:, :, 0:EXP].rearrange("p t (g e) -> p t g e", g=NG),
                                             s4(GROUP).unsqueeze(3).to_broadcast([P, NT, NG, 4]),
                                             s4(WITHIN).unsqueeze(2).to_broadcast([P, NT, NG, 4]), ALU.mult))
                make_put(0)

                def tokens_out(n, b):
                    dve.wait_ge(rs_gathered, n)
                    nc.vector.tensor_reduce(rs_slot[:, b:b + 1], ps[0:CAP, b, 508:511], AX_X,
                                            ALU.add).then_inc(rs_slot_done, 1)
                    dve.wait_ge(gathered, n)
                    for h in range(2):
                        last = nc.vector.tensor_tensor(
                            xg[:, b, 8 * h:8 * h + 8, :], ps[:, 6 + h, :].rearrange("p (k s) -> p k s", k=8),
                            per_feature(ffn_gain[:, l, 8 * h:8 * h + 8], 8, CAP), ALU.mult)
                    last.then_inc(xg_done, 1)

                G0 = (EXP + 1) * l
                tokens_out(G0 + 1, 0)
                step(nc.vector.scalar_tensor_tensor(out=over_gate[:, :, :], in0=slot_of[:, :, 0:EXP],
                                                    scalar=float(CAP), in1=gate[:, :, 0:EXP], op0=ALU.is_ge, op1=ALU.mult))
                nc.vector.tensor_copy(flags[0:1, l:l + 1], most[0:1, :]).then_inc(route_dve, 1)
                with dve.Fori(0, NPAIR) as i:
                    for b in range(2):
                        dve.wait_ge(silu_done, EXP * l + 2 * i + b + 1)
                        nc.vector.scalar_tensor_tensor(out=hid[:, :], in0=ps[CAP:2 * CAP, b, :],
                                                       scalar=rs_slot[:, b:b + 1], in1=silu_g[:, :],
                                                       op0=ALU.mult, op1=ALU.mult).then_inc(hid_done, 1)
                        tokens_out(G0 + 2 * i + 2 + b, 1 - b)
                        if b == 0:
                            dve.wait_ge(put_done, (NPAIR + 1) * l + i + 1)
                            make_pick(i + 1)
                        dve.wait_ge(slot_read, n0 + SLOTS * (2 * i + b + 1))
                        for h in range(2):
                            last = nc.vector.tensor_copy(
                                y_rows[CAP * b:CAP * b + CAP, (2 * h + 1) * BLK:(2 * h + 2) * BLK],
                                ps[CAP:2 * CAP, 2 + h, :])
                        last.then_inc(y_dve, 1)
                    dve.wait_ge(hid_turned, EXP * l + 2 * i + 2)
                    make_put(i + 1)
                    for m in range(8):
                        c, t = m // 2, m % 2
                        dve.wait_ge(mix_done, 8 * NPAIR * l + 8 * i + m + 1)
                        rb = resid[:, t, c * BLK:(c + 1) * BLK]
                        nc.vector.tensor_tensor(rb, rb, ps[:, 4 + t, :], ALU.add).then_inc(resid_added, 1)
                most_count = dve.value_load(flags[0:1, l:l + 1], min_val=0, max_val=SEQ)
                with dve.If(most_count > CAP):
                    dve.wait_ge(resid_added, add0 + 8 * NPAIR)
                    with dve.Fori(0, EXP) as e:
                        for t in range(NT):
                            dve.wait_ge(over[l]["silu"], NT * e + t + 1)
                            nc.vector.scalar_tensor_tensor(out=o_hid[:, :], in0=ps[:, 1, :], scalar=rs[:, t:t + 1],
                                                           in1=o_silu[:, :], op0=ALU.mult,
                                                           op1=ALU.mult).then_inc(over[l]["hid"], 1)
                            dve.wait_ge(over[l]["down"], NT * e + t + 1)
                            for c in range(NBLK):
                                rb = resid[:, t, c * BLK:(c + 1) * BLK]
                                nc.vector.scalar_tensor_tensor(
                                    out=rb, in0=ps[:, 4 + c, :], scalar=over_gate[:, t, bass.ds(e, 1)],
                                    in1=rb, op0=ALU.mult, op1=ALU.add).then_inc(over[l]["added"], 1)
                            dve.wait_ge(over[l]["added"], 4 * NT * e + 4 * t + 4)
                with dve.Else():
                    dve.nop()

            dve.wait_ge(vec_turned, 1)
            step(nc.vector.tensor_copy(vecs[:], ps[:, 4, 0:V_END]))
            step(nc.vector.tensor_scalar(vecs[:, V_END - 1:V_END], vecs[:, V_END - 1:V_END], HD ** -0.5, None, ALU.mult))
            dve.wait_ge(vec_turned, 2)
            nc.vector.tensor_copy(w_route[:, 0], ps[:, 6, 128:448].rearrange("p (e k) -> p k e", e=20)).then_inc(vec_done, 1)
            nc.vector.tensor_copy(w_route[:, 1], ps[:, 7, 128:448].rearrange("p (e k) -> p k e", e=20)).then_inc(vec_done, 1)
            mean_square(0, True)
            dve.wait_ge(rs_done, 1)
            dve.wait_ge(band_loaded, 32)
            for t, (lo, hi) in enumerate(((0, 2), (2, 3))):
                nc.vector.tensor_scalar(band_s[:, :, lo:hi, :], band[:, :, lo:hi, :], rs[:, t:t + 1], None,
                                        ALU.mult).then_inc(band_done, 1)
            for u in range(UNIT_BUFS):
                unit(u, u // 2, u % 2)
            for b in range(8):
                dve.wait_ge(xs_hi, b + 1)
                for k in range(2):
                    last = nc.vector.scalar_tensor_tensor(
                        out=xs[:, 1, 2 * b + k, :], in0=ps[:, b, k * SEQ:(k + 1) * SEQ],
                        scalar=vecs[:, V_MIX + 2 * b + k:V_MIX + 2 * b + k + 1],
                        in1=xs[:, 0, 2 * b + k, :].bitcast(F32), op0=ALU.mult, op1=ALU.subtract)
                last.then_inc(xs_lo, 1)
            dve.wait_ge(smalls_loaded, SMALLS)
            for g in range(NG):
                for u in (2 * g + 3, 2 * g + 4):
                    if u < UNIT_ATT:
                        unit(u, u // 2, u % 2)
                for t in range(NT):
                    if t == 0:
                        dve.wait_ge(tile0_done, g + 1)
                    else:
                        dve.wait_ge(unit_used, 2 * g + 2)
                    if g:
                        dve.wait_ge(resid_added, 2 * g + t - 1)
                    nc.vector.tensor_tensor(mixed[:, t, :], ps[:, 4 + t, :], scale_bc[:, g * BLK:(g + 1) * BLK],
                                            ALU.mult).then_inc(mixed_done, 1)
                    rb = resid[:, t, g * BLK:(g + 1) * BLK]
                    dve.wait_ge(mixed_done, 2 * g + t + 1)
                    nc.vector.tensor_tensor(rb, rb, mixed[:, t, :], ALU.add).then_inc(resid_added, 1)
                if g:
                    router_rows(0, g - 1)
                    tile0_parts(0, g - 1)
                    tile0_last(0, g - 1)
            moe(0)

            def att_unit(g, j, i=0):
                kind = j // 8
                unit(UNIT_ATT + 24 * g + j, START_ATT + SLOTS * g + j // 2, j % 2,
                     (V_KV, V_Q, V_KV)[kind] + 2 * (j % 8), i, 24)

            def head_squares(g, kind):
                for t in range(NT):
                    dve.wait_ge(proj_out, 6 * g + 2 * kind + t + 1)
                    dve.wait_ge(table_loaded, TABLES)
                    nc.vector.tensor_tensor(squares[:, :, :], raw[:, t], raw[:, t], ALU.mult).then_inc(sq_done, 1)
                    dve.wait_ge(sq_done, 8 * g + 4 * kind + 2 * t + 1)
                    nc.vector.tensor_reduce(head_ssq[:, t, :], squares[:, :, :], AX_X, ALU.add).then_inc(sq_done, 1)
                    dve.wait_ge(sq_done, 8 * g + 4 * kind + 2 * t + 2)
                nc.vector.tensor_scalar(head_ssq[:, :, :], head_ssq[:, :, :], 1.0 / HD, EPS,
                                        ALU.mult, ALU.add).then_inc(head_sums, 1)

            def head_scale(g, kind):
                dve.wait_ge(head_rs_done, 2 * g + kind + 1)
                nc.vector.tensor_tensor(raw[:, :, :, :], raw[:, :, :, :],
                                        head_rs[:, :, :].unsqueeze(3).to_broadcast([P, NT, HG, HD]),
                                        ALU.mult).then_inc(head_normed, 1)

            def softplus(g):
                dve.wait_ge(ln_done, g + 1)
                nc.vector.scalar_tensor_tensor(out=soft[:, :, :], in0=ps[:, 0:HG, 0:ZC], scalar=0.0, in1=lnk[:, :, :],
                                               op0=ALU.max, op1=ALU.add).then_inc(soft_done, 1)
                dve.wait_ge(soft_done, 2 * g + 1)
                nc.vector.scalar_tensor_tensor(out=soft[:, :, :],
                                               in0=const[:, C_ADD:C_ADD + ZC].unsqueeze(1).to_broadcast([P, HG, ZC]),
                                               scalar=0.0, in1=soft[:, :, :], op0=ALU.is_ge,
                                               op1=ALU.mult).then_inc(soft_done, 1)

            def shift(g):
                dve.wait_ge(cum_done, g + 1)
                nc.vector.tensor_tensor(lnk[:, :, :], ps[:, 0:HG, 0:ZC],
                                        const[:, C_ADD:C_ADD + ZC].unsqueeze(1).to_broadcast([P, HG, ZC]),
                                        ALU.add).then_inc(shift_done, 1)

            def outputs(g):
                for b in range(2):
                    dve.wait_ge(o_done, 2 * g + b + 1)
                    nc.vector.tensor_copy(oT[:, bass.ds(HG * g + 2 * b, 2), :],
                                          ps[:, 6 + b, :].rearrange("p (h q) -> p h q", h=2)).then_inc(o_out, 1)

            def group(g, i, first):
                G = g + i

                def units(*js):
                    for j in js:
                        att_unit(g, j, i)

                if not first:
                    units(0, 1, 2)
                    softplus(G - 1)
                units(3, 4, 5, 6, 7, 8, 9)
                head_squares(G, 0)
                units(10)
                head_scale(G, 0)
                units(11)
                if not first:
                    shift(G - 1)
                units(12, 13, 14, 15, 16, 17)
                if not first:
                    outputs(G - 1)
                head_squares(G, 1)
                units(18)
                head_scale(G, 1)
                units(19, 20, 21, 22, 23)

            att_unit(0, 0)
            for b in range(8):
                dve.wait_ge(xs_hi, 8 + b + 1)
                nc.vector.tensor_tensor(xs[:, 1, 2 * b:2 * b + 2, :],
                                        ps[:, X_BANKS[b], :].rearrange("p (k t) -> p k t", k=2),
                                        xs[:, 0, 2 * b:2 * b + 2, :].bitcast(F32), ALU.subtract).then_inc(xs_lo, 1)
            att_unit(0, 1)
            att_unit(0, 2)
            mean_square(2, True)
            group(0, 0, True)
            with dve.Fori(1, NG) as g:
                group(1, g - 1, False)

            def o_unit(j):
                unit(UNIT_O + j, START_O + j // 2, j % 2)

            def o_chunk(c):
                dve.wait_ge(xs_hi, 16 + c + 1)
                if c < 3:
                    nc.vector.tensor_tensor(xs[:, 1, 4 * c:4 * c + 4, :], oT[:, 4 * c:4 * c + 4, :],
                                            xs[:, 0, 4 * c:4 * c + 4, :].bitcast(F32), ALU.subtract).then_inc(xs_lo, 1)
                else:
                    nc.vector.tensor_tensor(xs[:, 1, 12:16, :].rearrange("p (b h) t -> p b (h t)", b=2), ps[:, 6:8, :],
                                            xs[:, 0, 12:16, :].rearrange("p (b h) t -> p b (h t)", b=2).bitcast(F32),
                                            ALU.subtract).then_inc(xs_lo, 1)

            o_unit(0)
            o_chunk(0)
            o_unit(1)
            o_unit(2)
            o_chunk(1)
            softplus(NG - 1)
            o_chunk(2)
            o_unit(3)
            o_unit(4)
            shift(NG - 1)
            o_unit(5)
            o_unit(6)
            o_chunk(3)
            o_unit(7)
            for c in range(NBLK):
                if c + 1 < NBLK:
                    o_unit(8 * c + 8)
                    o_unit(8 * c + 9)
                for t in range(NT):
                    if t == 0:
                        dve.wait_ge(tile0_done, TILE0_O + c + 1)
                    else:
                        dve.wait_ge(unit_used, UNIT_O + 8 * c + 8)
                    rb = resid[:, t, c * BLK:(c + 1) * BLK]
                    nc.vector.tensor_tensor(rb, rb, ps[:, 4 + t, :], ALU.add).then_inc(resid_added, 1)
                if c + 1 < NBLK:
                    o_unit(8 * c + 10)
                    tile0_parts(1, c)
                    o_unit(8 * c + 11)
                    o_unit(8 * c + 12)
                    tile0_last(1, c)
                    o_unit(8 * c + 13)
                    router_rows(1, c)
                    o_unit(8 * c + 14)
                    o_unit(8 * c + 15)
            moe(1)
            nc.vector.tensor_copy(most[:], ssq[:, 0:1]).then_inc(final_ready, 1)

        @block.tensor
        def _(pe):
            mm = nc.tensor.matmul

            def unit(u, tiles, first, last_unit, free=None, i=0, per_u=0):
                pe.wait_ge(unit_lo, u + 1 + i * per_u)
                b = u % UNIT_BUFS
                for t in range(NT):
                    if first and free is not None:
                        free(t)
                    for j, k in enumerate(tiles):
                        cols = slice(t * P, (t + 1) * P)
                        for n, (px, pw) in enumerate(((0, 0), (0, 1), (1, 0))):
                            last = mm(ps[:, 4 + t, :], xs[:, px, k, cols], ws[:, b, pw, j, :],
                                      start=(first and j == 0 and n == 0), stop=(last_unit and j == 1 and n == 2))
                    if last_unit and t == 0:
                        last.then_inc(tile0_done, 1)
                last.then_inc(unit_used, 1)

            def turn_block(l, c):
                pe.wait_ge(resid_added, (0, ADD_O)[l] + 2 * c + 2)
                if c > 1:
                    pe.wait_ge(turned_out, 8 * l + 2 * (c - 2) + 2)
                for j in range(4):
                    k = 4 * c + j
                    for t in range(NT):
                        col = (j % 2) * SEQ + t * P
                        last = nc.tensor.transpose(ps[:, 2 * (c % 2) + j // 2, col:col + P],
                                                   resid[:, t, k * P:(k + 1) * P], ident)
                    if j % 2:
                        last.then_inc(turned, 1)

            def route_block(l, c):
                for j in range(4):
                    if j % 2 == 0:
                        pe.wait_ge(turned_out, 8 * l + 2 * c + j // 2 + 1)
                    k = 4 * c + j
                    last = mm(ps[0:20, 6, 0:SEQ], w_route[:, l, k, :], xr[:, k, :], start=(k == 0), stop=(k == KD - 1))
                if c == NBLK - 1:
                    last.then_inc(route_mm, 1)

            def moe(l):
                n0 = START_MOE[l]
                add0 = ADD_BASE[l]
                turn_block(l, NBLK - 1)
                route_block(l, NBLK - 1)
                pe.wait_ge(hidT_done, (EXP + 1) * l + 1)
                for t in range(NT):
                    last = nc.tensor.transpose(ps[:, 7, 32 * t:32 * t + 20], logitsT[:, t * P:(t + 1) * P],
                                               const[0:20, C_ID:C_ID + 20])
                last.then_inc(route_mm, 1)
                pe.wait_ge(member_done, l + 1)
                mm(ps[:, 7, 64:80], tri, member[:, 0, :], start=True, stop=True)
                mm(ps[:, 7, 80:96], ones, member[:, 0, :], start=True, stop=False)
                mm(ps[:, 7, 80:96], tri, member[:, 1, :], start=False, stop=True)
                mm(ps[:, 7, 96:112], ones, member[:, 0, :], start=True, stop=False)
                mm(ps[:, 7, 96:112], ones, member[:, 1, :], start=False, stop=True).then_inc(route_mm, 1)

                def gather(e):
                    for t in range(NT):
                        last = mm(ps[0:CAP, e, 508:511], pick[:, t, e, :], rs_parts[:, t, :], start=(t == 0),
                                  stop=(t == NT - 1))
                    last.then_inc(rs_gathered, 1)
                    for k in range(KD):
                        for s in range(3):
                            for t in range(NT):
                                last = mm(ps[:, 6 + k // 8, (k % 8) * CAP:(k % 8 + 1) * CAP],
                                          parts[:, s, t, k * P:(k + 1) * P], pick[:, t, e, :],
                                          start=(s == 0 and t == 0), stop=(s == 2 and t == NT - 1))
                    last.then_inc(gathered, 1)

                PICKS = (NPAIR + 1) * l
                XG = (EXP + 1) * l
                for t in range(NT):
                    pe.wait_ge(lo_done[t], NBLK * (l + 1))
                pe.wait_ge(rs_parts_done, l + 1)
                pe.wait_ge(pick_done, PICKS + 1)
                gather(0)
                with pe.Fori(0, NPAIR) as i:
                    for b in range(2):
                        pe.wait_ge(xg_done, XG + 2 * i + b + 1)
                        pe.wait_ge(hidT_done, (EXP + 1) * l + 2 * i + b + 1)
                        for q in range(4):
                            n = n0 + SLOTS * b + 2 * q
                            slot_in(pe, n, i, PAIR_SLOTS)
                            slot_in(pe, n + 1, i, PAIR_SLOTS)
                            for j in range(4):
                                k = 4 * q + j
                                for h in range(2):
                                    last = mm(ps[CAP * h:CAP * h + CAP, b, :], xg[:, b, k, :], four(n + h)[:, j, :],
                                              start=(k == 0), stop=(k == KD - 1))
                            last.then_inc(slot_read, 2)
                        if b == 1:
                            pe.wait_ge(pick_done, PICKS + i + 2)
                        gather(1 - b)
                        pe.wait_ge(rs_slot_done, XG + 2 * i + b + 2)
                        pe.wait_ge(put_done, PICKS + i + 1)
                        pe.wait_ge(hid_done, EXP * l + 2 * i + b + 1)
                        nc.tensor.transpose(ps[:, 1 - b, SEQ:SEQ + P], put[:, b].rearrange("p e s -> p (e s)"), ident)
                        for k in range(KF):
                            last = nc.tensor.transpose(ps[:, 1 - b, k * CAP:(k + 1) * CAP], hid[:, k * P:(k + 1) * P],
                                                       const[0:CAP, C_ID:C_ID + CAP])
                        last.then_inc(hid_turned, 1)
                        pe.wait_ge(hidT_done, (EXP + 1) * l + 2 * i + b + 2)
                        if b == 1:
                            pe.wait_ge(y_act, EXP * l + 2 * i + 1)
                            pe.wait_ge(y_dve, EXP * l + 2 * i + 1)
                        for k in range(KF):
                            n = n0 + SLOTS * b + 8 + k
                            slot_in(pe, n, i, PAIR_SLOTS)
                            for c in range(NBLK):
                                h = c % 2
                                last = mm(ps[CAP * h:CAP * h + CAP, 2 + c // 2, :], hidT[:, b, k, :],
                                          slot(n)[:, c * BLK:(c + 1) * BLK], start=(k == 0), stop=(k == KF - 1))
                            last.then_inc(slot_read, 1)
                    pe.wait_ge(y_act, EXP * l + 2 * i + 2)
                    pe.wait_ge(y_dve, EXP * l + 2 * i + 2)
                    for m in range(8):
                        c, t = m // 2, m % 2
                        pe.wait_ge(resid_added, add0 + 8 * i + m - 1)
                        mm(ps[:, 4 + t, :], putT[:, t * P:(t + 1) * P], y_rows[:, c * BLK:(c + 1) * BLK],
                           start=True, stop=True).then_inc(mix_done, 1)
                pe.wait_ge(route_dve, 3 * (l + 1))
                count = pe.value_load(flags[0:1, l:l + 1], min_val=0, max_val=SEQ)
                with pe.If(count > CAP):
                    o = over[l]
                    pe.wait_ge(resid_added, add0 + 8 * NPAIR)
                    pe.wait_ge(xg_done, (EXP + 1) * (l + 1))
                    with pe.Fori(0, EXP) as e:
                        pe.wait_ge(o["loaded"], 16 * SLOTS * e + 16 * SLOTS)
                        for t in range(NT):
                            for h in range(2):
                                for k in range(KD):
                                    last = mm(ps[:, h, :], xr[:, k, t * P:(t + 1) * P], four(2 * (k // 4) + h)[:, k % 4, :],
                                              start=(k == 0), stop=(k == KD - 1))
                            last.then_inc(o["gu"], 1)
                            pe.wait_ge(o["hid"], NT * e + t + 1)
                            for k in range(KF):
                                last = nc.tensor.transpose(ps[:, 2, k * P:(k + 1) * P], o_hid[:, k * P:(k + 1) * P], ident)
                            last.then_inc(o["turned"], 1)
                            pe.wait_ge(o["hidT"], NT * e + t + 1)
                            for c in range(NBLK):
                                for k in range(KF):
                                    last = mm(ps[:, 4 + c, :], o_hidT[:, k, :], slot(8 + k)[:, c * BLK:(c + 1) * BLK],
                                              start=(k == 0), stop=(k == KF - 1))
                            last.then_inc(o["down"], 1)
                            pe.wait_ge(o["added"], 4 * NT * e + 4 * t + 4)
                with pe.Else():
                    pe.nop()

            pe.wait_ge(table_loaded, TABLES)
            pe.wait_ge(band_loaded, 32)
            nc.tensor.transpose(ps[:, 4, 0:V_END], vec_rows[:, :], const[0:V_END, C_ID:C_ID + V_END]).then_inc(vec_turned, 1)
            pe.wait_ge(route_loaded, 64)
            for l in range(2):
                for g in range(5):
                    rows = route_rows[:, l, g].rearrange("k (p e) -> k e p", e=4)
                    for e in range(4):
                        c = 128 + KD * (4 * g + e)
                        last = nc.tensor.transpose(ps[:, 6 + l, c:c + KD], rows[:, e, :], const[0:KD, C_ID:C_ID + KD])
            last.then_inc(vec_turned, 1)
            for t in range(NT):
                pe.wait_ge(x_loaded[t], 16)
            pe.wait_ge(band_done, 2)
            for b in range(8):
                g = b // 2
                if b == 6:
                    pe.wait_ge(vec_done, 2)
                for k in (2 * b, 2 * b + 1):
                    c = (k % 2) * SEQ
                    mm(ps[:, b, c:c + SEQ], resid[:, 0, k * P:(k + 1) * P], band_s[:, g, 0:2, :], start=True, stop=False)
                    last = mm(ps[:, b, c + P:c + SEQ], resid[:, 1, k * P:(k + 1) * P], band_s[:, g, 2, :],
                              start=False, stop=True)
                last.then_inc(turned, 1)
            pe.wait_ge(xs_lo, 8)
            for g in range(NG):
                def added(t, g=g):
                    if g:
                        pe.wait_ge(resid_added, 2 * (g - 1) + t + 1)

                unit(2 * g, (4 * g, 4 * g + 1), True, False, added)
                unit(2 * g + 1, (4 * g + 2, 4 * g + 3), False, True)
                if g > 0:
                    turn_block(0, g - 1)
                if g > 1:
                    route_block(0, g - 2)
            route_block(0, NBLK - 2)
            moe(0)

            pe.wait_ge(resid_added, ADD_O)
            for b in range(8):
                if b >= 6:
                    pe.wait_ge(xs_lo, 8 + b - 6 + 1)
                for k in (2 * b, 2 * b + 1):
                    for t in range(NT):
                        c = (k % 2) * SEQ + t * P
                        last = nc.tensor.transpose(ps[:, X_BANKS[b], c:c + P], resid[:, t, k * P:(k + 1) * P], ident)
                last.then_inc(turned, 1)

            def att_unit(g, j, i=0, first=False):
                kind = j // 8

                def evacuated(t):
                    if not first:
                        pe.wait_ge(proj_out, 6 * (g + i) + 2 * kind + t - 1)

                if first:
                    pe.wait_ge(xs_lo, 8 + j + 1)
                unit(UNIT_ATT + 24 * g + j, (2 * (j % 8), 2 * (j % 8) + 1), j % 8 == 0, j % 8 == 7, evacuated, i, 24)

            def turn_heads(g, kind):
                pe.wait_ge(head_normed, 2 * g + kind + 1)
                for t in range(NT):
                    for h in range(HG):
                        last = nc.tensor.transpose(ps[:, 6 + t, h * P:(h + 1) * P], raw[:, t, h, :], ident)
                    last.then_inc(heads_turned, 1)

            def scores(g):
                pe.wait_ge(heads_out, 4 * g + 4)
                for h in range(HG):
                    mm(ps[:, h, 0:SEQ], kT[:, h, 0:P], qT[:, h, :], start=True, stop=False, skip_group_check=True)
                    last = mm(ps[:, h, SEQ:ZC], kT[:, h, P:SEQ], qT[:, h, P:SEQ], start=False, stop=True,
                              skip_group_check=True)
                last.then_inc(z_done, 1)

            def suffix_sums(g):
                pe.wait_ge(soft_done, 2 * g + 2)
                for h in range(HG):
                    mm(ps[:, h, 0:ZC], const[:, C_NSUF:C_NSUF + P], soft[:, h, :], start=False, stop=False,
                       skip_group_check=True)
                    last = mm(ps[:, h, P:SEQ], const[:, C_NONE:C_NONE + P], soft[:, h, SEQ:ZC], start=False, stop=True,
                              skip_group_check=True)
                last.then_inc(cum_done, 1)

            def mix_values(g):
                pe.wait_ge(att_done, g + 1)
                for h in range(HG):
                    c = (h % 2) * SEQ
                    mm(ps[:, 6 + h // 2, c:c + SEQ], vrow[:, 0, h * P:(h + 1) * P], att[:, h, 0:SEQ], start=True,
                       stop=False)
                    last = mm(ps[:, 6 + h // 2, c + P:c + SEQ], vrow[:, 1, h * P:(h + 1) * P], att[:, h, SEQ:ZC],
                              start=False, stop=True)
                    if h % 2:
                        last.then_inc(o_done, 1)

            def group(g, i, first):
                G = g + i
                if not first:
                    scores(G - 1)
                for j in range(8):
                    att_unit(g, j, i, first)
                if not first:
                    suffix_sums(G - 1)
                for j in range(8, 12):
                    att_unit(g, j, i)
                turn_heads(G, 0)
                for j in range(12, 16):
                    att_unit(g, j, i)
                pe.wait_ge(heads_out, 4 * G + 2)
                if not first:
                    mix_values(G - 1)
                for j in range(16, 20):
                    att_unit(g, j, i)
                if not first:
                    pe.wait_ge(o_out, 2 * G)
                turn_heads(G, 1)
                for j in range(20, 24):
                    att_unit(g, j, i)

            group(0, 0, True)
            with pe.Fori(1, NG) as g:
                group(1, g - 1, False)

            def o_unit(j):
                def free(t):
                    if j == 0:
                        pe.wait_ge(proj_out, 6 * NG - 1 + t)
                    else:
                        pe.wait_ge(resid_added, ADD_O + 2 * (j // 8 - 1) + t + 1)

                if j < 8 and j % 2 == 0:
                    pe.wait_ge(xs_lo, 16 + j // 2 + 1)
                unit(UNIT_O + j, (2 * (j % 8), 2 * (j % 8) + 1), j % 8 == 0, j % 8 == 7, free)

            scores(NG - 1)
            for j in range(4):
                o_unit(j)
            suffix_sums(NG - 1)
            o_unit(4)
            o_unit(5)
            pe.wait_ge(heads_out, 4 * NG)
            pe.wait_ge(proj_out, 6 * NG)
            mix_values(NG - 1)
            o_unit(6)
            o_unit(7)
            for c in range(1, NBLK):
                for j in range(4):
                    o_unit(8 * c + j)
                if c == 1:
                    pe.wait_ge(shift_done, NG)
                turn_block(1, c - 1)
                for j in range(4, 8):
                    o_unit(8 * c + j)
                route_block(1, c - 1)
            moe(1)


_INS = ["x", "norm_mix", "norm_ffn", "pool_w", "pool_scale", "kv_norm", "w_kv", "k_norm", "w_q", "q_norm", "w_o",
        "moe_w_grp", "moe_b_grp", "moe_w_rt", "moe_b_rt", "moe_w_gate", "moe_w_up", "moe_w_down"]


def kernel(**inputs):
    import concourse.bacc as bacc
    from concourse.bass_utils import run_bass_kernel_spmd

    nc = bacc.Bacc("TRN2", target_bir_lowering=False, num_devices=1, dynamic_dma_scratch_size=1024)
    arrays, args = {}, []
    tables = {"constant_table": constant_table(), "band_table": band_table()}
    for name in [*_INS, *tables]:
        a = tables[name] if name in tables else np.ascontiguousarray(inputs[name])
        arrays[f"in_{name}"] = a
        args.append(nc.dram_tensor(f"in_{name}", a.shape, mybir.dt.from_np(a.dtype), kind="ExternalInput").ap())
    out = nc.dram_tensor("out_rows", (1, SEQ, D), F32, kind="ExternalOutput").ap()
    build(nc, *args, out)
    r = run_bass_kernel_spmd(nc, [arrays], core_ids=[0])
    return r.results[0]["out_rows"]
```

```python
from contextlib import ExitStack

import numpy as np

import concourse.bass as bass
from concourse import mybir

F32 = mybir.dt.float32
BF16 = mybir.dt.bfloat16
I32 = mybir.dt.int32
ALU = mybir.AluOpType
ACT = mybir.ActivationFunctionType
AX_X = mybir.AxisListType.X

P = 128
SEQ = 256
D = 2048
NT = SEQ // P
KD = D // P
NG = 4
GD = D // NG
WINDOWS = (2, 4, 8, 16)
HD = 128
NH = D // HD
HG = NH // NG
EXP = 16
EPG = EXP // NG
FF = 512
KF = FF // P
CAP = 64
NPAIR = EXP // 2
NBLK = 4
BLK = D // NBLK
SLOTS = 12
PAIR_SLOTS = 2 * SLOTS
UNIT_BUFS = 3
EPS = 1e-6
BIG = 1e30
F32R = mybir.dt.float32r
ZC = SEQ + P

C_ID, C_TRI, C_ONE, C_NSUF, C_NONE, C_ADD = 0, 128, 256, 384, 512, 640
C_IOTA = C_ADD + ZC
C_RANK = C_IOTA + CAP
C_END = C_RANK + 4
BANDS = NG * 3 * P
V_MIX, V_KV, V_Q, V_FFN, V_HEAD, V_END = 0, 16, 32, 48, 80, 82


def constant_table():
    c = np.zeros((P, C_END), np.float32)
    row, col = np.arange(P)[:, None], np.arange(P)[None, :]
    c[:, C_ID:C_ID + P] = row == col
    c[:, C_TRI:C_TRI + P] = row < col
    c[:, C_ONE:C_ONE + P] = 1.0
    c[:, C_NSUF:C_NSUF + P] = -(row >= col).astype(np.float32)
    c[:, C_NONE:C_NONE + P] = -1.0
    seen = (row < col).astype(np.float32)
    c[:, C_ADD:C_ADD + ZC] = (np.concatenate([seen, np.ones((P, P), np.float32), seen], 1) - 1.0) * BIG
    c[:, C_IOTA:C_IOTA + CAP] = np.arange(CAP)
    c[:, C_RANK:C_RANK + 4] = [4, 3, 2, 1]
    return c


def band_table():
    src, dst = np.arange(SEQ)[:, None], np.arange(SEQ)[None, :]
    out = np.zeros((P, NG, 3, P), np.float32)
    for g, w in enumerate(WINDOWS):
        m = ((src <= dst) & (src > dst - w)) / np.minimum(dst + 1, w) - (src == dst)
        out[:, g, 0], out[:, g, 1], out[:, g, 2] = m[:P, :P], m[:P, P:], m[P:, P:]
    return out.reshape(P, BANDS)


def build(nc, x, norm_mix, norm_ffn, pool_w, pool_scale, kv_norm, w_kv, k_norm, w_q, q_norm, w_o,
          w_grp, b_grp, w_rt, b_rt, w_gate, w_up, w_down, table, bands, out):
    with ExitStack() as ctx:
        def sb(name, shape, dt=F32):
            return ctx.enter_context(nc.sbuf_tensor(name, shape, dt))

        def sem(name):
            return ctx.enter_context(nc.semaphore(name))

        ring = sb("ring", [P, SLOTS, 2048])
        resid = sb("resid", [P, NT, D])
        const = sb("const", [P, C_END])
        vecs = sb("vecs", [P, V_END])
        ffn_gain = sb("ffn_gain", [P, 2, KD])
        bias = sb("bias", [P, 2, 20])
        w_route = sb("w_route", [P, 2, KD, 20])
        ssq_part = sb("ssq_part", [P, NT, NBLK])
        ssq = sb("ssq", [P, NT])
        rs = sb("rs", [P, NT])
        rs_rest = sb("rs_rest", [P, NT])
        rs_parts = sb("rs_parts", [P, NT, 3], BF16)
        rs_slot = sb("rs_slot", [CAP, 2])
        half = sb("half", [P, NT * HG])
        head_ssq = sb("head_ssq", [P, NT, HG])
        head_rs = sb("head_rs", [P, NT, HG])
        flags = sb("flags", [1, 2], I32)
        most = sb("most", [P, 1])
        counters = sb("counters", [P, 2, P], BF16)
        KB = 1024
        ARENA = -(-nc.sbuf_base // 32) * 32
        sb("arena", [P, 102 * KB // 4])

        def at(offset, name, shape, dt=F32):
            return nc.alloc_sbuf_tensor_at(name, shape, dt, offset=ARENA + offset)


        xs = at(0, "xs", [P, 2, KD, SEQ], F32R)
        ws = at(32 * KB, "ws", [P, UNIT_BUFS, 2, 2, BLK], F32R)
        junk_rows = at(20 * KB, "junk_rows", [P, D])
        band = at(56 * KB, "band", [P, NG, 3, P])
        band_s = at(62 * KB, "band_s", [P, NG, 3, P])
        vec_rows = at(72 * KB, "vec_rows", [V_END, P])
        route_rows = at(74 * KB, "route_rows", [KD, 2, 5, 4 * P])
        mixed = at(68 * KB, "mixed", [P, NT, BLK])
        scale_bc = ring[:, SLOTS - 1, :]
        xr = at(56 * KB, "xr", [P, KD, SEQ])
        parts = at(72 * KB, "parts", [P, 3, NT, D], BF16)
        rest = at(96 * KB, "rest", [P, NT, BLK])
        junk = at(100 * KB, "junk", [P, BLK])
        oT = at(56 * KB, "oT", [P, NH, SEQ])
        kT = at(72 * KB, "kT", [P, HG, SEQ])
        qT = at(76 * KB, "qT", [P, HG, SEQ])
        vrow = at(80 * KB, "vrow", [P, NT, HG * HD])
        raw = at(84 * KB, "raw", [P, NT, HG, HD])
        lnk = at(88 * KB, "lnk", [P, HG, ZC])
        soft = at(94 * KB, "soft", [P, HG, ZC])
        att = soft
        squares = at(100 * KB, "squares", [P, HG, HD])
        junk_att = at(88 * KB, "junk_att", [P, D])
        xg = at(0, "xg", [P, 2, KD, CAP])
        y_rows = at(8 * KB, "y_rows", [P, D])
        silu_g = at(16 * KB, "silu_g", [CAP, FF])
        hid = at(18 * KB, "hid", [CAP, FF])
        hidT = at(20 * KB, "hidT", [P, 2, KF, CAP])
        pick = at(22 * KB, "pick", [P, NT, 2, CAP], BF16)
        put = at(23 * KB, "put", [P, NT, 2, CAP])
        putT = at(24 * KB, "putT", [P, SEQ])
        logitsT = at(25 * KB, "logitsT", [20, SEQ])
        lg = at(26 * KB, "lg", [P, NT, 20])
        member = at(27 * KB + 512, "member", [P, NT, EXP], BF16)
        gate = at(27 * KB + 768, "gate", [P, NT, EXP + 2])
        slot_of = at(28 * KB, "slot_of", [P, NT, EXP + 2])
        over_gate = at(28 * KB + 256, "over_gate", [P, NT, EXP])
        route5 = at(28 * KB + 512, "route5", [P, 5, NT, 5, 4])
        route4 = at(29 * KB + 512, "route4", [P, 3, NT, 4])
        route1 = at(30 * KB, "route1", [P, 8, NT, 5])
        o_silu = at(32 * KB, "o_silu", [P, FF])
        o_hid = at(34 * KB, "o_hid", [P, FF])
        o_hidT = at(36 * KB, "o_hidT", [P, KF, P])

        ident = const[:, C_ID:C_ID + P]
        ones = const[:, C_ONE:C_ONE + P]
        tri = const[:, C_TRI:C_TRI + P]
        iota = const[:, C_IOTA:C_IOTA + CAP]
        rank = const[:, C_RANK:C_RANK + 4]

        ps = ctx.enter_context(nc.psum_tensor("ps", [P, 8, 512], F32))

        slot_loaded = [sem(f"slot_loaded{j}") for j in range(SLOTS)]
        slot_read = sem("slot_read")
        x_loaded = [sem(f"x_loaded{t}") for t in range(NT)]
        table_loaded = sem("table_loaded")
        band_loaded = sem("band_loaded")
        route_loaded = sem("route_loaded")
        smalls_loaded = sem("smalls_loaded")
        ssq_done = sem("ssq_done")
        ms_done = sem("ms_done")
        pool_step = sem("pool_step")
        rs_done = sem("rs_done")
        band_done = sem("band_done")
        vec_turned = sem("vec_turned")
        vec_done = sem("vec_done")
        turned = sem("turned")
        turned_out = sem("turned_out")
        xs_hi = sem("xs_hi")
        xs_lo = sem("xs_lo")
        unit_hi = sem("unit_hi")
        unit_lo = sem("unit_lo")
        unit_used = sem("unit_used")
        tile0_done = sem("tile0_done")
        mixed_done = sem("mixed_done")
        mix_done = sem("mix_done")
        resid_added = sem("resid_added")
        dve_step = sem("dve_step")
        hi_done = sem("hi_done")
        rest_done = [sem(f"rest_done{t}") for t in range(NT)]
        mid_done = [sem(f"mid_done{t}") for t in range(NT)]
        lo_done = [sem(f"lo_done{t}") for t in range(NT)]
        route_mm = sem("route_mm")
        route_act = sem("route_act")
        route_dve = sem("route_dve")
        member_done = sem("member_done")
        rs_parts_done = sem("rs_parts_done")
        pick_done = sem("pick_done")
        put_done = sem("put_done")
        rs_gathered = sem("rs_gathered")
        rs_slot_done = sem("rs_slot_done")
        gathered = sem("gathered")
        xg_done = sem("xg_done")
        silu_done = sem("silu_done")
        hid_done = sem("hid_done")
        hid_turned = sem("hid_turned")
        hidT_done = sem("hidT_done")
        y_act = sem("y_act")
        y_dve = sem("y_dve")
        over = [{n: sem(f"over{l}_{n}") for n in
                 ("loaded", "gu", "silu", "hid", "turned", "hidT", "down", "added")}
                for l in range(2)]
        proj_out = sem("proj_out")
        sq_done = sem("sq_done")
        head_sums = sem("head_sums")
        head_rs_done = sem("head_rs_done")
        head_normed = sem("head_normed")
        heads_turned = sem("heads_turned")
        heads_out = sem("heads_out")
        z_done = sem("z_done")
        act_step = sem("act_step")
        ln_done = sem("ln_done")
        soft_done = sem("soft_done")
        cum_done = sem("cum_done")
        shift_done = sem("shift_done")
        att_done = sem("att_done")
        o_done = sem("o_done")
        o_out = sem("o_out")
        final_ready = sem("final_ready")
        stored = sem("stored")

        START_MOE = [NG, NG + NPAIR * PAIR_SLOTS + NG * SLOTS + NBLK * 4]
        START_ATT = START_MOE[0] + NPAIR * PAIR_SLOTS
        START_O = START_ATT + NG * SLOTS
        UNIT_ATT = 2 * NG
        UNIT_O = UNIT_ATT + 2 * NG * SLOTS
        ADD_BASE = [8, 16 + 8 * NPAIR]
        ADD_O = 8 + 8 * NPAIR
        TURN_ROUTE = [8, 24]
        TURN_ATT = 16
        TILE0_ATT = NG
        TILE0_O = NG + 3 * NG
        SSQ = [2, 2 + 8, 2 + 8 + 2, 2 + 8 + 2 + 8]
        TABLES = 16 * 7
        SMALLS = 16 * 7

        def slot(n):
            return ring[:, n % SLOTS, :]

        def turn_bank(l, c):
            return 2 * (c % 2) if l else 0

        def four(n):
            return slot(n).rearrange("p (k c) -> p k c", k=4)

        def when_read(n):
            if n < START_MOE[0]:
                return unit_lo, 2 * n + 2
            if n < START_ATT:
                return slot_read, n - START_MOE[0] + 1
            if n < START_O:
                return unit_lo, UNIT_ATT + 2 * (n - START_ATT) + 2
            if n < START_MOE[1]:
                return unit_lo, UNIT_O + 2 * (n - START_O) + 2
            return slot_read, NPAIR * PAIR_SLOTS + n - START_MOE[1] + 1

        def slot_in(eng, n, i=0, per=0):
            eng.wait_ge(slot_loaded[n % SLOTS], 16 * (n // SLOTS + 1) + i * (16 * per // SLOTS))

        w_gate_v = w_gate.rearrange("l e (p k) f -> l e p k f", k=KD)
        w_up_v = w_up.rearrange("l e (p k) f -> l e p k f", k=KD)
        w_down_v = w_down.rearrange("l e (k p) d -> l e p k d", p=P)
        w_gate_k = w_gate.rearrange("l e (k p) f -> l e p k f", p=P)
        w_up_k = w_up.rearrange("l e (k p) f -> l e p k f", p=P)
        w_kv_v = w_kv.rearrange("(k p) (b c) -> b p k c", p=P, c=BLK)
        w_q_v = w_q[0].rearrange("(k p) (b c) -> b p k c", p=P, c=BLK)
        w_o_v = w_o[0].rearrange("(k p) (b c) -> b p k c", p=P, c=BLK)
        pool_w_v = pool_w[0].rearrange("g (k p) c -> g p k c", p=P)

        MIX_BANKS = (4, 2)
        X_BANKS = (0, 1, 2, 3, 6, 7, 0, 1)

        def in_tiles(s, t, c):
            return parts[:, s, t, :].rearrange("q (k p) -> q p k", k=KD)[:, c * (BLK // KD):(c + 1) * (BLK // KD), :]

        block = ctx.enter_context(nc.Block())

        @block.sync
        def _(sp):
            def load(n, src, dst=None, i=0, per=0):
                if n >= SLOTS:
                    before, value = when_read(n - SLOTS)
                    sp.wait_ge(before, value + i * per * (2 if before is unit_lo else 1))
                if n == SLOTS - 1:
                    sp.wait_ge(mixed_done, 8)
                sp.dma_start(four(n) if dst is None else dst, src).then_inc(slot_loaded[n % SLOTS], 16)

            def expert(l, e, n0, i=0, per=0):
                for q in range(4):
                    for h, w in enumerate((w_gate_v, w_up_v)):
                        load(n0 + 2 * q + h, w[l, e, :, 4 * q:4 * q + 4, :], None, i, per)
                for q in range(KF):
                    load(n0 + 8 + q, w_down_v[l, e, :, q, :], slot(n0 + 8 + q), i, per)

            def moe(l):
                n0 = START_MOE[l]
                expert(l, 0, n0)
                expert(l, 1, n0 + SLOTS)
                with sp.Fori(1, NPAIR) as i:
                    for b in range(2):
                        expert(l, 2 * i + b, n0 + PAIR_SLOTS + SLOTS * b, i - 1, PAIR_SLOTS)
                sp.wait_ge(route_dve, 3 * (l + 1))
                count = sp.value_load(flags[0:1, l:l + 1], min_val=0, max_val=SEQ)
                with sp.If(count > CAP):
                    sp.wait_ge(slot_read, NPAIR * PAIR_SLOTS * (l + 1))

                    def again(e):
                        for q in range(4):
                            for h, w in enumerate((w_gate_k, w_up_k)):
                                sp.dma_start(four(2 * q + h), w[l, e, :, 4 * q:4 * q + 4, :]).then_inc(over[l]["loaded"], 16)
                            sp.dma_start(slot(8 + q), w_down_v[l, e, :, q, :]).then_inc(over[l]["loaded"], 16)

                    again(0)
                    with sp.Fori(1, EXP) as e:
                        sp.wait_ge(over[l]["down"], NT * e)
                        again(e)
                    sp.wait_ge(over[l]["down"], NT * EXP)
                with sp.Else():
                    sp.nop()

            sp.dma_start(const[:], table).then_inc(table_loaded, 16)
            for row, v in ((V_MIX, norm_mix[0]), (V_KV, kv_norm), (V_Q, norm_mix[1]), (V_FFN, norm_ffn[0]),
                           (V_FFN + KD, norm_ffn[1])):
                sp.dma_start(vec_rows[row:row + KD, :], v.rearrange("(k p) -> k p", p=P)).then_inc(table_loaded, 16)
            sp.dma_start(vec_rows[V_HEAD:V_HEAD + 1, :], k_norm.rearrange("(a p) -> a p", a=1)).then_inc(table_loaded, 16)
            sp.dma_start(vec_rows[V_HEAD + 1:V_END, :], q_norm).then_inc(band_loaded, 16)
            load(0, pool_w_v[0])
            for l in range(2):
                sp.dma_start(route_rows[:, l, 0], w_grp[l].rearrange("(k p) g -> k (p g)", k=KD)).then_inc(route_loaded, 16)
                sp.dma_start(route_rows[:, l, 1:5], w_rt[l].rearrange("g (k p) e -> k g (p e)", k=KD)).then_inc(route_loaded, 16)
            load(1, pool_w_v[1])
            sp.dma_start(scale_bc, pool_scale.to_broadcast([P, D])).then_inc(smalls_loaded, 16)
            load(2, pool_w_v[2])
            load(3, pool_w_v[3])
            for l in range(2):
                sp.dma_start(ffn_gain[:, l, :], norm_ffn[l].rearrange("(p k) -> p k", k=KD)).then_inc(smalls_loaded, 16)
                sp.dma_start(bias[:, l, 0:4], b_grp[l:l + 1, :].to_broadcast([P, 4])).then_inc(smalls_loaded, 16)
                sp.dma_start(bias[:, l, 4:20], b_rt[l:l + 1].rearrange("a g e -> a (g e)").to_broadcast([P, EXP])).then_inc(smalls_loaded, 16)
            moe(0)

            def group(g, n, i):
                for kind, src in enumerate((w_kv_v[g], w_q_v[g], w_kv_v[g + NG])):
                    for q in range(4):
                        load(n + 4 * kind + q, src[:, 4 * q:4 * q + 4, :], None, i, SLOTS)

            group(0, START_ATT, 0)
            with sp.Fori(1, NG) as g:
                group(g, START_ATT + SLOTS, g - 1)
            for b in range(NBLK):
                for q in range(4):
                    load(START_O + 4 * b + q, w_o_v[b, :, 4 * q:4 * q + 4, :])
            moe(1)
            sp.wait_ge(final_ready, 1)
            for m in range(8):
                c, t = m // 2, m % 2
                sp.wait_ge(resid_added, ADD_BASE[1] + 8 * (NPAIR - 1) + m + 1)
                sp.dma_start(out[0, t * P:(t + 1) * P, c * BLK:(c + 1) * BLK],
                             resid[:, t, c * BLK:(c + 1) * BLK]).then_inc(stored, 16)
            sp.wait_ge(stored, 16 * 8)

        @block.gpsimd
        def _(pool):
            def inverse_rms(n):
                pool.wait_ge(ms_done, n + 1)
                nc.gpsimd.tensor_tensor(rs[:], ssq[:], half[:, 0:NT], ALU.pow).then_inc(rs_done, 1)

            def tile1_parts(l, c):
                blk = slice(c * BLK, (c + 1) * BLK)
                if l + c:
                    pool.wait_ge(lo_done[1], NBLK * l + c)
                pool.wait_ge(hi_done, 8 * l + 2 * c + 2)
                nc.gpsimd.tensor_tensor(rest[:, 1].rearrange("q (p k) -> q p k", k=KD),
                                        resid[:, 1, blk].rearrange("q (p k) -> q p k", k=KD),
                                        in_tiles(0, 1, c), ALU.subtract).then_inc(rest_done[1], 1)
                pool.wait_ge(mid_done[1], NBLK * l + c + 1)
                nc.gpsimd.tensor_tensor(in_tiles(2, 1, c), rest[:, 1].rearrange("q (p k) -> q p k", k=KD),
                                        in_tiles(1, 1, c), ALU.subtract).then_inc(lo_done[1], 1)

            def tile0_last(l):
                pool.wait_ge(mid_done[0], NBLK * (l + 1))
                nc.gpsimd.tensor_tensor(in_tiles(2, 0, NBLK - 1), rest[:, 0].rearrange("q (p k) -> q p k", k=KD),
                                        in_tiles(1, 0, NBLK - 1), ALU.subtract).then_inc(lo_done[0], 1)

            nc.gpsimd.memset(half[:], -0.5).then_inc(pool_step, 1)
            pool.wait_ge(pool_step, 1)
            inverse_rms(0)
            for c in range(NBLK - 1):
                tile1_parts(0, c)
            inverse_rms(1)
            tile1_parts(0, NBLK - 1)
            tile0_last(0)
            inverse_rms(2)
            hs = head_ssq[:, :, :].rearrange("p t h -> p (t h)")
            hr = head_rs[:, :, :].rearrange("p t h -> p (t h)")
            with pool.Fori(0, NG) as g:
                for kind in range(2):
                    pool.wait_ge(head_sums, 2 * g + kind + 1)
                    nc.gpsimd.tensor_tensor(hr, hs, half[:, :], ALU.pow).then_inc(head_rs_done, 1)
            for c in range(NBLK - 1):
                tile1_parts(1, c)
            inverse_rms(3)
            tile1_parts(1, NBLK - 1)
            tile0_last(1)

        @block.scalar
        def _(act):
            for t in range(NT):
                act.dma_start(resid[:, t, :], x[0, t * P:(t + 1) * P, :]).then_inc(x_loaded[t], 16)
            act.dma_start(band[:, :, :, :], bands.rearrange("p (g b q) -> p g b q", g=NG, b=3)).then_inc(band_loaded, 16)

            def unit(u, n, h, gain=None, used=True, i=0, per_u=0, per_n=0):
                if used:
                    act.wait_ge(unit_used, u - UNIT_BUFS + 1 + i * per_u)
                slot_in(act, n, i, per_n)
                dst = ws[:, u % UNIT_BUFS, 0]
                if gain is None:
                    nc.scalar.activation(dst, four(n)[:, 2 * h:2 * h + 2, :], ACT.Copy).then_inc(unit_hi, 1)
                else:
                    for k in range(2):
                        last = nc.scalar.activation(dst[:, k, :], four(n)[:, 2 * h + k, :], ACT.Copy,
                                                    scale=vecs[:, gain + k:gain + k + 1])
                    last.then_inc(unit_hi, 1)

            def squares_and_first(l, c):
                act.wait_ge(resid_added, (0, ADD_O)[l] + 2 * c + 2)
                for t in range(NT):
                    if c + t or l:
                        act.wait_ge(ssq_done, SSQ[2 * l] + 2 * c + t)
                    nc.scalar.activation(junk[:, :], resid[:, t, c * BLK:(c + 1) * BLK], ACT.Square,
                                         accum_out=ssq_part[:, t, c:c + 1]).then_inc(ssq_done, 1)
                for t in range(NT):
                    nc.scalar.activation(in_tiles(0, t, c),
                                         resid[:, t, c * BLK:(c + 1) * BLK].rearrange("q (p k) -> q p k", k=KD),
                                         ACT.Copy).then_inc(hi_done, 1)

            def second(l, c, t):
                act.wait_ge(rest_done[t], NBLK * l + c + 1)
                nc.scalar.activation(in_tiles(1, t, c), rest[:, t].rearrange("q (p k) -> q p k", k=KD),
                                     ACT.Copy).then_inc(mid_done[t], 1)

            def moe(l):
                n0 = NPAIR * PAIR_SLOTS * l
                act.wait_ge(route_mm, 4 * l + 1)
                nc.scalar.activation(logitsT[:, :], ps[0:20, 6, 0:SEQ], ACT.Copy).then_inc(hidT_done, 1)
                second(l, NBLK - 1, 0)
                second(l, NBLK - 1, 1)
                act.wait_ge(route_dve, 3 * l + 1)
                nc.scalar.activation(route4[:, 0], route4[:, 0], ACT.Exp).then_inc(route_act, 1)
                act.wait_ge(route_dve, 3 * l + 2)
                nc.scalar.activation(route1[:, 3, :, 1:5], route1[:, 3, :, 1:5], ACT.Exp).then_inc(route_act, 1)
                with act.Fori(0, NPAIR) as i:
                    for b in range(2):
                        act.wait_ge(slot_read, n0 + SLOTS * (2 * i + b) + 8)
                        nc.scalar.activation(silu_g[:, :], ps[0:CAP, b, :], ACT.Silu,
                                             scale=rs_slot[:, b:b + 1]).then_inc(silu_done, 1)
                        act.wait_ge(hid_turned, EXP * l + 2 * i + b + 1)
                        nc.scalar.activation(putT[:, b * P:(b + 1) * P], ps[:, 1 - b, SEQ:SEQ + P], ACT.Copy)
                        nc.scalar.activation(hidT[:, b], ps[:, 1 - b, 0:KF * CAP].rearrange("p (k s) -> p k s", k=KF),
                                             ACT.Copy).then_inc(hidT_done, 1)
                        act.wait_ge(slot_read, n0 + SLOTS * (2 * i + b + 1))
                        for h in range(2):
                            last = nc.scalar.activation(
                                y_rows[CAP * b:CAP * b + CAP, 2 * h * BLK:(2 * h + 1) * BLK],
                                ps[0:CAP, 2 + h, :], ACT.Copy)
                        last.then_inc(y_act, 1)
                act.wait_ge(route_dve, 3 * (l + 1))
                count = act.value_load(flags[0:1, l:l + 1], min_val=0, max_val=SEQ)
                with act.If(count > CAP):
                    with act.Fori(0, EXP) as e:
                        for t in range(NT):
                            act.wait_ge(over[l]["gu"], NT * e + t + 1)
                            nc.scalar.activation(o_silu[:, :], ps[:, 0, :], ACT.Silu,
                                                 scale=rs[:, t:t + 1]).then_inc(over[l]["silu"], 1)
                            act.wait_ge(over[l]["turned"], NT * e + t + 1)
                            nc.scalar.activation(o_hidT[:, :, :], ps[:, 2, :].rearrange("p (k s) -> p k s", k=KF),
                                                 ACT.Copy).then_inc(over[l]["hidT"], 1)
                    act.wait_ge(over[l]["added"], 4 * NT * EXP)
                with act.Else():
                    act.nop()

            for t in range(NT):
                act.wait_ge(x_loaded[t], 16)
                if t:
                    act.wait_ge(ssq_done, t)
                nc.scalar.activation(junk_rows[:, :], resid[:, t, :], ACT.Square,
                                     accum_out=ssq[:, t:t + 1]).then_inc(ssq_done, 1)
            act.wait_ge(vec_done, 1)
            for u in range(UNIT_BUFS):
                unit(u, u // 2, u % 2, used=False)
            for b in range(8):
                act.wait_ge(turned, b + 1)
                for k in range(2):
                    last = nc.scalar.activation(xs[:, 0, 2 * b + k, :], ps[:, b, k * SEQ:(k + 1) * SEQ], ACT.Copy,
                                                scale=vecs[:, V_MIX + 2 * b + k:V_MIX + 2 * b + k + 1])
                last.then_inc(xs_hi, 1)
            for g in range(NG):
                for u in (2 * g + 3, 2 * g + 4):
                    if u < UNIT_ATT:
                        unit(u, u // 2, u % 2)
                if g:
                    squares_and_first(0, g - 1)
                    second(0, g - 1, 0)
                    second(0, g - 1, 1)
            squares_and_first(0, NBLK - 1)
            moe(0)

            def att_unit(g, j, used=True, i=0):
                kind = j % 24 // 8
                k = 2 * (j % 8)
                unit(UNIT_ATT + 24 * g + j, START_ATT + SLOTS * g + j // 2, j % 2, (V_KV, V_Q, V_KV)[kind] + k,
                     used, i, 24, SLOTS)

            def projected(g, kind):
                for t in range(NT):
                    if t == 0:
                        act.wait_ge(tile0_done, TILE0_ATT + 3 * g + kind + 1)
                    else:
                        act.wait_ge(unit_used, UNIT_ATT + 24 * g + 8 * kind + 8)
                    dst = vrow[:, t, :] if kind == 2 else raw[:, t].rearrange("p h d -> p (h d)")
                    nc.scalar.activation(dst, ps[:, 4 + t, :], ACT.Copy, scale=rs[:, t:t + 1]).then_inc(proj_out, 1)

            def heads(g, kind):
                for t in range(NT):
                    act.wait_ge(heads_turned, 4 * g + 2 * kind + t + 1)
                    nc.scalar.activation((kT, qT)[kind][:, :, t * P:(t + 1) * P],
                                         ps[:, 6 + t, :].rearrange("p (h q) -> p h q", h=HG),
                                         ACT.Copy, scale=vecs[:, V_HEAD + kind:V_HEAD + kind + 1]).then_inc(heads_out, 1)

            def exp_terms(g):
                act.wait_ge(z_done, g + 1)
                nc.scalar.activation(lnk[:, :, :], ps[:, 0:HG, 0:ZC], ACT.Abs).then_inc(act_step, 1)
                act.wait_ge(act_step, 2 * g + 1)
                nc.scalar.activation(lnk[:, :, :], lnk[:, :, :], ACT.Exp, scale=-1.0).then_inc(act_step, 1)

            def log_terms(g):
                act.wait_ge(act_step, 2 * g + 2)
                nc.scalar.activation(lnk[:, :, :], lnk[:, :, :], ACT.Ln, bias=1.0).then_inc(ln_done, 1)

            def weights(g):
                act.wait_ge(shift_done, g + 1)
                nc.scalar.activation(att[:, :, :], lnk[:, :, :], ACT.Exp).then_inc(att_done, 1)

            def square_rows(t):
                act.wait_ge(ssq_done, SSQ[1] + t)
                nc.scalar.activation(junk_att[:, :], resid[:, t, :], ACT.Square,
                                     accum_out=ssq[:, t:t + 1]).then_inc(ssq_done, 1)

            def group(g, i, first=False, last=False):
                G = g + i

                def units(*js):
                    for j in js:
                        att_unit(g, j, True, i)

                units(2)
                if not first:
                    exp_terms(G - 1)
                units(3)
                if first:
                    square_rows(0)
                else:
                    log_terms(G - 1)
                units(4, 5)
                if first:
                    square_rows(1)
                units(6, 7, 8, 9)
                if first:
                    act.wait_ge(rs_done, 3)
                projected(G, 0)
                units(10, 11)
                if not first:
                    weights(G - 1)
                units(12, 13)
                heads(G, 0)
                units(14, 15, 16, 17)
                projected(G, 1)
                units(18, 19, 20, 21)
                heads(G, 1)
                units(22, 23)
                if last:
                    o_unit(0)
                    o_unit(1)
                else:
                    units(24, 25)
                projected(G, 2)

            def o_unit(j):
                unit(UNIT_O + j, START_O + j // 2, j % 2)

            act.wait_ge(resid_added, ADD_O)
            att_unit(0, 0)
            for b in range(8):
                act.wait_ge(turned, TURN_ATT + b + 1)
                nc.scalar.activation(xs[:, 0, 2 * b:2 * b + 2, :],
                                     ps[:, X_BANKS[b], :].rearrange("p (k t) -> p k t", k=2),
                                     ACT.Copy).then_inc(xs_hi, 1)
                if b == 3:
                    att_unit(0, 1)
            group(0, 0, first=True)
            with act.Fori(1, NG - 1) as g:
                group(1, g - 1)
            group(NG - 1, 0, last=True)

            def o_chunk(c):
                if c == 0:
                    act.wait_ge(unit_used, UNIT_O)
                if c < 3:
                    act.wait_ge(o_out, 2 * c + 2)
                    nc.scalar.activation(xs[:, 0, 4 * c:4 * c + 4, :], oT[:, 4 * c:4 * c + 4, :],
                                         ACT.Copy).then_inc(xs_hi, 1)
                else:
                    act.wait_ge(o_done, 2 * c + 2)
                    nc.scalar.activation(xs[:, 0, 12:16, :].rearrange("p (b h) t -> p b (h t)", b=2), ps[:, 6:8, :],
                                         ACT.Copy).then_inc(xs_hi, 1)

            o_chunk(0)
            o_chunk(1)
            o_unit(2)
            exp_terms(NG - 1)
            o_unit(3)
            log_terms(NG - 1)
            o_chunk(2)
            o_unit(4)
            o_unit(5)
            weights(NG - 1)
            o_unit(6)
            o_unit(7)
            o_chunk(3)
            for c in range(NBLK):
                if c + 1 < NBLK:
                    o_unit(8 * c + 8)
                    o_unit(8 * c + 9)
                squares_and_first(1, c)
                if c + 1 < NBLK:
                    o_unit(8 * c + 10)
                    o_unit(8 * c + 11)
                    second(1, c, 0)
                    second(1, c, 1)
                    for j in range(8 * c + 12, 8 * c + 16):
                        o_unit(j)
            moe(1)

        @block.vector
        def _(dve):
            steps = [0]

            def step(ins):
                steps[0] += 1
                ins.then_inc(dve_step, 1)
                dve.wait_ge(dve_step, steps[0])

            def per_feature(gain, n, width):
                return gain.unsqueeze(2).to_broadcast([P, n, width])

            def unit(u, n, h, gain=None, i=0, per_u=0):
                dve.wait_ge(unit_hi, u + 1 + i * per_u)
                b = u % UNIT_BUFS
                src = four(n)[:, 2 * h:2 * h + 2, :]
                if gain is None:
                    nc.vector.tensor_tensor(ws[:, b, 1], src, ws[:, b, 0].bitcast(F32), ALU.subtract).then_inc(unit_lo, 1)
                else:
                    for k in range(2):
                        last = nc.vector.scalar_tensor_tensor(
                            out=ws[:, b, 1, k, :], in0=src[:, k, :], scalar=vecs[:, gain + k:gain + k + 1],
                            in1=ws[:, b, 0, k, :].bitcast(F32), op0=ALU.mult, op1=ALU.subtract)
                    last.then_inc(unit_lo, 1)

            def tile0_parts(l, c):
                blk = slice(c * BLK, (c + 1) * BLK)
                if l + c:
                    dve.wait_ge(lo_done[0], NBLK * l + c)
                dve.wait_ge(hi_done, 8 * l + 2 * c + 1)
                nc.vector.tensor_tensor(rest[:, 0].rearrange("q (p k) -> q p k", k=KD),
                                        resid[:, 0, blk].rearrange("q (p k) -> q p k", k=KD),
                                        in_tiles(0, 0, c), ALU.subtract).then_inc(rest_done[0], 1)

            def tile0_last(l, c):
                dve.wait_ge(mid_done[0], NBLK * l + c + 1)
                nc.vector.tensor_tensor(in_tiles(2, 0, c), rest[:, 0].rearrange("q (p k) -> q p k", k=KD),
                                        in_tiles(1, 0, c), ALU.subtract).then_inc(lo_done[0], 1)

            def router_rows(l, c):
                for j in range(2):
                    dve.wait_ge(turned, TURN_ROUTE[l] + 2 * c + j + 1)
                    k = 4 * c + 2 * j
                    nc.vector.tensor_tensor(xr[:, k:k + 2, :],
                                            ps[:, turn_bank(l, c) + j, :].rearrange("p (k t) -> p k t", k=2),
                                            per_feature(vecs[:, V_FFN + KD * l + k:V_FFN + KD * l + k + 2], 2, SEQ),
                                            ALU.mult).then_inc(turned_out, 1)

            def mean_square(n, whole):
                dve.wait_ge(ssq_done, SSQ[n])
                if not whole:
                    step(nc.vector.tensor_reduce(ssq[:, :], ssq_part[:, :, :], AX_X, ALU.add))
                nc.vector.tensor_scalar(ssq[:, :], ssq[:, :], 1.0 / D, EPS, ALU.mult, ALU.add).then_inc(ms_done, 1)

            def moe(l):
                n0 = NPAIR * PAIR_SLOTS * l
                add0 = ADD_BASE[l]
                router_rows(l, NBLK - 1)
                mean_square(2 * l + 1, False)
                tile0_parts(l, NBLK - 1)
                dve.wait_ge(rs_done, 2 * l + 2)
                step(nc.vector.tensor_copy(rs_parts[:, :, 0], rs[:, :]))
                step(nc.vector.tensor_tensor(rs_rest[:, :], rs[:, :], rs_parts[:, :, 0], ALU.subtract))
                step(nc.vector.tensor_copy(rs_parts[:, :, 1], rs_rest[:, :]))
                nc.vector.tensor_tensor(rs_parts[:, :, 2], rs_rest[:, :], rs_parts[:, :, 1],
                                        ALU.subtract).then_inc(rs_parts_done, 1)
                dve.wait_ge(route_mm, 4 * l + 2)
                for t in range(NT):
                    step(nc.vector.scalar_tensor_tensor(out=lg[:, t, :], in0=ps[:, 7, 32 * t:32 * t + 20],
                                                        scalar=rs[:, t:t + 1], in1=bias[:, l, :], op0=ALU.mult,
                                                        op1=ALU.add))

                LOGITS = lg[:, :, :].rearrange("p t (r e) -> p t r e", r=5)
                HOT1, HOT2, SEL2, SCORE = (route5[:, j] for j in range(4))
                TOP1, TOP2, BEST, DIFF, DENOM, W1, W2, SUM = (route1[:, j] for j in range(8))
                GROUP_EXP, WITHIN, WITHIN2 = (route4[:, j] for j in range(3))
                GROUP = HOT1[:, :, 0, :]

                def wide(a, n=5):
                    return a.unsqueeze(3).to_broadcast([P, NT, n, 4])

                def first_best(src, top, hot):
                    step(nc.vector.tensor_reduce(top, src, AX_X, ALU.max))
                    step(nc.vector.tensor_tensor(SCORE, src, wide(top), ALU.is_ge))
                    step(nc.vector.tensor_tensor(SCORE, SCORE, rank.unsqueeze(1).unsqueeze(1).to_broadcast([P, NT, 5, 4]),
                                                 ALU.mult))
                    step(nc.vector.tensor_reduce(BEST, SCORE, AX_X, ALU.max))
                    step(nc.vector.tensor_tensor(hot, SCORE, wide(BEST), ALU.is_equal))

                first_best(LOGITS, TOP1, HOT1)
                nc.vector.tensor_tensor(GROUP_EXP, LOGITS[:, :, 0, :], TOP1[:, :, 0:1].to_broadcast([P, NT, 4]),
                                        ALU.subtract).then_inc(route_dve, 1)
                step(nc.vector.scalar_tensor_tensor(out=SEL2, in0=HOT1, scalar=-BIG, in1=LOGITS,
                                                    op0=ALU.mult, op1=ALU.add))
                first_best(SEL2, TOP2, HOT2)
                step(nc.vector.tensor_tensor(SCORE, HOT1, HOT2, ALU.add))
                nc.vector.tensor_tensor(member[:, :, :].rearrange("p t (g e) -> p t g e", g=NG),
                                        wide(GROUP, NG), SCORE[:, :, 1:5, :], ALU.mult).then_inc(member_done, 1)
                nc.vector.tensor_tensor(DIFF, TOP2, TOP1, ALU.subtract).then_inc(route_dve, 1)
                step(nc.vector.memset(slot_of[:, :, EXP:EXP + 2], -1.0))
                dve.wait_ge(route_mm, 4 * l + 3)
                dve.wait_ge(member_done, l + 1)
                count = ps[:, 7, 64:96].rearrange("p (t e) -> p t e", t=2)
                step(nc.vector.scalar_tensor_tensor(out=slot_of[:, :, 0:EXP], in0=count, scalar=1.0,
                                                    in1=member[:, :, :], op0=ALU.add, op1=ALU.mult))
                step(nc.vector.tensor_scalar(slot_of[:, :, 0:EXP], slot_of[:, :, 0:EXP], -1.0, None, ALU.add))
                dve.wait_ge(route_mm, 4 * l + 4)
                step(nc.vector.tensor_reduce(most[:], ps[:, 5, 0:EXP], AX_X, ALU.max))

                def make_pick(i):
                    mine = slot_of[:, :, bass.ds(2 * i, 2)].unsqueeze(3).to_broadcast([P, NT, 2, CAP])
                    nc.vector.tensor_tensor(pick[:, :, :, :], iota.unsqueeze(1).unsqueeze(1).to_broadcast([P, NT, 2, CAP]),
                                            mine, ALU.is_equal).then_inc(pick_done, 1)

                def make_put(i):
                    dve.wait_ge(pick_done, (NPAIR + 1) * l + i + 1)
                    nc.vector.tensor_tensor(put[:, :, :, :], pick[:, :, :, :],
                                            gate[:, :, bass.ds(2 * i, 2)].unsqueeze(3).to_broadcast([P, NT, 2, CAP]),
                                            ALU.mult).then_inc(put_done, 1)

                make_pick(0)
                dve.wait_ge(route_act, 2 * l + 1)
                step(nc.vector.tensor_reduce(SUM[:, :, 0:1], GROUP_EXP, AX_X, ALU.add))
                dve.wait_ge(route_act, 2 * l + 2)
                step(nc.vector.tensor_scalar(DENOM[:, :, 1:5], DIFF[:, :, 1:5], 1.0, None, ALU.add))
                step(nc.vector.tensor_tensor(DENOM[:, :, 1:5], DENOM[:, :, 1:5], SUM[:, :, 0:1].to_broadcast([P, NT, 4]),
                                             ALU.mult))
                step(nc.vector.reciprocal(W1[:, :, 1:5], DENOM[:, :, 1:5]))
                step(nc.vector.tensor_tensor(W2[:, :, 1:5], W1[:, :, 1:5], DIFF[:, :, 1:5], ALU.mult))
                step(nc.vector.tensor_tensor(HOT1[:, :, 1:5, :], HOT1[:, :, 1:5, :], wide(W1[:, :, 1:5], NG), ALU.mult))
                step(nc.vector.tensor_tensor(HOT2[:, :, 1:5, :], HOT2[:, :, 1:5, :], wide(W2[:, :, 1:5], NG), ALU.mult))
                step(nc.vector.tensor_tensor(SCORE[:, :, 1:5, :], HOT1[:, :, 1:5, :], HOT2[:, :, 1:5, :], ALU.add))
                step(nc.vector.memset(gate[:, :, EXP:EXP + 2], 0.0))
                step(nc.vector.tensor_tensor(gate[:, :, 0:EXP].rearrange("p t (g e) -> p t g e", g=NG),
                                             wide(GROUP, NG), SCORE[:, :, 1:5, :], ALU.mult))
                make_put(0)

                def tokens_out(n, b):
                    dve.wait_ge(rs_gathered, n)
                    nc.vector.tensor_reduce(rs_slot[:, b:b + 1], ps[0:CAP, b, 508:511], AX_X,
                                            ALU.add).then_inc(rs_slot_done, 1)
                    for h in range(2):
                        dve.wait_ge(gathered, 2 * n + h - 1)
                        nc.vector.tensor_tensor(
                            xg[:, b, 8 * h:8 * h + 8, :], ps[:, 6 + h, :].rearrange("p (k s) -> p k s", k=8),
                            per_feature(ffn_gain[:, l, 8 * h:8 * h + 8], 8, CAP), ALU.mult).then_inc(xg_done, 1)

                G0 = (EXP + 1) * l
                tokens_out(G0 + 1, 0)
                step(nc.vector.scalar_tensor_tensor(out=over_gate[:, :, :], in0=slot_of[:, :, 0:EXP],
                                                    scalar=float(CAP), in1=gate[:, :, 0:EXP], op0=ALU.is_ge, op1=ALU.mult))
                nc.vector.tensor_copy(flags[0:1, l:l + 1], most[0:1, :]).then_inc(route_dve, 1)
                with dve.Fori(0, NPAIR) as i:
                    for b in range(2):
                        dve.wait_ge(silu_done, EXP * l + 2 * i + b + 1)
                        nc.vector.scalar_tensor_tensor(out=hid[:, :], in0=ps[CAP:2 * CAP, b, :],
                                                       scalar=rs_slot[:, b:b + 1], in1=silu_g[:, :],
                                                       op0=ALU.mult, op1=ALU.mult).then_inc(hid_done, 1)
                        tokens_out(G0 + 2 * i + 2 + b, 1 - b)
                        if b == 0:
                            dve.wait_ge(put_done, (NPAIR + 1) * l + i + 1)
                            make_pick(i + 1)
                        dve.wait_ge(slot_read, n0 + SLOTS * (2 * i + b + 1))
                        for h in range(2):
                            last = nc.vector.tensor_copy(
                                y_rows[CAP * b:CAP * b + CAP, (2 * h + 1) * BLK:(2 * h + 2) * BLK],
                                ps[CAP:2 * CAP, 2 + h, :])
                        last.then_inc(y_dve, 1)
                    dve.wait_ge(hid_turned, EXP * l + 2 * i + 2)
                    make_put(i + 1)
                    for m in range(8):
                        c, t = m // 2, m % 2
                        dve.wait_ge(mix_done, 8 * NPAIR * l + 8 * i + m + 1)
                        rb = resid[:, t, c * BLK:(c + 1) * BLK]
                        nc.vector.tensor_tensor(rb, rb, ps[:, 4 + t, :], ALU.add).then_inc(resid_added, 1)
                most_count = dve.value_load(flags[0:1, l:l + 1], min_val=0, max_val=SEQ)
                with dve.If(most_count > CAP):
                    dve.wait_ge(resid_added, add0 + 8 * NPAIR)
                    with dve.Fori(0, EXP) as e:
                        for t in range(NT):
                            dve.wait_ge(over[l]["silu"], NT * e + t + 1)
                            nc.vector.scalar_tensor_tensor(out=o_hid[:, :], in0=ps[:, 1, :], scalar=rs[:, t:t + 1],
                                                           in1=o_silu[:, :], op0=ALU.mult,
                                                           op1=ALU.mult).then_inc(over[l]["hid"], 1)
                            dve.wait_ge(over[l]["down"], NT * e + t + 1)
                            for c in range(NBLK):
                                rb = resid[:, t, c * BLK:(c + 1) * BLK]
                                nc.vector.scalar_tensor_tensor(
                                    out=rb, in0=ps[:, 4 + c, :], scalar=over_gate[:, t, bass.ds(e, 1)],
                                    in1=rb, op0=ALU.mult, op1=ALU.add).then_inc(over[l]["added"], 1)
                            dve.wait_ge(over[l]["added"], 4 * NT * e + 4 * t + 4)
                with dve.Else():
                    dve.nop()

            dve.wait_ge(vec_turned, 1)
            step(nc.vector.tensor_copy(vecs[:], ps[:, 4, 0:V_END]))
            step(nc.vector.tensor_scalar(vecs[:, V_END - 1:V_END], vecs[:, V_END - 1:V_END], HD ** -0.5, None, ALU.mult))
            nc.vector.tensor_copy(counters[:, 0, :], tri)
            nc.vector.tensor_copy(counters[:, 1, :], ones).then_inc(vec_done, 1)
            mean_square(0, True)
            dve.wait_ge(rs_done, 1)
            dve.wait_ge(band_loaded, 32)
            for t, (lo, hi) in enumerate(((0, 2), (2, 3))):
                nc.vector.tensor_scalar(band_s[:, :, lo:hi, :], band[:, :, lo:hi, :], rs[:, t:t + 1], None,
                                        ALU.mult).then_inc(band_done, 1)
            for u in range(UNIT_BUFS):
                unit(u, u // 2, u % 2)
            for b in range(8):
                dve.wait_ge(xs_hi, b + 1)
                for k in range(2):
                    last = nc.vector.scalar_tensor_tensor(
                        out=xs[:, 1, 2 * b + k, :], in0=ps[:, b, k * SEQ:(k + 1) * SEQ],
                        scalar=vecs[:, V_MIX + 2 * b + k:V_MIX + 2 * b + k + 1],
                        in1=xs[:, 0, 2 * b + k, :].bitcast(F32), op0=ALU.mult, op1=ALU.subtract)
                last.then_inc(xs_lo, 1)
            dve.wait_ge(vec_turned, 2)
            for l in range(2):
                nc.vector.tensor_copy(w_route[:, l], ps[:, l, 0:320].rearrange("p (e k) -> p k e", e=20)).then_inc(vec_done, 1)
            dve.wait_ge(smalls_loaded, SMALLS)
            for g in range(NG):
                for u in (2 * g + 3, 2 * g + 4):
                    if u < UNIT_ATT:
                        unit(u, u // 2, u % 2)
                for t in range(NT):
                    if t == 0:
                        dve.wait_ge(tile0_done, g + 1)
                    else:
                        dve.wait_ge(unit_used, 2 * g + 2)
                    if g:
                        dve.wait_ge(resid_added, 2 * g + t - 1)
                    nc.vector.tensor_tensor(mixed[:, t, :], ps[:, MIX_BANKS[g % 2] + t, :], scale_bc[:, g * BLK:(g + 1) * BLK],
                                            ALU.mult).then_inc(mixed_done, 1)
                    rb = resid[:, t, g * BLK:(g + 1) * BLK]
                    dve.wait_ge(mixed_done, 2 * g + t + 1)
                    nc.vector.tensor_tensor(rb, rb, mixed[:, t, :], ALU.add).then_inc(resid_added, 1)
                if g:
                    router_rows(0, g - 1)
                    tile0_parts(0, g - 1)
                    tile0_last(0, g - 1)
            moe(0)

            def att_unit(g, j, i=0):
                kind = j % 24 // 8
                unit(UNIT_ATT + 24 * g + j, START_ATT + SLOTS * g + j // 2, j % 2,
                     (V_KV, V_Q, V_KV)[kind] + 2 * (j % 8), i, 24)

            def head_squares(g, kind):
                for t in range(NT):
                    dve.wait_ge(proj_out, 6 * g + 2 * kind + t + 1)
                    dve.wait_ge(table_loaded, TABLES)
                    nc.vector.tensor_tensor(squares[:, :, :], raw[:, t], raw[:, t], ALU.mult).then_inc(sq_done, 1)
                    dve.wait_ge(sq_done, 8 * g + 4 * kind + 2 * t + 1)
                    nc.vector.tensor_reduce(head_ssq[:, t, :], squares[:, :, :], AX_X, ALU.add).then_inc(sq_done, 1)
                    dve.wait_ge(sq_done, 8 * g + 4 * kind + 2 * t + 2)
                nc.vector.tensor_scalar(head_ssq[:, :, :], head_ssq[:, :, :], 1.0 / HD, EPS,
                                        ALU.mult, ALU.add).then_inc(head_sums, 1)

            def head_scale(g, kind):
                dve.wait_ge(head_rs_done, 2 * g + kind + 1)
                nc.vector.tensor_tensor(raw[:, :, :, :], raw[:, :, :, :],
                                        head_rs[:, :, :].unsqueeze(3).to_broadcast([P, NT, HG, HD]),
                                        ALU.mult).then_inc(head_normed, 1)

            def softplus(g):
                dve.wait_ge(ln_done, g + 1)
                nc.vector.scalar_tensor_tensor(out=soft[:, :, :], in0=ps[:, 0:HG, 0:ZC], scalar=0.0, in1=lnk[:, :, :],
                                               op0=ALU.max, op1=ALU.add).then_inc(soft_done, 1)

            def masked(g):
                dve.wait_ge(soft_done, 2 * g + 1)
                nc.vector.scalar_tensor_tensor(out=soft[:, :, :],
                                               in0=const[:, C_ADD:C_ADD + ZC].unsqueeze(1).to_broadcast([P, HG, ZC]),
                                               scalar=0.0, in1=soft[:, :, :], op0=ALU.is_ge,
                                               op1=ALU.mult).then_inc(soft_done, 1)

            def shift(g):
                dve.wait_ge(cum_done, g + 1)
                nc.vector.tensor_tensor(lnk[:, :, :], ps[:, 0:HG, 0:ZC],
                                        const[:, C_ADD:C_ADD + ZC].unsqueeze(1).to_broadcast([P, HG, ZC]),
                                        ALU.add).then_inc(shift_done, 1)

            def outputs(g):
                for b in range(2):
                    dve.wait_ge(o_done, 2 * g + b + 1)
                    nc.vector.tensor_copy(oT[:, bass.ds(HG * g + 2 * b, 2), :],
                                          ps[:, 6 + b, :].rearrange("p (h q) -> p h q", h=2)).then_inc(o_out, 1)

            def group(g, i, first=False, last=False):
                G = g + i

                def units(*js):
                    for j in js:
                        att_unit(g, j, i)

                units(2, 3)
                if not first:
                    softplus(G - 1)
                units(4, 5)
                if first:
                    mean_square(2, True)
                else:
                    masked(G - 1)
                units(6, 7, 8, 9)
                head_squares(G, 0)
                units(10)
                head_scale(G, 0)
                units(11)
                if not first:
                    shift(G - 1)
                units(12, 13, 14, 15, 16, 17)
                if not first:
                    outputs(G - 1)
                head_squares(G, 1)
                units(18)
                head_scale(G, 1)
                units(19, 20, 21, 22, 23)
                if last:
                    o_unit(0)
                    o_unit(1)
                else:
                    units(24, 25)

            def o_unit(j):
                unit(UNIT_O + j, START_O + j // 2, j % 2)

            att_unit(0, 0)
            for b in range(8):
                dve.wait_ge(xs_hi, 8 + b + 1)
                nc.vector.tensor_tensor(xs[:, 1, 2 * b:2 * b + 2, :],
                                        ps[:, X_BANKS[b], :].rearrange("p (k t) -> p k t", k=2),
                                        xs[:, 0, 2 * b:2 * b + 2, :].bitcast(F32), ALU.subtract).then_inc(xs_lo, 1)
                if b == 3:
                    att_unit(0, 1)
            group(0, 0, first=True)
            with dve.Fori(1, NG - 1) as g:
                group(1, g - 1)
            group(NG - 1, 0, last=True)

            def o_chunk(c):
                dve.wait_ge(xs_hi, 16 + c + 1)
                if c < 3:
                    nc.vector.tensor_tensor(xs[:, 1, 4 * c:4 * c + 4, :], oT[:, 4 * c:4 * c + 4, :],
                                            xs[:, 0, 4 * c:4 * c + 4, :].bitcast(F32), ALU.subtract).then_inc(xs_lo, 1)
                else:
                    nc.vector.tensor_tensor(xs[:, 1, 12:16, :].rearrange("p (b h) t -> p b (h t)", b=2), ps[:, 6:8, :],
                                            xs[:, 0, 12:16, :].rearrange("p (b h) t -> p b (h t)", b=2).bitcast(F32),
                                            ALU.subtract).then_inc(xs_lo, 1)

            o_chunk(0)
            o_chunk(1)
            o_unit(2)
            o_unit(3)
            softplus(NG - 1)
            masked(NG - 1)
            o_chunk(2)
            o_unit(4)
            shift(NG - 1)
            o_unit(5)
            o_unit(6)
            o_unit(7)
            o_chunk(3)
            for c in range(NBLK):
                if c + 1 < NBLK:
                    o_unit(8 * c + 8)
                    o_unit(8 * c + 9)
                for t in range(NT):
                    if t == 0:
                        dve.wait_ge(tile0_done, TILE0_O + c + 1)
                    else:
                        dve.wait_ge(unit_used, UNIT_O + 8 * c + 8)
                    rb = resid[:, t, c * BLK:(c + 1) * BLK]
                    nc.vector.tensor_tensor(rb, rb, ps[:, 4 + t, :], ALU.add).then_inc(resid_added, 1)
                if c + 1 < NBLK:
                    o_unit(8 * c + 10)
                    tile0_parts(1, c)
                    o_unit(8 * c + 11)
                    o_unit(8 * c + 12)
                    tile0_last(1, c)
                    o_unit(8 * c + 13)
                    router_rows(1, c)
                    o_unit(8 * c + 14)
                    o_unit(8 * c + 15)
            moe(1)
            nc.vector.tensor_copy(most[:], ssq[:, 0:1]).then_inc(final_ready, 1)

        @block.tensor
        def _(pe):
            mm = nc.tensor.matmul

            def unit(u, tiles, first, last_unit, free=None, i=0, per_u=0, bank=4):
                pe.wait_ge(unit_lo, u + 1 + i * per_u)
                b = u % UNIT_BUFS
                for t in range(NT):
                    if first and free is not None:
                        free(t)
                    for j, k in enumerate(tiles):
                        cols = slice(t * P, (t + 1) * P)
                        for n, (px, pw) in enumerate(((0, 0), (0, 1), (1, 0))):
                            last = mm(ps[:, bank + t, :], xs[:, px, k, cols], ws[:, b, pw, j, :],
                                      start=(first and j == 0 and n == 0), stop=(last_unit and j == 1 and n == 2))
                    if last_unit and t == 0:
                        last.then_inc(tile0_done, 1)
                last.then_inc(unit_used, 1)

            def turn_block(l, c):
                pe.wait_ge(resid_added, (0, ADD_O)[l] + 2 * c + 2)
                if l == 0:
                    if c == 0:
                        pe.wait_ge(vec_done, 3)
                    else:
                        pe.wait_ge(turned_out, 2 * (c - 1) + 2)
                elif c > 1:
                    pe.wait_ge(turned_out, 8 + 2 * (c - 2) + 2)
                for j in range(4):
                    k = 4 * c + j
                    for t in range(NT):
                        col = (j % 2) * SEQ + t * P
                        last = nc.tensor.transpose(ps[:, turn_bank(l, c) + j // 2, col:col + P],
                                                   resid[:, t, k * P:(k + 1) * P], ident)
                    if j % 2:
                        last.then_inc(turned, 1)

            def route_block(l, c):
                for j in range(4):
                    if j % 2 == 0:
                        pe.wait_ge(turned_out, 8 * l + 2 * c + j // 2 + 1)
                    k = 4 * c + j
                    last = mm(ps[0:20, 6, 0:SEQ], w_route[:, l, k, :], xr[:, k, :], start=(k == 0), stop=(k == KD - 1))
                if c == NBLK - 1:
                    last.then_inc(route_mm, 1)

            def moe(l):
                n0 = START_MOE[l]
                add0 = ADD_BASE[l]
                turn_block(l, NBLK - 1)
                route_block(l, NBLK - 1)
                pe.wait_ge(hidT_done, (EXP + 1) * l + 1)
                for t in range(NT):
                    last = nc.tensor.transpose(ps[:, 7, 32 * t:32 * t + 20], logitsT[:, t * P:(t + 1) * P],
                                               const[0:20, C_ID:C_ID + 20])
                last.then_inc(route_mm, 1)
                pe.wait_ge(member_done, l + 1)
                before, every = counters[:, 0, :], counters[:, 1, :]
                mm(ps[:, 7, 64:80], before, member[:, 0, :], start=True, stop=True)
                mm(ps[:, 7, 80:96], every, member[:, 0, :], start=True, stop=False)
                mm(ps[:, 7, 80:96], before, member[:, 1, :], start=False, stop=True).then_inc(route_mm, 1)
                mm(ps[:, 5, 0:EXP], every, member[:, 0, :], start=True, stop=False)
                mm(ps[:, 5, 0:EXP], every, member[:, 1, :], start=False, stop=True).then_inc(route_mm, 1)

                def gather(e):
                    for t in range(NT):
                        last = mm(ps[0:CAP, e, 508:511], pick[:, t, e, :], rs_parts[:, t, :], start=(t == 0),
                                  stop=(t == NT - 1))
                    last.then_inc(rs_gathered, 1)
                    for k in range(KD):
                        for s in range(3):
                            for t in range(NT):
                                last = mm(ps[:, 6 + k // 8, (k % 8) * CAP:(k % 8 + 1) * CAP],
                                          parts[:, s, t, k * P:(k + 1) * P], pick[:, t, e, :],
                                          start=(s == 0 and t == 0), stop=(s == 2 and t == NT - 1))
                        if k % 8 == 7:
                            last.then_inc(gathered, 1)

                PICKS = (NPAIR + 1) * l
                XG = (EXP + 1) * l
                for t in range(NT):
                    pe.wait_ge(lo_done[t], NBLK * (l + 1))
                pe.wait_ge(rs_parts_done, l + 1)
                pe.wait_ge(pick_done, PICKS + 1)
                gather(0)
                with pe.Fori(0, NPAIR) as i:
                    for b in range(2):
                        pe.wait_ge(xg_done, 2 * (XG + 2 * i + b) + 1)
                        pe.wait_ge(hidT_done, (EXP + 1) * l + 2 * i + b + 1)
                        for q in range(4):
                            n = n0 + SLOTS * b + 2 * q
                            slot_in(pe, n, i, PAIR_SLOTS)
                            slot_in(pe, n + 1, i, PAIR_SLOTS)
                            if q == 2:
                                pe.wait_ge(xg_done, 2 * (XG + 2 * i + b) + 2)
                            for j in range(4):
                                k = 4 * q + j
                                for h in range(2):
                                    last = mm(ps[CAP * h:CAP * h + CAP, b, :], xg[:, b, k, :], four(n + h)[:, j, :],
                                              start=(k == 0), stop=(k == KD - 1))
                            last.then_inc(slot_read, 2)
                        if b == 1:
                            pe.wait_ge(pick_done, PICKS + i + 2)
                        gather(1 - b)
                        pe.wait_ge(rs_slot_done, XG + 2 * i + b + 2)
                        pe.wait_ge(put_done, PICKS + i + 1)
                        pe.wait_ge(hid_done, EXP * l + 2 * i + b + 1)
                        nc.tensor.transpose(ps[:, 1 - b, SEQ:SEQ + P], put[:, b].rearrange("p e s -> p (e s)"), ident)
                        for k in range(KF):
                            last = nc.tensor.transpose(ps[:, 1 - b, k * CAP:(k + 1) * CAP], hid[:, k * P:(k + 1) * P],
                                                       const[0:CAP, C_ID:C_ID + CAP])
                        last.then_inc(hid_turned, 1)
                        pe.wait_ge(hidT_done, (EXP + 1) * l + 2 * i + b + 2)
                        if b == 1:
                            pe.wait_ge(y_act, EXP * l + 2 * i + 1)
                            pe.wait_ge(y_dve, EXP * l + 2 * i + 1)
                        for k in range(KF):
                            n = n0 + SLOTS * b + 8 + k
                            slot_in(pe, n, i, PAIR_SLOTS)
                            for c in range(NBLK):
                                h = c % 2
                                last = mm(ps[CAP * h:CAP * h + CAP, 2 + c // 2, :], hidT[:, b, k, :],
                                          slot(n)[:, c * BLK:(c + 1) * BLK], start=(k == 0), stop=(k == KF - 1))
                            last.then_inc(slot_read, 1)
                    pe.wait_ge(y_act, EXP * l + 2 * i + 2)
                    pe.wait_ge(y_dve, EXP * l + 2 * i + 2)
                    for m in range(8):
                        c, t = m // 2, m % 2
                        pe.wait_ge(resid_added, add0 + 8 * i + m - 1)
                        mm(ps[:, 4 + t, :], putT[:, t * P:(t + 1) * P], y_rows[:, c * BLK:(c + 1) * BLK],
                           start=True, stop=True).then_inc(mix_done, 1)
                pe.wait_ge(route_dve, 3 * (l + 1))
                count = pe.value_load(flags[0:1, l:l + 1], min_val=0, max_val=SEQ)
                with pe.If(count > CAP):
                    o = over[l]
                    pe.wait_ge(resid_added, add0 + 8 * NPAIR)
                    pe.wait_ge(xg_done, 2 * (EXP + 1) * (l + 1))
                    with pe.Fori(0, EXP) as e:
                        pe.wait_ge(o["loaded"], 16 * SLOTS * e + 16 * SLOTS)
                        for t in range(NT):
                            for h in range(2):
                                for k in range(KD):
                                    last = mm(ps[:, h, :], xr[:, k, t * P:(t + 1) * P], four(2 * (k // 4) + h)[:, k % 4, :],
                                              start=(k == 0), stop=(k == KD - 1))
                            last.then_inc(o["gu"], 1)
                            pe.wait_ge(o["hid"], NT * e + t + 1)
                            for k in range(KF):
                                last = nc.tensor.transpose(ps[:, 2, k * P:(k + 1) * P], o_hid[:, k * P:(k + 1) * P], ident)
                            last.then_inc(o["turned"], 1)
                            pe.wait_ge(o["hidT"], NT * e + t + 1)
                            for c in range(NBLK):
                                for k in range(KF):
                                    last = mm(ps[:, 4 + c, :], o_hidT[:, k, :], slot(8 + k)[:, c * BLK:(c + 1) * BLK],
                                              start=(k == 0), stop=(k == KF - 1))
                            last.then_inc(o["down"], 1)
                            pe.wait_ge(o["added"], 4 * NT * e + 4 * t + 4)
                with pe.Else():
                    pe.nop()

            pe.wait_ge(table_loaded, TABLES)
            pe.wait_ge(band_loaded, 32)
            nc.tensor.transpose(ps[:, 4, 0:V_END], vec_rows[:, :], const[0:V_END, C_ID:C_ID + V_END]).then_inc(vec_turned, 1)
            for t in range(NT):
                pe.wait_ge(x_loaded[t], 16)
            pe.wait_ge(band_done, 2)
            for b in range(8):
                g = b // 2
                for k in (2 * b, 2 * b + 1):
                    c = (k % 2) * SEQ
                    mm(ps[:, b, c:c + SEQ], resid[:, 0, k * P:(k + 1) * P], band_s[:, g, 0:2, :], start=True, stop=False)
                    last = mm(ps[:, b, c + P:c + SEQ], resid[:, 1, k * P:(k + 1) * P], band_s[:, g, 2, :],
                              start=False, stop=True)
                last.then_inc(turned, 1)
            pe.wait_ge(route_loaded, 64)
            pe.wait_ge(xs_lo, 2)
            for l in range(2):
                for g in range(5):
                    rows = route_rows[:, l, g].rearrange("k (p e) -> k e p", e=4)
                    for e in range(4):
                        c = KD * (4 * g + e)
                        last = nc.tensor.transpose(ps[:, l, c:c + KD], rows[:, e, :], const[0:KD, C_ID:C_ID + KD])
            last.then_inc(vec_turned, 1)
            pe.wait_ge(xs_lo, 8)
            for g in range(NG):
                def read(t, g=g):
                    if g > 1:
                        pe.wait_ge(mixed_done, 2 * (g - 2) + t + 1)

                unit(2 * g, (4 * g, 4 * g + 1), True, False, read, bank=MIX_BANKS[g % 2])
                unit(2 * g + 1, (4 * g + 2, 4 * g + 3), False, True, bank=MIX_BANKS[g % 2])
                if g > 0:
                    turn_block(0, g - 1)
                if g > 1:
                    route_block(0, g - 2)
            route_block(0, NBLK - 2)
            moe(0)

            pe.wait_ge(resid_added, ADD_O)
            for b in range(8):
                if b >= 6:
                    pe.wait_ge(xs_lo, 8 + b - 6 + 1)
                for k in (2 * b, 2 * b + 1):
                    for t in range(NT):
                        c = (k % 2) * SEQ + t * P
                        last = nc.tensor.transpose(ps[:, X_BANKS[b], c:c + P], resid[:, t, k * P:(k + 1) * P], ident)
                last.then_inc(turned, 1)

            def att_unit(g, j, i=0, first=False):
                kind = j // 8

                def evacuated(t):
                    if not first:
                        pe.wait_ge(proj_out, 6 * (g + i) + 2 * kind + t - 1)

                if first:
                    pe.wait_ge(xs_lo, 8 + j + 1)
                unit(UNIT_ATT + 24 * g + j, (2 * (j % 8), 2 * (j % 8) + 1), j % 8 == 0, j % 8 == 7, evacuated, i, 24)

            def turn_heads(g, kind):
                pe.wait_ge(head_normed, 2 * g + kind + 1)
                for t in range(NT):
                    for h in range(HG):
                        last = nc.tensor.transpose(ps[:, 6 + t, h * P:(h + 1) * P], raw[:, t, h, :], ident)
                    last.then_inc(heads_turned, 1)

            def scores(g):
                pe.wait_ge(heads_out, 4 * g + 4)
                for h in range(HG):
                    mm(ps[:, h, 0:SEQ], kT[:, h, 0:P], qT[:, h, :], start=True, stop=False, skip_group_check=True)
                    last = mm(ps[:, h, SEQ:ZC], kT[:, h, P:SEQ], qT[:, h, P:SEQ], start=False, stop=True,
                              skip_group_check=True)
                last.then_inc(z_done, 1)

            def suffix_sums(g):
                pe.wait_ge(soft_done, 2 * g + 2)
                for h in range(HG):
                    mm(ps[:, h, 0:ZC], const[:, C_NSUF:C_NSUF + P], soft[:, h, :], start=False, stop=False,
                       skip_group_check=True)
                    last = mm(ps[:, h, P:SEQ], const[:, C_NONE:C_NONE + P], soft[:, h, SEQ:ZC], start=False, stop=True,
                              skip_group_check=True)
                last.then_inc(cum_done, 1)

            def mix_values(g):
                pe.wait_ge(att_done, g + 1)
                for h in range(HG):
                    c = (h % 2) * SEQ
                    mm(ps[:, 6 + h // 2, c:c + SEQ], vrow[:, 0, h * P:(h + 1) * P], att[:, h, 0:SEQ], start=True,
                       stop=False)
                    last = mm(ps[:, 6 + h // 2, c + P:c + SEQ], vrow[:, 1, h * P:(h + 1) * P], att[:, h, SEQ:ZC],
                              start=False, stop=True)
                    if h % 2:
                        last.then_inc(o_done, 1)

            def group(g, i, first):
                G = g + i
                if not first:
                    scores(G - 1)
                for j in range(8):
                    att_unit(g, j, i, first)
                if not first:
                    suffix_sums(G - 1)
                for j in range(8, 12):
                    att_unit(g, j, i)
                turn_heads(G, 0)
                for j in range(12, 16):
                    att_unit(g, j, i)
                pe.wait_ge(heads_out, 4 * G + 2)
                if not first:
                    mix_values(G - 1)
                for j in range(16, 20):
                    att_unit(g, j, i)
                if not first:
                    pe.wait_ge(o_out, 2 * G)
                turn_heads(G, 1)
                for j in range(20, 24):
                    att_unit(g, j, i)

            group(0, 0, True)
            with pe.Fori(1, NG - 1) as g:
                group(1, g - 1, False)
            group(NG - 1, 0, False)

            def o_unit(j):
                def free(t):
                    if j == 0:
                        pe.wait_ge(proj_out, 6 * NG - 1 + t)
                    else:
                        pe.wait_ge(resid_added, ADD_O + 2 * (j // 8 - 1) + t + 1)

                if j < 8 and j % 2 == 0:
                    pe.wait_ge(xs_lo, 16 + j // 2 + 1)
                unit(UNIT_O + j, (2 * (j % 8), 2 * (j % 8) + 1), j % 8 == 0, j % 8 == 7, free)

            scores(NG - 1)
            for j in range(4):
                o_unit(j)
            suffix_sums(NG - 1)
            o_unit(4)
            o_unit(5)
            pe.wait_ge(heads_out, 4 * NG)
            pe.wait_ge(proj_out, 6 * NG)
            mix_values(NG - 1)
            o_unit(6)
            o_unit(7)
            for c in range(1, NBLK):
                for j in range(4):
                    o_unit(8 * c + j)
                if c == 1:
                    pe.wait_ge(shift_done, NG)
                turn_block(1, c - 1)
                for j in range(4, 8):
                    o_unit(8 * c + j)
                route_block(1, c - 1)
            moe(1)


_INS = ["x", "norm_mix", "norm_ffn", "pool_w", "pool_scale", "kv_norm", "w_kv", "k_norm", "w_q", "q_norm", "w_o",
        "moe_w_grp", "moe_b_grp", "moe_w_rt", "moe_b_rt", "moe_w_gate", "moe_w_up", "moe_w_down"]


def kernel(**inputs):
    import concourse.bacc as bacc
    from concourse.bass_utils import run_bass_kernel_spmd

    nc = bacc.Bacc("TRN2", target_bir_lowering=False, num_devices=1, dynamic_dma_scratch_size=1024)
    arrays, args = {}, []
    tables = {"constant_table": constant_table(), "band_table": band_table()}
    for name in [*_INS, *tables]:
        a = tables[name] if name in tables else np.ascontiguousarray(inputs[name])
        arrays[f"in_{name}"] = a
        args.append(nc.dram_tensor(f"in_{name}", a.shape, mybir.dt.from_np(a.dtype), kind="ExternalInput").ap())
    out = nc.dram_tensor("out_rows", (1, SEQ, D), F32, kind="ExternalOutput").ap()
    build(nc, *args, out)
    r = run_bass_kernel_spmd(nc, [arrays], core_ids=[0])
    return r.results[0]["out_rows"]
```

```python
from contextlib import ExitStack

import numpy as np

import concourse.bass as bass
from concourse import mybir

F32 = mybir.dt.float32
BF16 = mybir.dt.bfloat16
I32 = mybir.dt.int32
ALU = mybir.AluOpType
ACT = mybir.ActivationFunctionType
AX_X = mybir.AxisListType.X

P = 128
SEQ = 256
D = 2048
NT = SEQ // P
KD = D // P
NG = 4
GD = D // NG
WINDOWS = (2, 4, 8, 16)
HD = 128
NH = D // HD
HG = NH // NG
EXP = 16
EPG = EXP // NG
FF = 512
KF = FF // P
CAP = 64
NPAIR = EXP // 2
NBLK = 4
BLK = D // NBLK
SLOTS = 12
PAIR_SLOTS = 2 * SLOTS
EXTRA = 5
MOE_SLOTS = NPAIR * PAIR_SLOTS - EXTRA
UNIT_BUFS = 3
EPS = 1e-6
BIG = 1e30
F32R = mybir.dt.float32r
ZC = SEQ + P

C_ID, C_TRI, C_ONE, C_NSUF, C_NONE, C_ADD = 0, 128, 256, 384, 512, 640
C_IOTA = C_ADD + ZC
C_RANK = C_IOTA + CAP
C_STACK = C_RANK + 4
C_END = C_STACK + 20
BANDS = NG * 3 * P
V_MIX, V_KV, V_Q, V_FFN, V_HEAD, V_END = 0, 16, 32, 48, 80, 82
V_SCALE, V_ROWS = 82, 98


def constant_table():
    c = np.zeros((P, C_END), np.float32)
    row, col = np.arange(P)[:, None], np.arange(P)[None, :]
    c[:, C_ID:C_ID + P] = row == col
    c[:, C_TRI:C_TRI + P] = row < col
    c[:, C_ONE:C_ONE + P] = 1.0
    c[:, C_NSUF:C_NSUF + P] = -(row >= col).astype(np.float32)
    c[:, C_NONE:C_NONE + P] = -1.0
    seen = (row < col).astype(np.float32)
    c[:, C_ADD:C_ADD + ZC] = (np.concatenate([seen, np.ones((P, P), np.float32), seen], 1) - 1.0) * BIG
    c[:, C_IOTA:C_IOTA + CAP] = np.arange(1, CAP + 1)
    c[:, C_RANK:C_RANK + 4] = [4, 3, 2, 1]
    c[:, C_STACK:C_STACK + 20] = row % 32 == np.arange(20)
    return c


def band_table():
    src, dst = np.arange(SEQ)[:, None], np.arange(SEQ)[None, :]
    out = np.zeros((P, NG, 3, P), np.float32)
    for g, w in enumerate(WINDOWS):
        m = ((src <= dst) & (src > dst - w)) / np.minimum(dst + 1, w) - (src == dst)
        out[:, g, 0], out[:, g, 1], out[:, g, 2] = m[:P, :P], m[:P, P:], m[P:, P:]
    return out.reshape(P, BANDS)


def build(nc, x, norm_mix, norm_ffn, pool_w, pool_scale, kv_norm, w_kv, k_norm, w_q, q_norm, w_o,
          w_grp, b_grp, w_rt, b_rt, w_gate, w_up, w_down, table, bands, out):
    with ExitStack() as ctx:
        def sb(name, shape, dt=F32):
            return ctx.enter_context(nc.sbuf_tensor(name, shape, dt))

        def sem(name):
            return ctx.enter_context(nc.semaphore(name))

        ring = sb("ring", [P, SLOTS, 2048])
        resid = sb("resid", [P, NT, D])
        const = sb("const", [P, C_END])
        vecs = sb("vecs", [P, V_END])
        ffn_gain = sb("ffn_gain", [P, 2, KD])
        bias = sb("bias", [P, 2, 20])
        w_route = sb("w_route", [P, 2 * KD * 20 + 12])
        ssq_part = sb("ssq_part", [P, NT, NBLK])
        ssq = sb("ssq", [P, NT])
        rs = sb("rs", [P, NT])
        rs_rest = sb("rs_rest", [P, NT])
        rs_parts = sb("rs_parts", [P, NT, 3], BF16)
        rs_slot = sb("rs_slot", [CAP, 2])
        half = sb("half", [P, NT * HG])
        head_ssq = sb("head_ssq", [P, NT, HG])
        head_rs = sb("head_rs", [P, NT, HG])
        flags = sb("flags", [1, 2], I32)
        most = sb("most", [P, 1])
        counters = sb("counters", [P, 2, P], BF16)
        ident_b = sb("ident_b", [P, P], BF16)
        KB = 1024
        ARENA = -(-nc.sbuf_base // 32) * 32
        sb("arena", [P, 102 * KB // 4])

        def at(offset, name, shape, dt=F32):
            return nc.alloc_sbuf_tensor_at(name, shape, dt, offset=ARENA + offset)


        xs = at(0, "xs", [P, 2, KD, SEQ], F32R)
        ws = at(32 * KB, "ws", [P, UNIT_BUFS, 2, 2, BLK], F32R)
        junk_rows = at(20 * KB, "junk_rows", [P, D])
        band = at(56 * KB, "band", [P, NG, 3, P])
        band_s = at(62 * KB, "band_s", [P, NG, 3, P])
        vec_rows = at(101 * KB, "vec_rows", [V_ROWS, P])
        route_rows = at(74 * KB, "route_rows", [KD, 2, 5, 4 * P])
        mixed = at(68 * KB, "mixed", [P, NT, BLK])
        xr = at(56 * KB, "xr", [P, KD, SEQ])
        parts = at(72 * KB, "parts", [P, 3, NT, D], BF16)
        rest = at(96 * KB, "rest", [P, NT, BLK])
        junk = at(100 * KB, "junk", [P, BLK], BF16)
        oT = at(56 * KB, "oT", [P, NH, SEQ])
        kT = at(72 * KB, "kT", [P, HG, SEQ])
        qT = at(76 * KB, "qT", [P, HG, SEQ])
        vrow = at(80 * KB, "vrow", [P, NT, HG * HD])
        raw = at(84 * KB, "raw", [P, NT, HG, HD])
        lnk = at(88 * KB, "lnk", [P, HG, ZC])
        soft = at(94 * KB, "soft", [P, HG, ZC])
        att = soft
        squares = at(100 * KB, "squares", [P, HG, HD])
        junk_att = at(88 * KB, "junk_att", [P, D])
        xg = at(0, "xg", [P, 2, KD, CAP])
        y_rows = at(8 * KB, "y_rows", [P, D])
        silu_g = at(16 * KB, "silu_g", [CAP, FF])
        hid = at(18 * KB, "hid", [CAP, FF])
        hidT = at(20 * KB, "hidT", [P, 2, KF, CAP])
        pick = at(22 * KB, "pick", [P, NT, 2, CAP], BF16)
        put = at(23 * KB, "put", [P, NT, 2, CAP])
        putT = at(24 * KB, "putT", [P, SEQ])
        logitsT = at(25 * KB, "logitsT", [P, SEQ])
        lg = at(26 * KB, "lg", [P, NT, 20])
        member = at(27 * KB + 512, "member", [P, NT, EXP], BF16)
        gate = at(27 * KB + 768, "gate", [P, NT, EXP + 2])
        slot_of = at(28 * KB, "slot_of", [P, NT, EXP + 2])
        over_gate = at(28 * KB + 256, "over_gate", [P, NT, EXP])
        route5 = at(28 * KB + 512, "route5", [P, 5, NT, 5, 4])
        route4 = at(29 * KB + 512, "route4", [P, 3, NT, 4])
        route1 = at(30 * KB, "route1", [P, 8, NT, 5])
        extra = at(32 * KB, "extra", [P, EXTRA, 2048])
        o_silu = at(32 * KB, "o_silu", [P, FF])
        o_hid = at(34 * KB, "o_hid", [P, FF])
        o_hidT = at(36 * KB, "o_hidT", [P, KF, P])

        ident = const[:, C_ID:C_ID + P]
        ones = const[:, C_ONE:C_ONE + P]
        tri = const[:, C_TRI:C_TRI + P]
        iota = const[:, C_IOTA:C_IOTA + CAP]
        rank = const[:, C_RANK:C_RANK + 4]

        ps = ctx.enter_context(nc.psum_tensor("ps", [P, 8, 512], F32))

        slot_loaded = [sem(f"slot_loaded{j}") for j in range(SLOTS)]
        extra_loaded = [sem(f"extra_loaded{j}") for j in range(EXTRA)]
        slot_read = sem("slot_read")
        x_loaded = [sem(f"x_loaded{t}") for t in range(NT)]
        table_loaded = sem("table_loaded")
        band_loaded = sem("band_loaded")
        route_loaded = sem("route_loaded")
        smalls_loaded = sem("smalls_loaded")
        ssq_done = sem("ssq_done")
        ms_done = sem("ms_done")
        pool_step = sem("pool_step")
        rs_done = sem("rs_done")
        band_done = sem("band_done")
        vec_turned = sem("vec_turned")
        vec_done = sem("vec_done")
        turned = sem("turned")
        turned_out = sem("turned_out")
        xs_hi = sem("xs_hi")
        xs_lo = sem("xs_lo")
        unit_hi = sem("unit_hi")
        unit_lo = sem("unit_lo")
        unit_used = sem("unit_used")
        tile0_done = sem("tile0_done")
        scale_spread = sem("scale_spread")
        scale_out = sem("scale_out")
        mixed_done = sem("mixed_done")
        mix_done = sem("mix_done")
        resid_added = sem("resid_added")
        dve_step = sem("dve_step")
        hi_done = sem("hi_done")
        rest_done = [sem(f"rest_done{t}") for t in range(NT)]
        mid_done = [sem(f"mid_done{t}") for t in range(NT)]
        lo_done = [sem(f"lo_done{t}") for t in range(NT)]
        route_mm = sem("route_mm")
        route_act = sem("route_act")
        route_dve = sem("route_dve")
        member_done = sem("member_done")
        rs_parts_done = sem("rs_parts_done")
        pick_done = sem("pick_done")
        put_done = sem("put_done")
        rs_gathered = sem("rs_gathered")
        rs_slot_done = sem("rs_slot_done")
        gathered = sem("gathered")
        xg_done = sem("xg_done")
        silu_done = sem("silu_done")
        hid_done = sem("hid_done")
        hid_turned = sem("hid_turned")
        hidT_done = sem("hidT_done")
        y_act = sem("y_act")
        y_dve = sem("y_dve")
        over = [{n: sem(f"over{l}_{n}") for n in
                 ("rows", "xr", "loaded", "gu", "silu", "hid", "turned", "hidT", "down", "added")}
                for l in range(2)]
        proj_out = sem("proj_out")
        sq_done = sem("sq_done")
        head_sums = sem("head_sums")
        head_rs_done = sem("head_rs_done")
        head_normed = sem("head_normed")
        heads_turned = sem("heads_turned")
        heads_out = sem("heads_out")
        z_done = sem("z_done")
        act_step = sem("act_step")
        ln_done = sem("ln_done")
        soft_done = sem("soft_done")
        cum_done = sem("cum_done")
        shift_done = sem("shift_done")
        att_done = sem("att_done")
        o_done = sem("o_done")
        o_out = sem("o_out")
        stored = sem("stored")

        START_MOE = [NG, NG + MOE_SLOTS + NG * SLOTS + NBLK * 4]
        START_ATT = START_MOE[0] + MOE_SLOTS
        START_O = START_ATT + NG * SLOTS
        UNIT_ATT = 2 * NG
        UNIT_O = UNIT_ATT + 2 * NG * SLOTS
        ADD_BASE = [8, 16 + 8 * NPAIR]
        ADD_O = 8 + 8 * NPAIR
        TURN_ROUTE = [8, 24]
        TURN_ATT = 16
        TILE0_ATT = NG
        TILE0_O = NG + 3 * NG
        SSQ = [2, 2 + 8, 2 + 8 + 2, 2 + 8 + 2 + 8]
        TABLES = 16 * 8
        SMALLS = 16 * 6

        def slot(n):
            return ring[:, n % SLOTS, :]

        def turn_bank(l, c):
            return 2 * (c % 2) if l else 0

        def four(n):
            return slot(n).rearrange("p (k c) -> p k c", k=4)

        def expert_loads_read(l, n):
            m = n - START_MOE[l]
            return NPAIR * PAIR_SLOTS * l + m + 1 + (EXTRA if m >= SLOTS else 0)

        def when_read(n):
            if n < START_MOE[0]:
                return unit_lo, 2 * n + 2
            if n < START_ATT:
                return slot_read, expert_loads_read(0, n)
            if n < START_O:
                return unit_lo, UNIT_ATT + 2 * (n - START_ATT) + 2
            if n < START_MOE[1]:
                return unit_lo, UNIT_O + 2 * (n - START_O) + 2
            return slot_read, expert_loads_read(1, n)

        def slot_in(eng, n, i=0, per=0):
            eng.wait_ge(slot_loaded[n % SLOTS], 16 * (n // SLOTS + 1) + i * (16 * per // SLOTS))

        w_gate_v = w_gate.rearrange("l e (p k) f -> l e p k f", k=KD)
        w_up_v = w_up.rearrange("l e (p k) f -> l e p k f", k=KD)
        w_down_v = w_down.rearrange("l e (k p) d -> l e p k d", p=P)
        w_kv_v = w_kv.rearrange("(k p) (b c) -> b p k c", p=P, c=BLK)
        w_q_v = w_q[0].rearrange("(k p) (b c) -> b p k c", p=P, c=BLK)
        w_o_v = w_o[0].rearrange("(k p) (b c) -> b p k c", p=P, c=BLK)
        pool_w_v = pool_w[0].rearrange("g (k p) c -> g p k c", p=P)

        WARM_START, WARM_ROUTE, WARM_PICK = 9, 24, 10
        WS_EXTRA = 3
        MIX_BANKS = (4, 2)
        X_BANKS = (0, 1, 2, 3, 6, 7, 0, 1)

        def in_tiles(s, t, c):
            return parts[:, s, t, :].rearrange("q (k p) -> q p k", k=KD)[:, c * (BLK // KD):(c + 1) * (BLK // KD), :]

        block = ctx.enter_context(nc.Block())

        @block.sync
        def _(sp):
            def load(n, src, dst=None, i=0, per=0):
                if n >= SLOTS:
                    before, value = when_read(n - SLOTS)
                    sp.wait_ge(before, value + i * per * (2 if before is unit_lo else 1))
                sp.dma_start(four(n) if dst is None else dst, src).then_inc(slot_loaded[n % SLOTS], 16)

            def expert_load(l, e, m):
                if m < 8:
                    return (w_gate_v, w_up_v)[m % 2][l, e, :, 4 * (m // 2):4 * (m // 2) + 4, :]
                return w_down_v[l, e, :, m - 8, :]

            def ring_view(n, m):
                return four(n) if m < 8 else slot(n)

            def moe(l):
                n0 = START_MOE[l]
                for m in range(SLOTS):
                    load(n0 + m, expert_load(l, 0, m), ring_view(n0 + m, m))
                sp.wait_ge(unit_used, (UNIT_ATT, UNIT_O + 8 * NBLK)[l])
                for m in range(EXTRA):
                    if m == WS_EXTRA:
                        sp.wait_ge(route_mm, 4 * l + 1)
                    sp.dma_start(extra[:, m, :].rearrange("p (k c) -> p k c", k=4),
                                 expert_load(l, 1, m)).then_inc(extra_loaded[m], 16)
                for m in range(EXTRA, SLOTS):
                    n = n0 + SLOTS + m - EXTRA
                    load(n, expert_load(l, 1, m), ring_view(n, m))
                for m in range(PAIR_SLOTS):
                    n = n0 + PAIR_SLOTS - EXTRA + m
                    load(n, expert_load(l, 2 + m // SLOTS, m % SLOTS), ring_view(n, m % SLOTS))
                n1 = n0 + PAIR_SLOTS - EXTRA
                with sp.Fori(2, NPAIR) as i:
                    for b in range(2):
                        for m in range(SLOTS):
                            n = n1 + SLOTS * b + m
                            sp.wait_ge(slot_read, PAIR_SLOTS * (NPAIR * l + i) + SLOTS * (b - 1) + m + 1)
                            sp.dma_start(ring_view(n, m), expert_load(l, 2 * i + b, m)).then_inc(slot_loaded[n % SLOTS], 16)
                sp.wait_ge(route_dve, 3 * (l + 1))
                count = sp.value_load(flags[0:1, l:l + 1], min_val=0, max_val=SEQ)
                with sp.If(count > CAP):
                    sp.wait_ge(slot_read, NPAIR * PAIR_SLOTS * (l + 1))

                    def again(e):
                        for q in range(4):
                            for h, w in enumerate((w_gate_v, w_up_v)):
                                sp.dma_start(four(2 * q + h), w[l, e, :, 4 * q:4 * q + 4, :]).then_inc(over[l]["loaded"], 16)
                            sp.dma_start(slot(8 + q), w_down_v[l, e, :, q, :]).then_inc(over[l]["loaded"], 16)

                    again(0)
                    with sp.Fori(1, EXP) as e:
                        sp.wait_ge(over[l]["down"], NT * e)
                        again(e)
                    sp.wait_ge(over[l]["down"], NT * EXP)
                    sp.wait_ge(over[l]["added"], 4 * NT * EXP)
                with sp.Else():
                    sp.nop()

            sp.dma_start(const[:], table).then_inc(table_loaded, 16)
            for row, v in ((V_MIX, norm_mix[0]), (V_KV, kv_norm), (V_Q, norm_mix[1]), (V_FFN, norm_ffn[0]),
                           (V_FFN + KD, norm_ffn[1])):
                sp.dma_start(vec_rows[row:row + KD, :], v.rearrange("(k p) -> k p", p=P)).then_inc(table_loaded, 16)
            sp.dma_start(vec_rows[V_HEAD:V_HEAD + 1, :], k_norm.rearrange("(a p) -> a p", a=1)).then_inc(table_loaded, 16)
            sp.dma_start(vec_rows[V_HEAD + 1:V_END, :], q_norm).then_inc(band_loaded, 16)
            sp.dma_start(vec_rows[V_SCALE:V_ROWS, :], pool_scale.rearrange("a (k p) -> (a k) p", p=P)).then_inc(table_loaded, 16)
            load(0, pool_w_v[0])
            for l in range(2):
                sp.dma_start(route_rows[:, l, 0], w_grp[l].rearrange("(k p) g -> k (p g)", k=KD)).then_inc(route_loaded, 16)
                sp.dma_start(route_rows[:, l, 1:5], w_rt[l].rearrange("g (k p) e -> k g (p e)", k=KD)).then_inc(route_loaded, 16)
            for g in range(1, NG):
                load(g, pool_w_v[g])
            for l in range(2):
                sp.dma_start(ffn_gain[:, l, :], norm_ffn[l].rearrange("(p k) -> p k", k=KD)).then_inc(smalls_loaded, 16)
                sp.dma_start(bias[:, l, 0:4], b_grp[l:l + 1, :].to_broadcast([P, 4])).then_inc(smalls_loaded, 16)
                sp.dma_start(bias[:, l, 4:20], b_rt[l:l + 1].rearrange("a g e -> a (g e)").to_broadcast([P, EXP])).then_inc(smalls_loaded, 16)
            moe(0)

            def group(g, n, i):
                for kind, src in enumerate((w_kv_v[g], w_q_v[g], w_kv_v[g + NG])):
                    for q in range(4):
                        load(n + 4 * kind + q, src[:, 4 * q:4 * q + 4, :], None, i, SLOTS)

            group(0, START_ATT, 0)
            with sp.Fori(1, NG) as g:
                group(g, START_ATT + SLOTS, g - 1)
            for b in range(NBLK):
                for q in range(4):
                    load(START_O + 4 * b + q, w_o_v[b, :, 4 * q:4 * q + 4, :])
            moe(1)
            for m in range(8):
                c, t = m // 2, m % 2
                sp.wait_ge(resid_added, ADD_BASE[1] + 8 * (NPAIR - 1) + m + 1)
                sp.dma_start(out[0, t * P:(t + 1) * P, c * BLK:(c + 1) * BLK],
                             resid[:, t, c * BLK:(c + 1) * BLK]).then_inc(stored, 16)
            sp.wait_ge(stored, 16 * 8)

        @block.gpsimd
        def _(pool):
            def inverse_rms(n):
                pool.wait_ge(ms_done, n + 1)
                nc.gpsimd.tensor_tensor(rs[:], ssq[:], half[:, 0:NT], ALU.pow).then_inc(rs_done, 1)

            def left(l, c):
                if l + c:
                    pool.wait_ge(lo_done[1], NBLK * l + c)
                pool.wait_ge(hi_done, 8 * l + 2 * c + 2)
                nc.gpsimd.tensor_tensor(rest[:, 1].rearrange("q (p k) -> q p k", k=KD),
                                        resid[:, 1, c * BLK:(c + 1) * BLK].rearrange("q (p k) -> q p k", k=KD),
                                        in_tiles(0, 1, c), ALU.subtract).then_inc(rest_done[1], 1)

            def third(l, c, t):
                pool.wait_ge(mid_done[t], NBLK * l + c + 1)
                nc.gpsimd.tensor_tensor(in_tiles(2, t, c), rest[:, t].rearrange("q (p k) -> q p k", k=KD),
                                        in_tiles(1, t, c), ALU.subtract).then_inc(lo_done[t], 1)

            def residual_parts(l):
                for c in range(NBLK - 1):
                    left(l, c)
                    third(l, c, 1)
                inverse_rms(2 * l + 1)
                for t in range(NT):
                    third(l, NBLK - 1, t)

            nc.gpsimd.memset(half[:], -0.5).then_inc(pool_step, 1)
            pool.wait_ge(pool_step, 1)
            inverse_rms(0)
            residual_parts(0)
            inverse_rms(2)
            hs = head_ssq[:, :, :].rearrange("p t h -> p (t h)")
            hr = head_rs[:, :, :].rearrange("p t h -> p (t h)")
            with pool.Fori(0, NG) as g:
                for kind in range(2):
                    pool.wait_ge(head_sums, 2 * g + kind + 1)
                    nc.gpsimd.tensor_tensor(hr, hs, half[:, :], ALU.pow).then_inc(head_rs_done, 1)
            residual_parts(1)

        @block.scalar
        def _(act):
            for t in range(NT):
                act.dma_start(resid[:, t, :], x[0, t * P:(t + 1) * P, :]).then_inc(x_loaded[t], 16)
            act.dma_start(band[:, :, :, :], bands.rearrange("p (g b q) -> p g b q", g=NG, b=3)).then_inc(band_loaded, 16)

            def unit(u, n, h, gain=None, used=True, i=0, per_u=0, per_n=0):
                if used:
                    act.wait_ge(unit_used, u - UNIT_BUFS + 1 + i * per_u)
                slot_in(act, n, i, per_n)
                dst = ws[:, u % UNIT_BUFS, 0]
                if gain is None:
                    nc.scalar.activation(dst, four(n)[:, 2 * h:2 * h + 2, :], ACT.Copy).then_inc(unit_hi, 1)
                else:
                    for k in range(2):
                        last = nc.scalar.activation(dst[:, k, :], four(n)[:, 2 * h + k, :], ACT.Copy,
                                                    scale=vecs[:, gain + k:gain + k + 1])
                    last.then_inc(unit_hi, 1)

            def squares_and_first(l, c):
                act.wait_ge(resid_added, (0, ADD_O)[l] + 2 * c + 2)
                for t in range(NT):
                    if c + t or l:
                        act.wait_ge(ssq_done, SSQ[2 * l] + 2 * c + t)
                    nc.scalar.activation(junk[:, :], resid[:, t, c * BLK:(c + 1) * BLK], ACT.Square,
                                         accum_out=ssq_part[:, t, c:c + 1]).then_inc(ssq_done, 1)
                for t in range(NT):
                    nc.scalar.activation(in_tiles(0, t, c),
                                         resid[:, t, c * BLK:(c + 1) * BLK].rearrange("q (p k) -> q p k", k=KD),
                                         ACT.Copy).then_inc(hi_done, 1)

            def second(l, c, t):
                act.wait_ge(rest_done[t], NBLK * l + c + 1)
                nc.scalar.activation(in_tiles(1, t, c), rest[:, t].rearrange("q (p k) -> q p k", k=KD),
                                     ACT.Copy).then_inc(mid_done[t], 1)

            def moe(l):
                n0 = NPAIR * PAIR_SLOTS * l
                act.wait_ge(route_mm, 4 * l + 1)
                nc.scalar.activation(logitsT[:, :], ps[:, 6, 0:SEQ], ACT.Copy).then_inc(hidT_done, 1)
                second(l, NBLK - 1, 0)
                second(l, NBLK - 1, 1)
                act.wait_ge(route_dve, 3 * l + 1)
                nc.scalar.activation(route4[:, 0], route4[:, 0], ACT.Exp).then_inc(route_act, 1)
                act.wait_ge(route_dve, 3 * l + 2)
                nc.scalar.activation(route1[:, 3, :, 1:5], route1[:, 3, :, 1:5], ACT.Exp).then_inc(route_act, 1)
                act.wait_ge(route_dve, 3 * (l + 1))
                count = act.value_load(flags[0:1, l:l + 1], min_val=0, max_val=SEQ)
                with act.Fori(0, NPAIR) as i:
                    for b in range(2):
                        act.wait_ge(slot_read, n0 + SLOTS * (2 * i + b) + 8)
                        nc.scalar.activation(silu_g[:, :], ps[0:CAP, b, :], ACT.Silu,
                                             scale=rs_slot[:, b:b + 1]).then_inc(silu_done, 1)
                        act.wait_ge(hid_turned, EXP * l + 2 * i + b + 1)
                        nc.scalar.activation(putT[:, b * P:(b + 1) * P], ps[:, 1 - b, SEQ:SEQ + P], ACT.Copy)
                        nc.scalar.activation(hidT[:, b], ps[:, 1 - b, 0:KF * CAP].rearrange("p (k s) -> p k s", k=KF),
                                             ACT.Copy).then_inc(hidT_done, 1)
                        act.wait_ge(slot_read, n0 + SLOTS * (2 * i + b + 1))
                        for h in range(2):
                            nc.scalar.activation(
                                y_rows[CAP * b:CAP * b + CAP, 2 * h * BLK:(2 * h + 1) * BLK],
                                ps[0:CAP, 2 + h, :], ACT.Copy).then_inc(y_act, 1)
                with act.If(count > CAP):
                    with act.Fori(0, EXP) as e:
                        for t in range(NT):
                            act.wait_ge(over[l]["gu"], NT * e + t + 1)
                            nc.scalar.activation(o_silu[:, :], ps[:, 0, :], ACT.Silu,
                                                 scale=rs[:, t:t + 1]).then_inc(over[l]["silu"], 1)
                            act.wait_ge(over[l]["turned"], NT * e + t + 1)
                            nc.scalar.activation(o_hidT[:, :, :], ps[:, 2, :].rearrange("p (k s) -> p k s", k=KF),
                                                 ACT.Copy).then_inc(over[l]["hidT"], 1)
                    act.wait_ge(over[l]["added"], 4 * NT * EXP)
                with act.Else():
                    act.nop()

            for t in range(NT):
                act.wait_ge(x_loaded[t], 16)
                if t:
                    act.wait_ge(ssq_done, t)
                nc.scalar.activation(junk_rows[:, :], resid[:, t, :], ACT.Square,
                                     accum_out=ssq[:, t:t + 1]).then_inc(ssq_done, 1)
            act.wait_ge(vec_done, 1)
            for u in range(UNIT_BUFS):
                unit(u, u // 2, u % 2, used=False)
            for b in range(8):
                act.wait_ge(turned, b + 1)
                for k in range(2):
                    last = nc.scalar.activation(xs[:, 0, 2 * b + k, :], ps[:, b, k * SEQ:(k + 1) * SEQ], ACT.Copy,
                                                scale=vecs[:, V_MIX + 2 * b + k:V_MIX + 2 * b + k + 1])
                last.then_inc(xs_hi, 1)
            for g in range(NG):
                if 2 * g + 3 < UNIT_ATT:
                    unit(2 * g + 3, g + 1, 1)
                act.wait_ge(scale_spread, g + 1)
                if g:
                    act.wait_ge(resid_added, 2 * g)
                nc.scalar.activation(mixed[:, :, :], ps[:, 7, :].unsqueeze(1).to_broadcast([P, NT, BLK]),
                                     ACT.Copy).then_inc(scale_out, 1)
                if 2 * g + 4 < UNIT_ATT:
                    unit(2 * g + 4, g + 2, 0)
                if g:
                    squares_and_first(0, g - 1)
                    second(0, g - 1, 0)
                    second(0, g - 1, 1)
            squares_and_first(0, NBLK - 1)
            moe(0)

            def att_unit(g, j, used=True, i=0):
                kind = j % 24 // 8
                k = 2 * (j % 8)
                unit(UNIT_ATT + 24 * g + j, START_ATT + SLOTS * g + j // 2, j % 2, (V_KV, V_Q, V_KV)[kind] + k,
                     used, i, 24, SLOTS)

            def projected(g, kind):
                for t in range(NT):
                    if t == 0:
                        act.wait_ge(tile0_done, TILE0_ATT + 3 * g + kind + 1)
                    else:
                        act.wait_ge(unit_used, UNIT_ATT + 24 * g + 8 * kind + 8)
                    dst = vrow[:, t, :] if kind == 2 else raw[:, t].rearrange("p h d -> p (h d)")
                    nc.scalar.activation(dst, ps[:, 4 + t, :], ACT.Copy, scale=rs[:, t:t + 1]).then_inc(proj_out, 1)

            def heads(g, kind):
                for t in range(NT):
                    act.wait_ge(heads_turned, 4 * g + 2 * kind + t + 1)
                    nc.scalar.activation((kT, qT)[kind][:, :, t * P:(t + 1) * P],
                                         ps[:, 6 + t, :].rearrange("p (h q) -> p h q", h=HG),
                                         ACT.Copy, scale=vecs[:, V_HEAD + kind:V_HEAD + kind + 1]).then_inc(heads_out, 1)

            def exp_terms(g):
                act.wait_ge(z_done, g + 1)
                nc.scalar.activation(lnk[:, :, :], ps[:, 0:HG, 0:ZC], ACT.Abs).then_inc(act_step, 1)
                act.wait_ge(act_step, 2 * g + 1)
                nc.scalar.activation(lnk[:, :, :], lnk[:, :, :], ACT.Exp, scale=-1.0).then_inc(act_step, 1)

            def log_terms(g):
                act.wait_ge(act_step, 2 * g + 2)
                nc.scalar.activation(lnk[:, :, :], lnk[:, :, :], ACT.Ln, bias=1.0).then_inc(ln_done, 1)

            def weights(g):
                act.wait_ge(shift_done, g + 1)
                nc.scalar.activation(att[:, :, :], lnk[:, :, :], ACT.Exp).then_inc(att_done, 1)

            def square_rows(t):
                act.wait_ge(ssq_done, SSQ[1] + t)
                nc.scalar.activation(junk_att[:, :], resid[:, t, :], ACT.Square,
                                     accum_out=ssq[:, t:t + 1]).then_inc(ssq_done, 1)

            def group(g, i, first=False, last=False):
                G = g + i

                def units(*js):
                    for j in js:
                        att_unit(g, j, True, i)

                units(2)
                if not first:
                    exp_terms(G - 1)
                units(3)
                if first:
                    square_rows(0)
                else:
                    log_terms(G - 1)
                units(4, 5)
                if first:
                    square_rows(1)
                units(6, 7, 8, 9)
                if first:
                    act.wait_ge(rs_done, 3)
                projected(G, 0)
                units(10, 11)
                if not first:
                    weights(G - 1)
                units(12, 13)
                heads(G, 0)
                units(14, 15, 16, 17)
                projected(G, 1)
                units(18, 19, 20, 21)
                heads(G, 1)
                units(22, 23)
                if last:
                    o_unit(0)
                    o_unit(1)
                else:
                    units(24, 25)
                projected(G, 2)

            def o_unit(j):
                unit(UNIT_O + j, START_O + j // 2, j % 2)

            act.wait_ge(resid_added, ADD_O)
            att_unit(0, 0)
            for b in range(8):
                act.wait_ge(turned, TURN_ATT + b + 1)
                nc.scalar.activation(xs[:, 0, 2 * b:2 * b + 2, :],
                                     ps[:, X_BANKS[b], :].rearrange("p (k t) -> p k t", k=2),
                                     ACT.Copy).then_inc(xs_hi, 1)
                if b == 3:
                    att_unit(0, 1)
            group(0, 0, first=True)
            with act.Fori(1, NG - 1) as g:
                group(1, g - 1)
            group(NG - 1, 0, last=True)

            def o_chunk(c):
                if c == 0:
                    act.wait_ge(unit_used, UNIT_O)
                if c < 3:
                    act.wait_ge(o_out, 2 * c + 2)
                    nc.scalar.activation(xs[:, 0, 4 * c:4 * c + 4, :], oT[:, 4 * c:4 * c + 4, :],
                                         ACT.Copy).then_inc(xs_hi, 1)
                else:
                    act.wait_ge(o_done, 2 * c + 2)
                    nc.scalar.activation(xs[:, 0, 12:16, :].rearrange("p (b h) t -> p b (h t)", b=2), ps[:, 6:8, :],
                                         ACT.Copy).then_inc(xs_hi, 1)

            o_chunk(0)
            o_chunk(1)
            o_unit(2)
            exp_terms(NG - 1)
            o_unit(3)
            log_terms(NG - 1)
            o_chunk(2)
            o_unit(4)
            o_unit(5)
            weights(NG - 1)
            o_unit(6)
            o_unit(7)
            o_chunk(3)
            for c in range(NBLK):
                if c + 1 < NBLK:
                    o_unit(8 * c + 8)
                    o_unit(8 * c + 9)
                squares_and_first(1, c)
                if c + 1 < NBLK:
                    o_unit(8 * c + 10)
                    o_unit(8 * c + 11)
                    second(1, c, 0)
                    second(1, c, 1)
                    for j in range(8 * c + 12, 8 * c + 16):
                        o_unit(j)
            moe(1)

        @block.vector
        def _(dve):
            steps = [0]

            def step(ins):
                steps[0] += 1
                ins.then_inc(dve_step, 1)
                dve.wait_ge(dve_step, steps[0])

            def per_feature(gain, n, width):
                return gain.unsqueeze(2).to_broadcast([P, n, width])

            def unit(u, n, h, gain=None, i=0, per_u=0):
                dve.wait_ge(unit_hi, u + 1 + i * per_u)
                b = u % UNIT_BUFS
                src = four(n)[:, 2 * h:2 * h + 2, :]
                if gain is None:
                    nc.vector.tensor_tensor(ws[:, b, 1], src, ws[:, b, 0].bitcast(F32), ALU.subtract).then_inc(unit_lo, 1)
                else:
                    for k in range(2):
                        last = nc.vector.scalar_tensor_tensor(
                            out=ws[:, b, 1, k, :], in0=src[:, k, :], scalar=vecs[:, gain + k:gain + k + 1],
                            in1=ws[:, b, 0, k, :].bitcast(F32), op0=ALU.mult, op1=ALU.subtract)
                    last.then_inc(unit_lo, 1)

            def left(l, c, t):
                if l + c:
                    dve.wait_ge(lo_done[t], NBLK * l + c)
                dve.wait_ge(hi_done, 8 * l + 2 * c + t + 1)
                nc.vector.tensor_tensor(rest[:, t].rearrange("q (p k) -> q p k", k=KD),
                                        resid[:, t, c * BLK:(c + 1) * BLK].rearrange("q (p k) -> q p k", k=KD),
                                        in_tiles(0, t, c), ALU.subtract).then_inc(rest_done[t], 1)

            def third(l, c):
                dve.wait_ge(mid_done[0], NBLK * l + c + 1)
                nc.vector.tensor_tensor(in_tiles(2, 0, c), rest[:, 0].rearrange("q (p k) -> q p k", k=KD),
                                        in_tiles(1, 0, c), ALU.subtract).then_inc(lo_done[0], 1)

            def router_rows(l, c):
                for j in range(2):
                    dve.wait_ge(turned, TURN_ROUTE[l] + 2 * c + j + 1)
                    k = 4 * c + 2 * j
                    nc.vector.tensor_tensor(xr[:, k:k + 2, :],
                                            ps[:, turn_bank(l, c) + j, :].rearrange("p (k t) -> p k t", k=2),
                                            per_feature(vecs[:, V_FFN + KD * l + k:V_FFN + KD * l + k + 2], 2, SEQ),
                                            ALU.mult).then_inc(turned_out, 1)

            def mean_square(n, whole):
                dve.wait_ge(ssq_done, SSQ[n])
                if not whole:
                    step(nc.vector.tensor_reduce(ssq[:, :], ssq_part[:, :, :], AX_X, ALU.add))
                nc.vector.tensor_scalar(ssq[:, :], ssq[:, :], 1.0 / D, EPS, ALU.mult, ALU.add).then_inc(ms_done, 1)

            def moe(l):
                n0 = NPAIR * PAIR_SLOTS * l
                add0 = ADD_BASE[l]
                router_rows(l, NBLK - 1)
                mean_square(2 * l + 1, False)
                for t in range(NT):
                    left(l, NBLK - 1, t)
                dve.wait_ge(rs_done, 2 * l + 2)
                dve.wait_ge(route_mm, 4 * l + 2)
                for t in range(NT):
                    last = nc.vector.scalar_tensor_tensor(out=lg[:, t, :], in0=ps[:, 7, 32 * t:32 * t + 20],
                                                          scalar=rs[:, t:t + 1], in1=bias[:, l, :], op0=ALU.mult,
                                                          op1=ALU.add)
                step(last)

                LOGITS = lg[:, :, :].rearrange("p t (r e) -> p t r e", r=5)
                HOT1, HOT2, SEL2, SCORE = (route5[:, j] for j in range(4))
                TOP1, TOP2, BEST, DIFF, DENOM, W1, W2, SUM = (route1[:, j] for j in range(8))
                GROUP_EXP, WITHIN, WITHIN2 = (route4[:, j] for j in range(3))
                GROUP = HOT1[:, :, 0, :]

                def wide(a, n=5):
                    return a.unsqueeze(3).to_broadcast([P, NT, n, 4])

                def first_best(src, top, hot):
                    step(nc.vector.tensor_reduce(top, src, AX_X, ALU.max))
                    step(nc.vector.tensor_tensor(SCORE, src, wide(top), ALU.is_ge))
                    step(nc.vector.tensor_tensor(SCORE, SCORE, rank.unsqueeze(1).unsqueeze(1).to_broadcast([P, NT, 5, 4]),
                                                 ALU.mult))
                    step(nc.vector.tensor_reduce(BEST, SCORE, AX_X, ALU.max))
                    step(nc.vector.tensor_tensor(hot, SCORE, wide(BEST), ALU.is_equal))

                first_best(LOGITS, TOP1, HOT1)
                nc.vector.tensor_tensor(GROUP_EXP, LOGITS[:, :, 0, :], TOP1[:, :, 0:1].to_broadcast([P, NT, 4]),
                                        ALU.subtract).then_inc(route_dve, 1)
                step(nc.vector.scalar_tensor_tensor(out=SEL2, in0=HOT1, scalar=-BIG, in1=LOGITS,
                                                    op0=ALU.mult, op1=ALU.add))
                first_best(SEL2, TOP2, HOT2)
                step(nc.vector.tensor_tensor(SCORE, HOT1, HOT2, ALU.add))
                nc.vector.tensor_tensor(member[:, :, :].rearrange("p t (g e) -> p t g e", g=NG),
                                        wide(GROUP, NG), SCORE[:, :, 1:5, :], ALU.mult).then_inc(member_done, 1)
                nc.vector.tensor_tensor(DIFF, TOP2, TOP1, ALU.subtract).then_inc(route_dve, 1)
                step(nc.vector.tensor_copy(rs_parts[:, :, 0], rs[:, :]))
                step(nc.vector.tensor_tensor(rs_rest[:, :], rs[:, :], rs_parts[:, :, 0], ALU.subtract))
                step(nc.vector.tensor_copy(rs_parts[:, :, 1], rs_rest[:, :]))
                nc.vector.tensor_tensor(rs_parts[:, :, 2], rs_rest[:, :], rs_parts[:, :, 1],
                                        ALU.subtract).then_inc(rs_parts_done, 1)
                nc.vector.memset(slot_of[:, :, EXP:EXP + 2], 0.0)
                dve.wait_ge(route_mm, 4 * l + 3)
                dve.wait_ge(member_done, l + 1)
                count = ps[:, 7, 64:96].rearrange("p (t e) -> p t e", t=2)
                step(nc.vector.scalar_tensor_tensor(out=slot_of[:, :, 0:EXP], in0=count, scalar=1.0,
                                                    in1=member[:, :, :], op0=ALU.add, op1=ALU.mult))
                dve.wait_ge(route_mm, 4 * l + 4)
                step(nc.vector.tensor_reduce(most[:], ps[:, 5, 0:EXP], AX_X, ALU.max))

                def make_pick(i):
                    mine = slot_of[:, :, bass.ds(2 * i, 2)].unsqueeze(3).to_broadcast([P, NT, 2, CAP])
                    nc.vector.tensor_tensor(pick[:, :, :, :], iota.unsqueeze(1).unsqueeze(1).to_broadcast([P, NT, 2, CAP]),
                                            mine, ALU.is_equal).then_inc(pick_done, 1)

                def make_put(i):
                    dve.wait_ge(pick_done, (NPAIR + 1) * l + i + 1)
                    nc.vector.tensor_tensor(put[:, :, :, :], pick[:, :, :, :],
                                            gate[:, :, bass.ds(2 * i, 2)].unsqueeze(3).to_broadcast([P, NT, 2, CAP]),
                                            ALU.mult).then_inc(put_done, 1)

                make_pick(0)
                nc.vector.tensor_copy(flags[0:1, l:l + 1], most[0:1, :]).then_inc(route_dve, 1)
                dve.wait_ge(route_act, 2 * l + 1)
                step(nc.vector.tensor_reduce(SUM[:, :, 0:1], GROUP_EXP, AX_X, ALU.add))
                dve.wait_ge(route_act, 2 * l + 2)
                step(nc.vector.tensor_scalar(DENOM[:, :, 1:5], DIFF[:, :, 1:5], 1.0, None, ALU.add))
                step(nc.vector.tensor_tensor(DENOM[:, :, 1:5], DENOM[:, :, 1:5], SUM[:, :, 0:1].to_broadcast([P, NT, 4]),
                                             ALU.mult))
                step(nc.vector.reciprocal(W1[:, :, 1:5], DENOM[:, :, 1:5]))
                step(nc.vector.tensor_tensor(W2[:, :, 1:5], W1[:, :, 1:5], DIFF[:, :, 1:5], ALU.mult))
                step(nc.vector.tensor_tensor(HOT1[:, :, 1:5, :], HOT1[:, :, 1:5, :], wide(W1[:, :, 1:5], NG), ALU.mult))
                step(nc.vector.tensor_tensor(HOT2[:, :, 1:5, :], HOT2[:, :, 1:5, :], wide(W2[:, :, 1:5], NG), ALU.mult))
                step(nc.vector.tensor_tensor(SCORE[:, :, 1:5, :], HOT1[:, :, 1:5, :], HOT2[:, :, 1:5, :], ALU.add))
                nc.vector.memset(gate[:, :, EXP:EXP + 2], 0.0)
                step(nc.vector.tensor_tensor(gate[:, :, 0:EXP].rearrange("p t (g e) -> p t g e", g=NG),
                                             wide(GROUP, NG), SCORE[:, :, 1:5, :], ALU.mult))

                def tokens_out(n, b):
                    dve.wait_ge(rs_gathered, n)
                    nc.vector.tensor_reduce(rs_slot[:, b:b + 1], ps[0:CAP, b, 508:511], AX_X,
                                            ALU.add).then_inc(rs_slot_done, 1)
                    for h in range(2):
                        dve.wait_ge(gathered, 2 * n + h - 1)
                        nc.vector.tensor_tensor(
                            xg[:, b, 8 * h:8 * h + 8, :], ps[:, 6 + h, :].rearrange("p (k s) -> p k s", k=8),
                            per_feature(ffn_gain[:, l, 8 * h:8 * h + 8], 8, CAP), ALU.mult).then_inc(xg_done, 1)

                G0 = (EXP + 1) * l
                tokens_out(G0 + 1, 0)
                make_put(0)
                step(nc.vector.scalar_tensor_tensor(out=over_gate[:, :, :], in0=slot_of[:, :, 0:EXP],
                                                    scalar=float(CAP), in1=gate[:, :, 0:EXP], op0=ALU.is_gt, op1=ALU.mult))
                dve.wait_ge(route_dve, 3 * (l + 1))
                most_count = dve.value_load(flags[0:1, l:l + 1], min_val=0, max_val=SEQ)
                with dve.Fori(0, NPAIR) as i:
                    for b in range(2):
                        dve.wait_ge(silu_done, EXP * l + 2 * i + b + 1)
                        nc.vector.scalar_tensor_tensor(out=hid[:, :], in0=ps[CAP:2 * CAP, b, :],
                                                       scalar=rs_slot[:, b:b + 1], in1=silu_g[:, :],
                                                       op0=ALU.mult, op1=ALU.mult).then_inc(hid_done, 1)
                        tokens_out(G0 + 2 * i + 2 + b, 1 - b)
                        if b == 0:
                            dve.wait_ge(put_done, (NPAIR + 1) * l + i + 1)
                            make_pick(i + 1)
                        dve.wait_ge(slot_read, n0 + SLOTS * (2 * i + b + 1))
                        for h in range(2):
                            nc.vector.tensor_copy(
                                y_rows[CAP * b:CAP * b + CAP, (2 * h + 1) * BLK:(2 * h + 2) * BLK],
                                ps[CAP:2 * CAP, 2 + h, :]).then_inc(y_dve, 1)
                    dve.wait_ge(hid_turned, EXP * l + 2 * i + 2)
                    make_put(i + 1)
                    for m in range(8):
                        c, t = m // 2, m % 2
                        dve.wait_ge(mix_done, 8 * NPAIR * l + 8 * i + m + 1)
                        rb = resid[:, t, c * BLK:(c + 1) * BLK]
                        nc.vector.tensor_tensor(rb, rb, ps[:, 4 + t, :], ALU.add).then_inc(resid_added, 1)
                with dve.If(most_count > CAP):
                    dve.wait_ge(resid_added, add0 + 8 * NPAIR)
                    for n in range(4 * NT):
                        t, k = n // 4, 4 * (n % 4)
                        dve.wait_ge(over[l]["rows"], n + 1)
                        nc.vector.tensor_tensor(xr[:, k:k + 4, t * P:(t + 1) * P],
                                                ps[:, n, :].rearrange("p (k s) -> p k s", k=4),
                                                per_feature(ffn_gain[:, l, k:k + 4], 4, P),
                                                ALU.mult).then_inc(over[l]["xr"], 1)
                    with dve.Fori(0, EXP) as e:
                        for t in range(NT):
                            dve.wait_ge(over[l]["silu"], NT * e + t + 1)
                            nc.vector.scalar_tensor_tensor(out=o_hid[:, :], in0=ps[:, 1, :], scalar=rs[:, t:t + 1],
                                                           in1=o_silu[:, :], op0=ALU.mult,
                                                           op1=ALU.mult).then_inc(over[l]["hid"], 1)
                            dve.wait_ge(over[l]["down"], NT * e + t + 1)
                            for c in range(NBLK):
                                rb = resid[:, t, c * BLK:(c + 1) * BLK]
                                nc.vector.scalar_tensor_tensor(
                                    out=rb, in0=ps[:, 4 + c, :], scalar=over_gate[:, t, bass.ds(e, 1)],
                                    in1=rb, op0=ALU.mult, op1=ALU.add).then_inc(over[l]["added"], 1)
                            dve.wait_ge(over[l]["added"], 4 * NT * e + 4 * t + 4)
                with dve.Else():
                    dve.nop()

            dve.wait_ge(vec_turned, 1)
            step(nc.vector.tensor_copy(vecs[:], ps[:, 4, 0:V_END]))
            step(nc.vector.tensor_scalar(vecs[:, V_END - 1:V_END], vecs[:, V_END - 1:V_END], HD ** -0.5, None, ALU.mult))
            nc.vector.memset(w_route[:, 2 * KD * 20:], 0.0)
            nc.vector.tensor_copy(counters[:, 0, :], tri)
            nc.vector.tensor_copy(ident_b[:, :], ident)
            nc.vector.tensor_copy(counters[:, 1, :], ones).then_inc(vec_done, 1)
            mean_square(0, True)
            dve.wait_ge(rs_done, 1)
            dve.wait_ge(band_loaded, 32)
            for t, (lo, hi) in enumerate(((0, 2), (2, 3))):
                nc.vector.tensor_scalar(band_s[:, :, lo:hi, :], band[:, :, lo:hi, :], rs[:, t:t + 1], None,
                                        ALU.mult).then_inc(band_done, 1)
            for u in range(UNIT_BUFS):
                unit(u, u // 2, u % 2)
            for b in range(8):
                dve.wait_ge(xs_hi, b + 1)
                for k in range(2):
                    last = nc.vector.scalar_tensor_tensor(
                        out=xs[:, 1, 2 * b + k, :], in0=ps[:, b, k * SEQ:(k + 1) * SEQ],
                        scalar=vecs[:, V_MIX + 2 * b + k:V_MIX + 2 * b + k + 1],
                        in1=xs[:, 0, 2 * b + k, :].bitcast(F32), op0=ALU.mult, op1=ALU.subtract)
                last.then_inc(xs_lo, 1)
            dve.wait_ge(vec_turned, 2)
            for l in range(2):
                nc.vector.tensor_copy(w_route[:, 320 * l:320 * l + 320].rearrange("p (k e) -> p k e", e=20),
                                      ps[:, l, 0:320].rearrange("p (e k) -> p k e", e=20)).then_inc(vec_done, 1)
            dve.wait_ge(smalls_loaded, SMALLS)
            for g in range(NG):
                for u in (2 * g + 3, 2 * g + 4):
                    if u < UNIT_ATT:
                        unit(u, u // 2, u % 2)
                for t in range(NT):
                    if t == 0:
                        dve.wait_ge(scale_out, g + 1)
                        dve.wait_ge(tile0_done, g + 1)
                    else:
                        dve.wait_ge(unit_used, 2 * g + 2)
                    nc.vector.tensor_tensor(mixed[:, t, :], ps[:, MIX_BANKS[g % 2] + t, :], mixed[:, t, :],
                                            ALU.mult).then_inc(mixed_done, 1)
                    rb = resid[:, t, g * BLK:(g + 1) * BLK]
                    dve.wait_ge(mixed_done, 2 * g + t + 1)
                    nc.vector.tensor_tensor(rb, rb, mixed[:, t, :], ALU.add).then_inc(resid_added, 1)
                if g:
                    router_rows(0, g - 1)
                    left(0, g - 1, 0)
                    third(0, g - 1)
            moe(0)

            def att_unit(g, j, i=0):
                kind = j % 24 // 8
                unit(UNIT_ATT + 24 * g + j, START_ATT + SLOTS * g + j // 2, j % 2,
                     (V_KV, V_Q, V_KV)[kind] + 2 * (j % 8), i, 24)

            def head_squares(g, kind):
                for t in range(NT):
                    dve.wait_ge(proj_out, 6 * g + 2 * kind + t + 1)
                    dve.wait_ge(table_loaded, TABLES)
                    nc.vector.tensor_tensor(squares[:, :, :], raw[:, t], raw[:, t], ALU.mult).then_inc(sq_done, 1)
                    dve.wait_ge(sq_done, 8 * g + 4 * kind + 2 * t + 1)
                    nc.vector.tensor_reduce(head_ssq[:, t, :], squares[:, :, :], AX_X, ALU.add).then_inc(sq_done, 1)
                    dve.wait_ge(sq_done, 8 * g + 4 * kind + 2 * t + 2)
                nc.vector.tensor_scalar(head_ssq[:, :, :], head_ssq[:, :, :], 1.0 / HD, EPS,
                                        ALU.mult, ALU.add).then_inc(head_sums, 1)

            def head_scale(g, kind):
                dve.wait_ge(head_rs_done, 2 * g + kind + 1)
                nc.vector.tensor_tensor(raw[:, :, :, :], raw[:, :, :, :],
                                        head_rs[:, :, :].unsqueeze(3).to_broadcast([P, NT, HG, HD]),
                                        ALU.mult).then_inc(head_normed, 1)

            def softplus(g):
                dve.wait_ge(ln_done, g + 1)
                nc.vector.scalar_tensor_tensor(out=soft[:, :, :], in0=ps[:, 0:HG, 0:ZC], scalar=0.0, in1=lnk[:, :, :],
                                               op0=ALU.max, op1=ALU.add).then_inc(soft_done, 1)

            def masked(g):
                dve.wait_ge(soft_done, 2 * g + 1)
                nc.vector.scalar_tensor_tensor(out=soft[:, :, :],
                                               in0=const[:, C_ADD:C_ADD + ZC].unsqueeze(1).to_broadcast([P, HG, ZC]),
                                               scalar=0.0, in1=soft[:, :, :], op0=ALU.is_ge,
                                               op1=ALU.mult).then_inc(soft_done, 1)

            def shift(g):
                dve.wait_ge(cum_done, g + 1)
                nc.vector.tensor_tensor(lnk[:, :, :], ps[:, 0:HG, 0:ZC],
                                        const[:, C_ADD:C_ADD + ZC].unsqueeze(1).to_broadcast([P, HG, ZC]),
                                        ALU.add).then_inc(shift_done, 1)

            def outputs(g):
                for b in range(2):
                    dve.wait_ge(o_done, 2 * g + b + 1)
                    nc.vector.tensor_copy(oT[:, bass.ds(HG * g + 2 * b, 2), :],
                                          ps[:, 6 + b, :].rearrange("p (h q) -> p h q", h=2)).then_inc(o_out, 1)

            def group(g, i, first=False, last=False):
                G = g + i

                def units(*js):
                    for j in js:
                        att_unit(g, j, i)

                units(2, 3)
                if not first:
                    softplus(G - 1)
                units(4, 5)
                if first:
                    mean_square(2, True)
                else:
                    masked(G - 1)
                units(6, 7, 8, 9)
                head_squares(G, 0)
                units(10)
                head_scale(G, 0)
                units(11)
                if not first:
                    shift(G - 1)
                units(12, 13, 14, 15, 16, 17)
                if not first:
                    outputs(G - 1)
                head_squares(G, 1)
                units(18)
                head_scale(G, 1)
                units(19, 20, 21, 22, 23)
                if last:
                    o_unit(0)
                    o_unit(1)
                else:
                    units(24, 25)

            def o_unit(j):
                unit(UNIT_O + j, START_O + j // 2, j % 2)

            att_unit(0, 0)
            for b in range(8):
                dve.wait_ge(xs_hi, 8 + b + 1)
                nc.vector.tensor_tensor(xs[:, 1, 2 * b:2 * b + 2, :],
                                        ps[:, X_BANKS[b], :].rearrange("p (k t) -> p k t", k=2),
                                        xs[:, 0, 2 * b:2 * b + 2, :].bitcast(F32), ALU.subtract).then_inc(xs_lo, 1)
                if b == 3:
                    att_unit(0, 1)
            group(0, 0, first=True)
            with dve.Fori(1, NG - 1) as g:
                group(1, g - 1)
            group(NG - 1, 0, last=True)

            def o_chunk(c):
                dve.wait_ge(xs_hi, 16 + c + 1)
                if c < 3:
                    nc.vector.tensor_tensor(xs[:, 1, 4 * c:4 * c + 4, :], oT[:, 4 * c:4 * c + 4, :],
                                            xs[:, 0, 4 * c:4 * c + 4, :].bitcast(F32), ALU.subtract).then_inc(xs_lo, 1)
                else:
                    nc.vector.tensor_tensor(xs[:, 1, 12:16, :].rearrange("p (b h) t -> p b (h t)", b=2), ps[:, 6:8, :],
                                            xs[:, 0, 12:16, :].rearrange("p (b h) t -> p b (h t)", b=2).bitcast(F32),
                                            ALU.subtract).then_inc(xs_lo, 1)

            o_chunk(0)
            o_chunk(1)
            o_unit(2)
            o_unit(3)
            softplus(NG - 1)
            masked(NG - 1)
            o_chunk(2)
            o_unit(4)
            shift(NG - 1)
            o_unit(5)
            o_unit(6)
            o_unit(7)
            o_chunk(3)
            for c in range(NBLK):
                if c + 1 < NBLK:
                    o_unit(8 * c + 8)
                    o_unit(8 * c + 9)
                for t in range(NT):
                    if t == 0:
                        dve.wait_ge(tile0_done, TILE0_O + c + 1)
                    else:
                        dve.wait_ge(unit_used, UNIT_O + 8 * c + 8)
                    rb = resid[:, t, c * BLK:(c + 1) * BLK]
                    nc.vector.tensor_tensor(rb, rb, ps[:, 4 + t, :], ALU.add).then_inc(resid_added, 1)
                if c + 1 < NBLK:
                    o_unit(8 * c + 10)
                    left(1, c, 0)
                    o_unit(8 * c + 11)
                    o_unit(8 * c + 12)
                    third(1, c)
                    o_unit(8 * c + 13)
                    router_rows(1, c)
                    o_unit(8 * c + 14)
                    o_unit(8 * c + 15)
            moe(1)

        @block.tensor
        def _(pe):
            mm = nc.tensor.matmul

            def unit(u, tiles, first, last_unit, free=None, i=0, per_u=0, bank=4):
                pe.wait_ge(unit_lo, u + 1 + i * per_u)
                b = u % UNIT_BUFS
                for t in range(NT):
                    if first and free is not None:
                        free(t)
                    for j, k in enumerate(tiles):
                        cols = slice(t * P, (t + 1) * P)
                        for n, (px, pw) in enumerate(((0, 0), (0, 1), (1, 0))):
                            last = mm(ps[:, bank + t, :], xs[:, px, k, cols], ws[:, b, pw, j, :],
                                      start=(first and j == 0 and n == 0), stop=(last_unit and j == 1 and n == 2))
                    if last_unit and t == 0:
                        last.then_inc(tile0_done, 1)
                last.then_inc(unit_used, 1)

            def turn_block(l, c):
                pe.wait_ge(resid_added, (0, ADD_O)[l] + 2 * c + 2)
                if l == 0:
                    if c == 0:
                        pe.wait_ge(vec_done, 3)
                    else:
                        pe.wait_ge(turned_out, 2 * (c - 1) + 2)
                elif c > 1:
                    pe.wait_ge(turned_out, 8 + 2 * (c - 2) + 2)
                for j in range(4):
                    k = 4 * c + j
                    for t in range(NT):
                        col = (j % 2) * SEQ + t * P
                        last = nc.tensor.transpose(ps[:, turn_bank(l, c) + j // 2, col:col + P],
                                                   resid[:, t, k * P:(k + 1) * P], ident)
                    if j % 2:
                        last.then_inc(turned, 1)

            def route_block(l, c):
                pe.wait_ge(turned_out, 8 * l + 2 * c + 2)
                for j in range(4):
                    k = 4 * c + j
                    col = 20 * (KD * l + k)
                    last = mm(ps[32 * j:32 * j + 32, 6, 0:SEQ], w_route[:, col:col + 32], xr[:, k, :],
                              start=(c == 0), stop=(c == NBLK - 1))
                if c == NBLK - 1:
                    last.then_inc(route_mm, 1)

            def spread_scale(g):
                if g:
                    pe.wait_ge(scale_out, g)
                for k in range(4):
                    row = V_SCALE + 4 * g + k
                    last = mm(ps[:, 7, k * P:(k + 1) * P], const[0:V_ROWS, row:row + 1].to_broadcast([V_ROWS, P]),
                              vec_rows[:, :], start=True, stop=True)
                last.then_inc(scale_spread, 1)

            def keep_clock(n):
                for _ in range(n):
                    mm(ps[:, 3, 0:2 * P], counters[:, 0, :], counters[:, :, :].rearrange("p a b -> p (a b)"),
                       start=True, stop=True)

            def moe(l):
                n0 = START_MOE[l]
                add0 = ADD_BASE[l]
                turn_block(l, NBLK - 1)
                route_block(l, NBLK - 1)
                pe.wait_ge(hidT_done, (EXP + 1) * l + 1)
                for t in range(NT):
                    last = mm(ps[:, 7, 32 * t:32 * t + 20], logitsT[:, t * P:(t + 1) * P],
                              const[:, C_STACK:C_STACK + 20], start=True, stop=True)
                last.then_inc(route_mm, 1)
                keep_clock(WARM_ROUTE)
                pe.wait_ge(member_done, l + 1)
                before, every = counters[:, 0, :], counters[:, 1, :]
                mm(ps[:, 7, 64:80], before, member[:, 0, :], start=True, stop=True)
                mm(ps[:, 7, 80:96], every, member[:, 0, :], start=True, stop=False)
                mm(ps[:, 7, 80:96], before, member[:, 1, :], start=False, stop=True).then_inc(route_mm, 1)
                mm(ps[:, 5, 0:EXP], every, member[:, 0, :], start=True, stop=False)
                mm(ps[:, 5, 0:EXP], every, member[:, 1, :], start=False, stop=True).then_inc(route_mm, 1)

                keep_clock(WARM_PICK)

                def gather(e):
                    for t in range(NT):
                        last = mm(ps[0:CAP, e, 508:511], pick[:, t, e, :], rs_parts[:, t, :], start=(t == 0),
                                  stop=(t == NT - 1))
                    last.then_inc(rs_gathered, 1)
                    for k in range(KD):
                        for s in range(3):
                            for t in range(NT):
                                last = mm(ps[:, 6 + k // 8, (k % 8) * CAP:(k % 8 + 1) * CAP],
                                          parts[:, s, t, k * P:(k + 1) * P], pick[:, t, e, :],
                                          start=(s == 0 and t == 0), stop=(s == 2 and t == NT - 1))
                        if k % 8 == 7:
                            last.then_inc(gathered, 1)

                PICKS = (NPAIR + 1) * l
                XG = (EXP + 1) * l
                for t in range(NT):
                    pe.wait_ge(lo_done[t], NBLK * (l + 1))
                pe.wait_ge(rs_parts_done, l + 1)
                pe.wait_ge(pick_done, PICKS + 1)
                gather(0)
                pe.wait_ge(route_dve, 3 * (l + 1))
                count = pe.value_load(flags[0:1, l:l + 1], min_val=0, max_val=SEQ)

                def loaded(i, b, m):
                    first = isinstance(i, int)
                    if first and b == 1 and m < EXTRA:
                        pe.wait_ge(extra_loaded[m], 16 * (l + 1))
                        return extra[:, m, :]
                    if first:
                        n = n0 + SLOTS * b + m - EXTRA * b
                        slot_in(pe, n)
                    else:
                        n = n0 + PAIR_SLOTS - EXTRA + SLOTS * b + m
                        slot_in(pe, n, i - 1, PAIR_SLOTS)
                    return slot(n)

                def pair(i):
                    for b in range(2):
                        pe.wait_ge(xg_done, 2 * (XG + 2 * i + b) + 1)
                        pe.wait_ge(hidT_done, (EXP + 1) * l + 2 * i + b + 1)
                        for q in range(4):
                            both = [loaded(i, b, 2 * q + h).rearrange("p (k c) -> p k c", k=4) for h in range(2)]
                            if q == 2:
                                pe.wait_ge(xg_done, 2 * (XG + 2 * i + b) + 2)
                            for j in range(4):
                                k = 4 * q + j
                                for h in range(2):
                                    last = mm(ps[CAP * h:CAP * h + CAP, b, :], xg[:, b, k, :], both[h][:, j, :],
                                              start=(k == 0), stop=(k == KD - 1))
                            last.then_inc(slot_read, 2)
                        if b == 1:
                            pe.wait_ge(pick_done, PICKS + i + 2)
                        gather(1 - b)
                        pe.wait_ge(rs_slot_done, XG + 2 * i + b + 2)
                        pe.wait_ge(put_done, PICKS + i + 1)
                        pe.wait_ge(hid_done, EXP * l + 2 * i + b + 1)
                        nc.tensor.transpose(ps[:, 1 - b, SEQ:SEQ + P], put[:, b].rearrange("p e s -> p (e s)"), ident)
                        for k in range(KF):
                            last = nc.tensor.transpose(ps[:, 1 - b, k * CAP:(k + 1) * CAP], hid[:, k * P:(k + 1) * P],
                                                       const[0:CAP, C_ID:C_ID + CAP])
                        last.then_inc(hid_turned, 1)
                        pe.wait_ge(hidT_done, (EXP + 1) * l + 2 * i + b + 2)
                        if b == 1:
                            pe.wait_ge(y_act, 2 * (EXP * l + 2 * i) + 2)
                            pe.wait_ge(y_dve, 2 * (EXP * l + 2 * i) + 2)
                        for k in range(KF):
                            down = loaded(i, b, 8 + k)
                            for c in range(NBLK):
                                h = c % 2
                                last = mm(ps[CAP * h:CAP * h + CAP, 2 + c // 2, :], hidT[:, b, k, :],
                                          down[:, c * BLK:(c + 1) * BLK], start=(k == 0), stop=(k == KF - 1))
                            last.then_inc(slot_read, 1)
                    for m in range(8):
                        c, t = m // 2, m % 2
                        if t == 0:
                            pe.wait_ge((y_act, y_dve)[c % 2], 2 * (EXP * l + 2 * i) + 3 + c // 2)
                        pe.wait_ge(resid_added, add0 + 8 * i + m - 1)
                        mm(ps[:, 4 + t, :], putT[:, t * P:(t + 1) * P], y_rows[:, c * BLK:(c + 1) * BLK],
                           start=True, stop=True).then_inc(mix_done, 1)

                pair(0)
                with pe.Fori(1, NPAIR) as i:
                    pair(i)
                with pe.If(count > CAP):
                    o = over[l]
                    pe.wait_ge(resid_added, add0 + 8 * NPAIR)
                    pe.wait_ge(xg_done, 2 * (EXP + 1) * (l + 1))
                    for t in range(NT):
                        for k in range(KD):
                            for part in range(3):
                                last = mm(ps[:, 4 * t + k // 4, (k % 4) * P:(k % 4 + 1) * P],
                                          parts[:, part, t, k * P:(k + 1) * P], ident_b[:, :], start=(part == 0),
                                          stop=(part == 2))
                            if k % 4 == 3:
                                last.then_inc(o["rows"], 1)
                    pe.wait_ge(o["xr"], 4 * NT)
                    with pe.Fori(0, EXP) as e:
                        pe.wait_ge(o["loaded"], 16 * SLOTS * e + 16 * SLOTS)
                        for t in range(NT):
                            for h in range(2):
                                for k in range(KD):
                                    last = mm(ps[:, h, :], xr[:, k, t * P:(t + 1) * P], four(2 * (k // 4) + h)[:, k % 4, :],
                                              start=(k == 0), stop=(k == KD - 1))
                            last.then_inc(o["gu"], 1)
                            pe.wait_ge(o["hid"], NT * e + t + 1)
                            for k in range(KF):
                                last = nc.tensor.transpose(ps[:, 2, k * P:(k + 1) * P], o_hid[:, k * P:(k + 1) * P], ident)
                            last.then_inc(o["turned"], 1)
                            pe.wait_ge(o["hidT"], NT * e + t + 1)
                            for c in range(NBLK):
                                for k in range(KF):
                                    last = mm(ps[:, 4 + c, :], o_hidT[:, k, :], slot(8 + k)[:, c * BLK:(c + 1) * BLK],
                                              start=(k == 0), stop=(k == KF - 1))
                            last.then_inc(o["down"], 1)
                            pe.wait_ge(o["added"], 4 * NT * e + 4 * t + 4)
                with pe.Else():
                    pe.nop()

            pe.wait_ge(table_loaded, TABLES)
            pe.wait_ge(band_loaded, 32)
            nc.tensor.transpose(ps[:, 4, 0:V_END], vec_rows[0:V_END, :], const[0:V_END, C_ID:C_ID + V_END]).then_inc(vec_turned, 1)
            pe.wait_ge(vec_done, 1)
            keep_clock(WARM_START)
            for t in range(NT):
                pe.wait_ge(x_loaded[t], 16)
            pe.wait_ge(band_done, 2)
            for b in range(8):
                g = b // 2
                for k in (2 * b, 2 * b + 1):
                    c = (k % 2) * SEQ
                    mm(ps[:, b, c:c + SEQ], resid[:, 0, k * P:(k + 1) * P], band_s[:, g, 0:2, :], start=True, stop=False)
                    last = mm(ps[:, b, c + P:c + SEQ], resid[:, 1, k * P:(k + 1) * P], band_s[:, g, 2, :],
                              start=False, stop=True)
                last.then_inc(turned, 1)
            pe.wait_ge(route_loaded, 64)
            pe.wait_ge(xs_lo, 2)
            for l in range(2):
                for g in range(5):
                    rows = route_rows[:, l, g].rearrange("k (p e) -> k e p", e=4)
                    for e in range(4):
                        c = KD * (4 * g + e)
                        last = nc.tensor.transpose(ps[:, l, c:c + KD], rows[:, e, :], const[0:KD, C_ID:C_ID + KD])
            last.then_inc(vec_turned, 1)
            pe.wait_ge(xs_lo, 8)
            for g in range(NG):
                def read(t, g=g):
                    if g > 1:
                        pe.wait_ge(mixed_done, 2 * (g - 2) + t + 1)

                unit(2 * g, (4 * g, 4 * g + 1), True, False, read, bank=MIX_BANKS[g % 2])
                spread_scale(g)
                unit(2 * g + 1, (4 * g + 2, 4 * g + 3), False, True, bank=MIX_BANKS[g % 2])
                if g > 0:
                    turn_block(0, g - 1)
                if g > 1:
                    route_block(0, g - 2)
            route_block(0, NBLK - 2)
            moe(0)

            for b in range(8):
                pe.wait_ge(resid_added, ADD_O - 8 + 2 * (b // 2) + 2)
                if b >= 6:
                    pe.wait_ge(xs_lo, 8 + b - 6 + 1)
                for k in (2 * b, 2 * b + 1):
                    for t in range(NT):
                        c = (k % 2) * SEQ + t * P
                        last = nc.tensor.transpose(ps[:, X_BANKS[b], c:c + P], resid[:, t, k * P:(k + 1) * P], ident)
                last.then_inc(turned, 1)

            def att_unit(g, j, i=0, first=False):
                kind = j // 8

                def evacuated(t):
                    if not first:
                        pe.wait_ge(proj_out, 6 * (g + i) + 2 * kind + t - 1)

                if first:
                    pe.wait_ge(xs_lo, 8 + j + 1)
                unit(UNIT_ATT + 24 * g + j, (2 * (j % 8), 2 * (j % 8) + 1), j % 8 == 0, j % 8 == 7, evacuated, i, 24)

            def turn_heads(g, kind):
                pe.wait_ge(head_normed, 2 * g + kind + 1)
                for t in range(NT):
                    for h in range(HG):
                        last = nc.tensor.transpose(ps[:, 6 + t, h * P:(h + 1) * P], raw[:, t, h, :], ident)
                    last.then_inc(heads_turned, 1)

            def scores(g):
                pe.wait_ge(heads_out, 4 * g + 4)
                for h in range(HG):
                    mm(ps[:, h, 0:SEQ], kT[:, h, 0:P], qT[:, h, :], start=True, stop=False, skip_group_check=True)
                    last = mm(ps[:, h, SEQ:ZC], kT[:, h, P:SEQ], qT[:, h, P:SEQ], start=False, stop=True,
                              skip_group_check=True)
                last.then_inc(z_done, 1)

            def suffix_sums(g):
                pe.wait_ge(soft_done, 2 * g + 2)
                for h in range(HG):
                    mm(ps[:, h, 0:ZC], const[:, C_NSUF:C_NSUF + P], soft[:, h, :], start=False, stop=False,
                       skip_group_check=True)
                    last = mm(ps[:, h, P:SEQ], const[:, C_NONE:C_NONE + P], soft[:, h, SEQ:ZC], start=False, stop=True,
                              skip_group_check=True)
                last.then_inc(cum_done, 1)

            def mix_values(g):
                pe.wait_ge(att_done, g + 1)
                for h in range(HG):
                    c = (h % 2) * SEQ
                    mm(ps[:, 6 + h // 2, c:c + SEQ], vrow[:, 0, h * P:(h + 1) * P], att[:, h, 0:SEQ], start=True,
                       stop=False)
                    last = mm(ps[:, 6 + h // 2, c + P:c + SEQ], vrow[:, 1, h * P:(h + 1) * P], att[:, h, SEQ:ZC],
                              start=False, stop=True)
                    if h % 2:
                        last.then_inc(o_done, 1)

            def group(g, i, first):
                G = g + i
                if not first:
                    scores(G - 1)
                for j in range(8):
                    att_unit(g, j, i, first)
                if not first:
                    suffix_sums(G - 1)
                for j in range(8, 12):
                    att_unit(g, j, i)
                turn_heads(G, 0)
                for j in range(12, 16):
                    att_unit(g, j, i)
                pe.wait_ge(heads_out, 4 * G + 2)
                if not first:
                    mix_values(G - 1)
                for j in range(16, 20):
                    att_unit(g, j, i)
                if not first:
                    pe.wait_ge(o_out, 2 * G)
                turn_heads(G, 1)
                for j in range(20, 24):
                    att_unit(g, j, i)

            group(0, 0, True)
            with pe.Fori(1, NG - 1) as g:
                group(1, g - 1, False)
            group(NG - 1, 0, False)

            def o_unit(j):
                def free(t):
                    if j == 0:
                        pe.wait_ge(proj_out, 6 * NG - 1 + t)
                    else:
                        pe.wait_ge(resid_added, ADD_O + 2 * (j // 8 - 1) + t + 1)

                if j < 8 and j % 2 == 0:
                    pe.wait_ge(xs_lo, 16 + j // 2 + 1)
                unit(UNIT_O + j, (2 * (j % 8), 2 * (j % 8) + 1), j % 8 == 0, j % 8 == 7, free)

            scores(NG - 1)
            for j in range(4):
                o_unit(j)
            suffix_sums(NG - 1)
            o_unit(4)
            o_unit(5)
            pe.wait_ge(heads_out, 4 * NG)
            pe.wait_ge(proj_out, 6 * NG)
            mix_values(NG - 1)
            o_unit(6)
            o_unit(7)
            for c in range(1, NBLK):
                for j in range(4):
                    o_unit(8 * c + j)
                if c == 1:
                    pe.wait_ge(shift_done, NG)
                turn_block(1, c - 1)
                for j in range(4, 8):
                    o_unit(8 * c + j)
                route_block(1, c - 1)
            moe(1)


_INS = ["x", "norm_mix", "norm_ffn", "pool_w", "pool_scale", "kv_norm", "w_kv", "k_norm", "w_q", "q_norm", "w_o",
        "moe_w_grp", "moe_b_grp", "moe_w_rt", "moe_b_rt", "moe_w_gate", "moe_w_up", "moe_w_down"]


def kernel(**inputs):
    import concourse.bacc as bacc
    from concourse.bass_utils import run_bass_kernel_spmd

    nc = bacc.Bacc("TRN2", target_bir_lowering=False, num_devices=1, dynamic_dma_scratch_size=1024)
    arrays, args = {}, []
    tables = {"constant_table": constant_table(), "band_table": band_table()}
    for name in [*_INS, *tables]:
        a = tables[name] if name in tables else np.ascontiguousarray(inputs[name])
        arrays[f"in_{name}"] = a
        args.append(nc.dram_tensor(f"in_{name}", a.shape, mybir.dt.from_np(a.dtype), kind="ExternalInput").ap())
    out = nc.dram_tensor("out_rows", (1, SEQ, D), F32, kind="ExternalOutput").ap()
    build(nc, *args, out)
    r = run_bass_kernel_spmd(nc, [arrays], core_ids=[0])
    return r.results[0]["out_rows"]
```
